# Optimizing a Trainium2 kernel written in Bass

```python
import math
import functools
import jax
import jax.numpy as jnp
from jax import lax
import numpy as np

D_MODEL = 2048
BATCH = 1
SEQ = 256
DEPTH = 2

N_EVEN = (DEPTH + 1) // 2
N_ODD = DEPTH // 2
N_MEM = 256
RMS_EPS = 1e-6
D_FF = 4 * D_MODEL

DN_HEADS = 8
DN_HEAD_DIM = 128
DN_WIDTH = DN_HEADS * DN_HEAD_DIM
DN_CONV = 3
DN_CHUNK = 64
SC_WIDTH = D_MODEL - DN_WIDTH
SC_CONV = 3
EV_IN = 4 * DN_WIDTH + 4 * DN_HEADS + 3 * SC_WIDTH
EV_OUT = DN_WIDTH + SC_WIDTH

DSA_PATTERNS = ((128, 1), (512, 4), (2048, 16))
DSA_GROUPS = len(DSA_PATTERNS)
DSA_HEADS_PER_GROUP = 4
DSA_HEAD_DIM = 128
DSA_HEADS = DSA_GROUPS * DSA_HEADS_PER_GROUP
DSA_QKV = DSA_HEADS * DSA_HEAD_DIM
DSA_OUT = DSA_HEADS_PER_GROUP * DSA_HEAD_DIM
REL_BUCKETS = 32
REL_MAX_DIST = 1024
NEG_INF = -1e30

RW_HEADS = 8
RW_HEAD_DIM = 64
RW_WIDTH = RW_HEADS * RW_HEAD_DIM
RW_DECAY_LORA = 64
RW_AAA_LORA = 64
RW_GATE_LORA = 128
RW_SPLITS = (RW_WIDTH, RW_WIDTH, RW_WIDTH, RW_DECAY_LORA, RW_DECAY_LORA, RW_AAA_LORA, RW_AAA_LORA, RW_GATE_LORA)
RW_IN = sum(RW_SPLITS)
RW_GN_EPS = 64e-5
OD_IN = 3 * DSA_QKV + RW_IN
OD_OUT = DSA_OUT + RW_WIDTH

XA_HEADS = 4
XA_HEAD_DIM = 128
XA_WIDTH = XA_HEADS * XA_HEAD_DIM

kernel_name = 'hybrid_deltanet_shortconv_dilated_rwkv7_encoder'

def rms_norm(x, g):
    xf = x.astype(jnp.float32)
    y = xf * lax.rsqrt(jnp.mean(xf * xf, axis=-1, keepdims=True) + RMS_EPS)
    return (y * g.astype(jnp.float32)).astype(x.dtype)

def l2_normalize(x):
    return x * lax.rsqrt(jnp.sum(x * x, axis=-1, keepdims=True) + 1e-6)

def centred_dwconv(x, w):
    k = w.shape[-1]
    rhs = jnp.transpose(w)[:, None, :].astype(x.dtype)
    return lax.conv_general_dilated(x, rhs, window_strides=(1,), padding=[(k // 2, k // 2)],
                                    dimension_numbers=('NWC', 'WIO', 'NWC'),
                                    feature_group_count=x.shape[-1])

def centred_token_shift(t):
    tp = jnp.pad(t, ((0, 0), (1, 1), (0, 0)))
    return 0.5 * (tp[:, :-2] + tp[:, 2:])

def t5_bucket(rel):
    half = REL_BUCKETS // 2
    max_exact = half // 2
    n = jnp.abs(rel)
    scaled = jnp.log(jnp.maximum(n, max_exact).astype(jnp.float32) / max_exact) / math.log(REL_MAX_DIST / max_exact)
    large = jnp.minimum(max_exact + (scaled * (half - max_exact)).astype(jnp.int32), half - 1)
    return jnp.where(rel > 0, half, 0) + jnp.where(n < max_exact, n, large)

def gated_delta_rule(q, k, v, g, beta):
    B, S, H, DK = q.shape
    DV = v.shape[-1]
    C = DN_CHUNK
    N = S // C

    def to_chunks(t):
        return jnp.swapaxes(t.reshape((B, N, C, H) + t.shape[3:]), 2, 3)

    qc, kc, vc = to_chunks(q), to_chunks(k), to_chunks(v)
    gc = jnp.cumsum(to_chunks(g), axis=-1)
    bc = to_chunks(beta)
    kb = kc * bc[..., None]
    vb = vc * bc[..., None]
    lower = jnp.tril(jnp.ones((C, C), dtype=bool))
    strict = jnp.tril(jnp.ones((C, C), dtype=bool), -1)
    diff = gc[..., :, None] - gc[..., None, :]
    decay = jnp.where(lower, jnp.exp(jnp.where(lower, diff, 0.0)), 0.0)
    a_mat = jnp.where(strict, jnp.einsum('bnhid,bnhjd->bnhij', kb, kc) * decay, 0.0)
    unit_lower = a_mat + jnp.eye(C, dtype=a_mat.dtype)
    solve = functools.partial(lax.linalg.triangular_solve, left_side=True, lower=True, unit_diagonal=True)
    u = solve(unit_lower, vb)
    w = solve(unit_lower, kb * jnp.exp(gc)[..., None])
    qk = jnp.where(lower, jnp.einsum('bnhid,bnhjd->bnhij', qc, kc) * decay, 0.0)

    def step(state, inp):
        q_i, k_i, u_i, w_i, g_i, qk_i = inp
        v_new = u_i - jnp.einsum('bhcd,bhde->bhce', w_i, state)
        o = (jnp.einsum('bhcd,bhde->bhce', q_i * jnp.exp(g_i)[..., None], state)
             + jnp.einsum('bhij,bhje->bhie', qk_i, v_new))
        g_last = g_i[..., -1:]
        state = (state * jnp.exp(g_last)[..., None]
                 + jnp.einsum('bhcd,bhce->bhde', k_i * jnp.exp(g_last - g_i)[..., None], v_new))
        return state, o

    xs = tuple(jnp.swapaxes(t, 0, 1) for t in (qc, kc, u, w, gc, qk))
    state0 = jnp.zeros((B, H, DK, DV), jnp.float32)
    _, o = lax.scan(step, state0, xs)
    return jnp.transpose(o, (1, 0, 3, 2, 4)).reshape(B, S, H, DV)

def even_mixer(h, w_in, w_out, conv_qkv, a_log, dt_bias, out_gain, conv_sc):
    B, S, _ = h.shape
    f32 = jnp.float32
    p = h @ w_in
    c1 = 3 * DN_WIDTH
    c2 = c1 + DN_WIDTH
    c3 = c2 + 4 * DN_HEADS
    qkv = jax.nn.silu(centred_dwconv(p[..., :c1], conv_qkv)).astype(f32)
    q, k, v = [t.reshape(B, S, DN_HEADS, DN_HEAD_DIM) for t in jnp.split(qkv, 3, axis=-1)]
    q = l2_normalize(q) * (DN_HEAD_DIM ** -0.5)
    k = l2_normalize(k)
    ab = p[..., c2:c3].astype(f32).reshape(B, S, 4, DN_HEADS)
    beta = jax.nn.sigmoid(ab[:, :, 0:2])
    g = -jnp.exp(a_log.astype(f32)) * jax.nn.softplus(ab[:, :, 2:4] + dt_bias.astype(f32))
    flip = lambda t: jnp.flip(t, axis=1)
    o_fwd = gated_delta_rule(q, k, v, g[:, :, 0], beta[:, :, 0])
    o_bwd = flip(gated_delta_rule(flip(q), flip(k), flip(v), flip(g[:, :, 1]), flip(beta[:, :, 1])))
    o = o_fwd + o_bwd
    o = o * lax.rsqrt(jnp.mean(o * o, axis=-1, keepdims=True) + RMS_EPS) * out_gain.astype(f32)
    gate = p[..., c1:c2].astype(f32).reshape(B, S, DN_HEADS, DN_HEAD_DIM)
    y_dn = (o * jax.nn.silu(gate)).reshape(B, S, DN_WIDTH).astype(h.dtype)
    b_gate, c_gate, u_in = jnp.split(p[..., c3:], 3, axis=-1)
    y_sc = b_gate * centred_dwconv(c_gate * u_in, conv_sc)
    return jnp.concatenate([y_dn, y_sc.astype(h.dtype)], axis=-1) @ w_out

def dilated_window_attention(q, k, v, bias, dil, n_side):
    B, S, H, E = q.shape
    f32 = jnp.float32
    L = S // dil
    blk = n_side
    nb = -(-L // blk)
    Lp = nb * blk

    def sub(t):
        return jnp.swapaxes(t.astype(f32).reshape(B, L, dil, H, E), 1, 2)

    qs, ks, vs = sub(q), sub(k), sub(v)
    qb = jnp.pad(qs, ((0, 0), (0, 0), (0, Lp - L), (0, 0), (0, 0))).reshape(B, dil, nb, blk, H, E)
    pad_kv = ((0, 0), (0, 0), (blk, Lp - L + blk), (0, 0), (0, 0))
    kp = jnp.pad(ks, pad_kv).reshape(B, dil, nb + 2, blk, H, E)
    vp = jnp.pad(vs, pad_kv).reshape(B, dil, nb + 2, blk, H, E)
    kw = jnp.concatenate([kp[:, :, 0:nb], kp[:, :, 1:nb + 1], kp[:, :, 2:nb + 2]], axis=3)
    vw = jnp.concatenate([vp[:, :, 0:nb], vp[:, :, 1:nb + 1], vp[:, :, 2:nb + 2]], axis=3)
    qi = jnp.arange(blk)[:, None]
    kj = jnp.arange(3 * blk)[None, :]
    rel = kj - blk - qi
    key_idx = jnp.arange(nb)[:, None, None] * blk + (kj - blk)[None]
    valid = (jnp.abs(rel) <= n_side)[None] & (key_idx >= 0) & (key_idx < L)
    bias_full = bias[:, jnp.clip(rel + n_side, 0, 2 * n_side)]
    logits = jnp.einsum('bdnqhe,bdnkhe->bdnhqk', qb, kw) * (E ** -0.5) + bias_full
    logits = jnp.where(valid[:, None], logits, NEG_INF)
    m = jnp.max(logits, axis=-1, keepdims=True)
    p = jnp.exp(logits - m)
    s = jnp.sum(p, axis=-1, keepdims=True)
    o = jnp.einsum('bdnhqk,bdnkhe->bdnqhe', p, vw) * jnp.swapaxes(1.0 / s, 3, 4)
    lse = jnp.swapaxes((m + jnp.log(s))[..., 0], 3, 4)
    o = jnp.swapaxes(o.reshape(B, dil, Lp, H, E)[:, :, :L], 1, 2).reshape(B, S, H, E)
    lse = jnp.swapaxes(lse.reshape(B, dil, Lp, H)[:, :, :L], 1, 2).reshape(B, S, H)
    return o, lse

def rwkv7_scan(r, w, k, v, a, b, reverse):
    B, S, H, N = r.shape

    def step(state, inp):
        r_t, w_t, k_t, v_t, a_t, b_t = inp
        sa = jnp.einsum('bhij,bhj->bhi', state, a_t)
        state = (state * w_t[:, :, None, :] + sa[..., None] * b_t[:, :, None, :]
                 + v_t[..., None] * k_t[:, :, None, :])
        return state, jnp.einsum('bhij,bhj->bhi', state, r_t)

    xs = tuple(jnp.moveaxis(t, 1, 0) for t in (r, w, k, v, a, b))
    _, y = lax.scan(step, jnp.zeros((B, H, N, N), jnp.float32), xs, reverse=reverse)
    return jnp.moveaxis(y, 0, 1)

def odd_mixer(h, w_in, w_out, qn, kn, rel_bias, mu, w0, w2, a0, a2, g2, k_k, k_a, r_k, ln_w, ln_b):
    B, S, _ = h.shape
    f32 = jnp.float32
    p = h @ w_in
    q, k, v = jnp.split(p[..., :3 * DSA_QKV], 3, axis=-1)
    q = rms_norm(q.reshape(B, S, DSA_HEADS, DSA_HEAD_DIM), qn)
    k = rms_norm(k.reshape(B, S, DSA_HEADS, DSA_HEAD_DIM), kn)
    v = v.reshape(B, S, DSA_HEADS, DSA_HEAD_DIM)
    outs, lses = [], []
    for gi, (window, dil) in enumerate(DSA_PATTERNS):
        n_side = window // (2 * dil)
        hs = slice(gi * DSA_HEADS_PER_GROUP, (gi + 1) * DSA_HEADS_PER_GROUP)
        offs = jnp.arange(-n_side, n_side + 1, dtype=jnp.int32) * dil
        bias = jnp.transpose(rel_bias[t5_bucket(offs), hs]).astype(f32)
        o_g, lse_g = dilated_window_attention(q[:, :, hs], k[:, :, hs], v[:, :, hs], bias, dil, n_side)
        outs.append(o_g)
        lses.append(lse_g)
    wts = jax.nn.softmax(jnp.stack(lses), axis=0)
    y_c = jnp.sum(wts[..., None] * jnp.stack(outs), axis=0).reshape(B, S, DSA_OUT)

    rw = p[..., 3 * DSA_QKV:]
    rw = (rw + mu * (centred_token_shift(rw) - rw)).astype(f32)
    r, kr, vr, wd_f, wd_b, ad_f, ad_b, gd = jnp.split(rw, np.cumsum(RW_SPLITS)[:-1].tolist(), axis=-1)
    heads = lambda t: t.reshape(B, S, RW_HEADS, RW_HEAD_DIM)
    kk = l2_normalize(heads(kr * k_k.astype(f32)))
    gate = jax.nn.sigmoid(gd) @ g2.astype(f32)
    rh, vh = heads(r), heads(vr)
    ys, bonuses = [], []
    for d, (wd, ad) in enumerate(((wd_f, ad_f), (wd_b, ad_b))):
        w_log = -jax.nn.softplus(-(w0[d].astype(f32) + jnp.tanh(wd) @ w2[d].astype(f32))) - 0.5
        decay = jnp.exp(-jnp.exp(w_log))
        a = jax.nn.sigmoid(a0[d].astype(f32) + ad @ a2[d].astype(f32))
        kdh = heads(kr * (1.0 + (a - 1.0) * k_a.astype(f32)))
        ys.append(rwkv7_scan(rh, heads(decay), kdh, vh, -kk, kk * heads(a), reverse=(d == 1)))
        bonuses.append(jnp.sum(rh * kdh * r_k.astype(f32), axis=-1, keepdims=True) * vh)
    y = ys[0] + ys[1]
    mean = jnp.mean(y, axis=-1, keepdims=True)
    var = jnp.mean(jnp.square(y - mean), axis=-1, keepdims=True)
    yn = ((y - mean) * lax.rsqrt(var + RW_GN_EPS)).reshape(B, S, RW_WIDTH) * ln_w.astype(f32) + ln_b.astype(f32)
    y_d = (yn + (bonuses[0] + bonuses[1]).reshape(B, S, RW_WIDTH)) * gate
    return jnp.concatenate([y_c.astype(h.dtype), y_d.astype(h.dtype)], axis=-1) @ w_out

def memory_cross_attention(h, mem_n, wq, wk, wv, wo, qn, kn):
    B, S, _ = h.shape
    M = mem_n.shape[1]
    q = rms_norm((h @ wq).reshape(B, S, XA_HEADS, XA_HEAD_DIM), qn)
    k = rms_norm((mem_n @ wk).reshape(B, M, XA_HEADS, XA_HEAD_DIM), kn)
    v = (mem_n @ wv).reshape(B, M, XA_HEADS, XA_HEAD_DIM)
    logits = jnp.einsum('bshe,bmhe->bhsm', q, k).astype(jnp.float32) * (XA_HEAD_DIM ** -0.5)
    p = jax.nn.softmax(logits, axis=-1)
    o = jnp.einsum('bhsm,bmhe->bshe', p.astype(v.dtype), v).reshape(B, S, XA_WIDTH)
    return o @ wo

def squared_relu_mlp(h, w1, w2):
    return jnp.square(jax.nn.relu(h @ w1)) @ w2

def setup_inputs(seed: int = 0) -> dict:
    key = jax.random.key(seed)
    ks = iter(jax.random.split(key, 48))
    f32 = jnp.float32
    D = D_MODEL
    NE, NO = N_EVEN, N_ODD

    def nrm(shape, scale):
        return jax.random.normal(next(ks), shape, f32) * scale

    def gain(shape):
        return 1.0 + 0.02 * jax.random.normal(next(ks), shape, f32)

    x = nrm((BATCH, SEQ, D), 1.0)
    mem = nrm((BATCH, N_MEM, D), 1.0)
    rel_bias = nrm((REL_BUCKETS, DSA_HEADS), 0.2)
    norm_mix = gain((DEPTH, D))
    norm_xattn = gain((DEPTH, D))
    norm_mem = gain((DEPTH, D))
    norm_ffn = gain((DEPTH, D))
    xa_wq = nrm((DEPTH, D, XA_WIDTH), D ** -0.5)
    xa_wk = nrm((DEPTH, D, XA_WIDTH), D ** -0.5)
    xa_wv = nrm((DEPTH, D, XA_WIDTH), D ** -0.5)
    xa_wo = nrm((DEPTH, XA_WIDTH, D), XA_WIDTH ** -0.5)
    xa_qn = gain((DEPTH, XA_HEAD_DIM))
    xa_kn = gain((DEPTH, XA_HEAD_DIM))
    ffn_w1 = nrm((DEPTH, D, D_FF), D ** -0.5)
    ffn_w2 = nrm((DEPTH, D_FF, D), D_FF ** -0.5)
    ev_w_in = nrm((NE, D, EV_IN), D ** -0.5)
    ev_w_out = nrm((NE, EV_OUT, D), EV_OUT ** -0.5)
    dn_conv = nrm((NE, 3 * DN_WIDTH, DN_CONV), DN_CONV ** -0.5)
    dn_a_log = jnp.log(jax.random.uniform(next(ks), (NE, 2, DN_HEADS), f32, 1.0, 16.0))
    dt = jnp.exp(jax.random.uniform(next(ks), (NE, 2, DN_HEADS), f32, math.log(1e-3), math.log(1e-1)))
    dn_dt_bias = dt + jnp.log(-jnp.expm1(-dt))
    dn_norm = gain((NE, DN_HEAD_DIM))
    sc_conv = nrm((NE, SC_WIDTH, SC_CONV), SC_CONV ** -0.5)
    od_w_in = nrm((NO, D, OD_IN), D ** -0.5)
    od_w_out = nrm((NO, OD_OUT, D), OD_OUT ** -0.5)
    ca_qn = gain((NO, DSA_HEAD_DIM))
    ca_kn = gain((NO, DSA_HEAD_DIM))
    rw_mu = jax.random.uniform(next(ks), (NO, RW_IN), f32, 0.0, 1.0)
    rw_w0 = -2.0 + nrm((NO, 2, RW_WIDTH), 0.5)
    rw_w2 = nrm((NO, 2, RW_DECAY_LORA, RW_WIDTH), 0.5 * RW_DECAY_LORA ** -0.5)
    rw_a0 = nrm((NO, 2, RW_WIDTH), 0.5)
    rw_a2 = nrm((NO, 2, RW_AAA_LORA, RW_WIDTH), 0.5 * RW_AAA_LORA ** -0.5)
    rw_g2 = nrm((NO, RW_GATE_LORA, RW_WIDTH), RW_GATE_LORA ** -0.5)
    rw_k_k = 0.85 + nrm((NO, RW_WIDTH), 0.02)
    rw_k_a = gain((NO, RW_WIDTH))
    rw_r_k = nrm((NO, RW_HEADS, RW_HEAD_DIM), 0.1)
    rw_ln_w = gain((NO, RW_WIDTH))
    rw_ln_b = nrm((NO, RW_WIDTH), 0.01)
    return {'x': x, 'mem': mem, 'rel_bias': rel_bias, 'norm_mix': norm_mix, 'norm_xattn': norm_xattn,
            'norm_mem': norm_mem, 'norm_ffn': norm_ffn, 'xa_wq': xa_wq, 'xa_wk': xa_wk, 'xa_wv': xa_wv,
            'xa_wo': xa_wo, 'xa_qn': xa_qn, 'xa_kn': xa_kn, 'ffn_w1': ffn_w1, 'ffn_w2': ffn_w2,
            'ev_w_in': ev_w_in, 'ev_w_out': ev_w_out, 'dn_conv': dn_conv, 'dn_a_log': dn_a_log,
            'dn_dt_bias': dn_dt_bias, 'dn_norm': dn_norm, 'sc_conv': sc_conv, 'od_w_in': od_w_in,
            'od_w_out': od_w_out, 'ca_qn': ca_qn, 'ca_kn': ca_kn, 'rw_mu': rw_mu, 'rw_w0': rw_w0,
            'rw_w2': rw_w2, 'rw_a0': rw_a0, 'rw_a2': rw_a2, 'rw_g2': rw_g2, 'rw_k_k': rw_k_k,
            'rw_k_a': rw_k_a, 'rw_r_k': rw_r_k, 'rw_ln_w': rw_ln_w, 'rw_ln_b': rw_ln_b}

def reference(x, mem, rel_bias, norm_mix, norm_xattn, norm_mem, norm_ffn, xa_wq, xa_wk, xa_wv, xa_wo,
              xa_qn, xa_kn, ffn_w1, ffn_w2, ev_w_in, ev_w_out, dn_conv, dn_a_log, dn_dt_bias, dn_norm,
              sc_conv, od_w_in, od_w_out, ca_qn, ca_kn, rw_mu, rw_w0, rw_w2, rw_a0, rw_a2, rw_g2,
              rw_k_k, rw_k_a, rw_r_k, rw_ln_w, rw_ln_b):
    for layer in range(DEPTH):
        i = layer // 2
        h = rms_norm(x, norm_mix[layer])
        if layer % 2 == 0:
            x = x + even_mixer(h, ev_w_in[i], ev_w_out[i], dn_conv[i], dn_a_log[i], dn_dt_bias[i],
                               dn_norm[i], sc_conv[i])
        else:
            x = x + odd_mixer(h, od_w_in[i], od_w_out[i], ca_qn[i], ca_kn[i], rel_bias, rw_mu[i],
                              rw_w0[i], rw_w2[i], rw_a0[i], rw_a2[i], rw_g2[i], rw_k_k[i], rw_k_a[i],
                              rw_r_k[i], rw_ln_w[i], rw_ln_b[i])
        x = x + memory_cross_attention(rms_norm(x, norm_xattn[layer]), rms_norm(mem, norm_mem[layer]),
                                       xa_wq[layer], xa_wk[layer], xa_wv[layer], xa_wo[layer],
                                       xa_qn[layer], xa_kn[layer])
        x = x + squared_relu_mlp(rms_norm(x, norm_ffn[layer]), ffn_w1[layer], ffn_w2[layer])
    return x


_drawn_inputs = setup_inputs


def setup_inputs(seed=0):
    import zlib

    import numpy as np

    out = dict(_drawn_inputs(seed))
    spreads = {}
    factors = {'rel_bias': 5.944,
     'norm_xattn': 8.0,
     'norm_mem': 8.0,
     'xa_qn': 8.0,
     'xa_kn': 8.0,
     'dn_norm': 7.691,
     'ca_qn': 8.0,
     'ca_kn': 8.0,
     'rw_w2': 3.732,
     'rw_k_k': 30.554,
     'rw_k_a': 8.0,
     'rw_ln_w': 8.0,
     'rw_ln_b': 29.275}
    for name, (base, spread) in spreads.items():
        noise = np.random.default_rng([zlib.crc32(name.encode()), seed]).standard_normal(out[name].shape)
        drawn = base * np.exp(spread * noise) if base else spread * noise
        out[name] = jnp.asarray(drawn.astype(out[name].dtype))
    for name, factor in factors.items():
        out[name] = (out[name] * factor).astype(out[name].dtype)
    return out
```

```python
from contextlib import ExitStack

import concourse.bass as bass
from concourse import mybir

P = 128
D = 2048
S = 256
NT = S // P
KD = D // P
RING = 4
WORK = 23040
UNIT_K = 8
UNIT = UNIT_K * 512
F_FF = 4 * D
RMS_EPS = 1e-6

ALU = mybir.AluOpType
ACT = mybir.ActivationFunctionType
F32 = mybir.dt.float32
AX_X = mybir.AxisListType.X

MULT, ADD, SUB, MAX = ALU.mult, ALU.add, ALU.subtract, ALU.max

DN_H = 8
DN_W = DN_H * P
DSA_G = 3
DSA_HG = 4
DSA_H = DSA_G * DSA_HG
DILATIONS = (1, 4, 16)
N_SIDE = 64
N_BUCKETS = 32
MAX_DIST = 1024
NEG = -1e30
RW_H = 8
RW_N = 64
RW_W = RW_H * RW_N
RW_F = RW_W // P
KAPPA = 0.6065306597126334
GN_EPS = 64e-5
XA_H = 4
HEAD_SCALE = float(P) ** -0.5
LEVELS = 7

GEMMS = [
    ("mem_k0", 1, 2), ("mem_v0", 1, 2), ("mem_k1", 1, 2), ("mem_v1", 1, 2),
    ("ev_qkv", 6, 2), ("ev_gate", 2, 2), ("ev_sc", 6, 2), ("ev_out", 4, 2),
    ("xa_q0", 1, 2), ("xa_o0", 4, 0.5), ("ffn_up0", 16, 2), ("ffn_down0", 4, 8),
    ("od_q", 3, 2), ("od_k", 3, 2), ("od_v", 3, 2), ("od_rw", 4, 2), ("od_out", 4, 1),
    ("xa_q1", 1, 2), ("xa_o1", 4, 0.5), ("ffn_up1", 16, 2), ("ffn_down1", 4, 8),
]


def gemm_starts():
    at, chunk, unit = {}, 0, 0
    for name, chunks, units in GEMMS:
        at[name] = (chunk, unit)
        chunk += chunks
        unit += int(chunks * units)
    return at, chunk, unit


CONST_COLS = [
    ("ident", P), ("level", 2 * LEVELS * P),
    ("neg", 2 * P), ("cum_mid", 4 * P), ("causal", 4 * P), ("halves", P), ("ones", 1), ("half_cols", 2),
]
PARAM_COLS = [
    ("g_mix0", 16), ("g_mix1", 16), ("g_xattn0", 16), ("g_xattn1", 16),
    ("g_mem0", 16), ("g_mem1", 16), ("g_ffn0", 16), ("g_ffn1", 16),
    ("xa_qn", 2), ("xa_kn", 2), ("dn_conv", 72), ("sc_conv", 24), ("dn_norm", P),
    ("a_log", 16), ("dt_bias", 16), ("ab_w", 512),
    ("ca_qn", 1), ("ca_kn", 1), ("rw_mu", 15), ("rw_a0", 8), ("rw_kk", 4), ("rw_ka", 4), ("rw_rk", 4),
]
WIDE_COLS = [("w2", 512), ("a2", 512), ("g2", 512), ("w0", 1024), ("ln_w", 512), ("ln_b", 512)]


def columns(table):
    at, n = {}, 0
    for name, width in table:
        at[name] = slice(n, n + width)
        n += width
    return at, n


class Chain:

    def __init__(self, engine, sem):
        self.engine, self.sem, self.n = engine, sem, 0

    def __call__(self, instruction):
        self.n += 1
        instruction.then_inc(self.sem, 1)
        self.engine.wait_ge(self.sem, self.n)


def build(nc, x_in, mem_in, stream, small, wide, masks, bias_table, rel_bias, bias_rows, x_out):
    starts, n_chunks, n_loaded = gemm_starts()
    C, n_const = columns(CONST_COLS)
    Q, n_param = columns(PARAM_COLS)
    WD, n_wide = columns(WIDE_COLS)

    ctx = ExitStack()
    with ctx:
        def sb(name, shape):
            return ctx.enter_context(nc.sbuf_tensor(name, shape, F32))

        def sem(name):
            return ctx.enter_context(nc.semaphore(name))

        x = sb("x", [P, NT, D])
        hT = sb("hT", [P, KD, S])
        ring = sb("ring", [P, RING, UNIT])
        work = sb("work", [P, WORK])
        const = sb("const", [P, n_const])
        par = sb("par", [P, n_param])
        mem_kT = [sb(f"mem_kT{l}", [P, XA_H, S]) for l in range(2)]
        mem_v = [sb(f"mem_v{l}", [P, NT, XA_H * P]) for l in range(2)]
        st = sb("st", [P, 768])
        bank = [ctx.enter_context(nc.psum_tensor(f"bank{i}", [P, 512], F32)) for i in range(8)]
        aux = bank[4:]

        def W(at, *shape):
            n = 1
            for d in shape:
                n *= d
            v = work[:, at:at + n]
            if len(shape) == 1:
                return v
            names = "abcd"[:len(shape)]
            return v.rearrange(f"p ({' '.join(names)}) -> p {' '.join(names)}",
                               **dict(zip(names[1:], shape[1:])))

        def four(ap):
            return ap[:, :].rearrange("p (m n) -> p m n", n=P)

        def const_of(name, i, width=P):
            return const[:, C[name].start + i * width:C[name].start + (i + 1) * width]

        ident = const[:, C["ident"]]
        ones_col = const[:, C["ones"]]

        s_load = sem("s_load")
        s_unit = [sem(f"s_unit{i}") for i in range(RING)]
        s_used = sem("s_used")
        s_taken = [sem(f"s_taken{i}") for i in range(2)]
        s_dve, s_act, s_pool = sem("s_dve"), sem("s_act"), sem("s_pool")
        s_sq = sem("s_sq")
        s_ms = sem("s_ms")
        s_sd = sem("s_sd")
        s_rstd = sem("s_rstd")
        s_xn = sem("s_xn")
        s_tr = sem("s_tr")
        s_hT_a, s_hT_d = sem("s_hT_a"), sem("s_hT_d")
        s_mk_sq, s_mk_ms, s_mk_sd, s_mk = sem("s_mk_sq"), sem("s_mk_ms"), sem("s_mk_sd"), sem("s_mk")
        s_mk_tr, s_mkT = sem("s_mk_tr"), sem("s_mkT")
        s_xq, s_xss, s_xms, s_xsd, s_xrq = (sem(n) for n in ("s_xq", "s_xss", "s_xms", "s_xsd", "s_xrq"))
        s_xlog, s_xnm, s_xexp, s_xp = sem("s_xlog"), sem("s_xnm"), sem("s_xexp"), sem("s_xp")
        s_xpt, s_xpt_a, s_xpt_d = sem("s_xpt"), sem("s_xpt_a"), sem("s_xpt_d")
        s_xo, s_xoT = sem("s_xo"), sem("s_xoT")
        s_u = sem("s_u")
        s_gqk = sem("s_gqk")
        s_out = sem("s_out")
        iv_mt, iv_p, iv_ps, iv_q, iv_t = (sem(n) for n in ("iv_mt", "iv_p", "iv_ps", "iv_q", "iv_t"))
        s_ab, s_abv, s_ax, s_sp, s_g = (sem(n) for n in ("s_ab", "s_abv", "s_ax", "s_sp", "s_g"))
        s_cv, s_silu, s_scb = sem("s_cv"), sem("s_silu"), sem("s_scb")
        s_dsq, s_kvt, s_kv_a, s_kv_d = sem("s_dsq"), sem("s_kvt"), sem("s_kv_a"), sem("s_kv_d")
        s_dss, s_cum, s_cumv, s_dms, s_dsd, s_dE, s_stats = (
            sem(n) for n in ("s_dss", "s_cum", "s_cumv", "s_dms", "s_dsd", "s_dE", "s_stats"))
        s_pre, s_diff, s_D, s_eg, s_AT, s_qtg, s_vb = (
            sem(n) for n in ("s_pre", "s_diff", "s_D", "s_eg", "s_AT", "s_qtg", "s_vb"))
        s_vn1, s_vn1s, s_S, s_Ss, s_kS, s_R, s_vn2, s_vn2s, s_o, s_os = (
            sem(n) for n in ("s_vn1", "s_vn1s", "s_S", "s_Ss", "s_kS", "s_R", "s_vn2", "s_vn2s", "s_o", "s_os"))
        s_oms, s_osd, s_y, s_yt, s_yT = (sem(n) for n in ("s_oms", "s_osd", "s_y", "s_yt", "s_yT"))
        s_bt_in, s_bias_m, s_bias_s, s_bias_out, s_bias_in = (
            sem(n) for n in ("s_bt_in", "s_bias_m", "s_bias_s", "s_bias_out", "s_bias_in"))
        s_neg = sem("s_neg")
        s_gca, s_oss, s_oms0, s_osd0, s_orq = (sem(n) for n in ("s_gca", "s_oss", "s_oms0", "s_osd0", "s_orq"))
        s_kms, s_ksd, s_ok, s_okt, s_okT_a, s_okT_d = (
            sem(n) for n in ("s_kms", "s_ksd", "s_ok", "s_okt", "s_okT_a", "s_okT_d"))
        s_ol, s_ol_used, s_onm, s_oexp, s_op, s_opt, s_opt_a, s_opt_d, s_opv, s_oyc = (
            sem(n) for n in ("s_ol", "s_ol_used", "s_onm", "s_oexp", "s_op", "s_opt", "s_opt_a", "s_opt_d", "s_opv", "s_oyc"))
        s_wide, s_rw, s_rtanh, s_rwm, s_rlw0, s_lw, s_rgm, s_rgs, s_ram, s_ra, s_rvt, s_rv = (
            sem(n) for n in ("s_wide", "s_rw", "s_rtanh", "s_rwm", "s_rlw0", "s_lw", "s_rgm", "s_rgs", "s_ram", "s_ra", "s_rvt", "s_rv"))
        s_kk0, s_kksq, s_kkm, s_kkms, s_kksd, s_kk, s_kd, s_pr, s_prm, s_bon, s_b = (
            sem(n) for n in ("s_kk0", "s_kksq", "s_kkm", "s_kkms", "s_kksd", "s_kk", "s_kd", "s_pr", "s_prm", "s_bon", "s_b"))
        s_rc, s_rF, s_rRA, s_rbk, s_rM, s_rMAT, s_rbt, s_rBK, s_rz1, s_rz1s = (
            sem(n) for n in ("s_rc", "s_rF", "s_rRA", "s_rbk", "s_rM", "s_rMAT", "s_rbt", "s_rBK", "s_rz1", "s_rz1s"))
        s_gms, s_gsd, s_ry, s_ryt, s_ryT = (sem(n) for n in ("s_gms", "s_gsd", "s_ry", "s_ryt", "s_ryT"))
        block = ctx.enter_context(nc.Block())

        NORMS = ["mem0", "mem1", "mix0", "xattn0", "ffn0", "mix1", "xattn1", "ffn1"]
        NORM_NO = {name: i for i, name in enumerate(NORMS)}
        xn = W(8192, NT, D)
        memx = W(12288, NT, D)

        dve_chain, act_chain, pool_chain = Chain(nc.vector, s_dve), Chain(nc.scalar, s_act), Chain(nc.gpsimd, s_pool)
        dve_step, act_step, pool_step = dve_chain, act_chain, pool_chain

        def wait_chunks_taken(eng, chunk):
            for parity in range(2):
                n = (chunk + 1 - parity) // 2
                if n:
                    eng.wait_ge(s_taken[parity], 2 * n)

        ss, msq, sdv, rstd = st[:, 0:2], st[:, 2:4], st[:, 4:6], st[:, 6:8]
        mk_ss, mk_ms, mk_sd, mk_r = (st[:, 8 + 8 * i:16 + 8 * i] for i in range(4))
        xa_ms, xa_sd, xa_r, xa_rq = (st[:, 40 + 8 * i:48 + 8 * i] for i in range(4))
        xa_mx, xa_nm, xa_sum, xa_rs = (st[:, 72 + 8 * i:80 + 8 * i] for i in range(4))
        gqk = st[:, 104:106]

        class Gemm:

            def __init__(self, pe, name):
                self.pe = pe
                self.chunk0, self.unit0 = starts[name]
                self.per = dict((n, u) for n, _, u in GEMMS)[name]

            def unit(self, j, turn=0, units_per_turn=0):
                u = self.unit0 + j
                self.pe.wait_ge(s_unit[u % RING], (turn * (units_per_turn // RING) + u // RING + 1) * 16)
                return ring[:, u % RING, :]

            def banks(self, c, turn=0, chunks_per_turn=0):
                g = self.chunk0 + c
                if g >= 2:
                    self.pe.wait_ge(s_taken[g % 2], (turn * (chunks_per_turn // 2) + g // 2) * 2)
                return bank[2 * (g % 2):2 * (g % 2) + 2]

            def row_chunk(self, c, lhsT, k_tiles=KD, turn=0, turns=(0, 0)):
                acc = self.banks(c, turn, turns[0])
                for j in range(k_tiles // UNIT_K):
                    w = self.unit(int(c * self.per) + j, turn, turns[1])
                    for kk in range(UNIT_K):
                        k = j * UNIT_K + kk
                        for t in range(NT):
                            m = nc.tensor.matmul(acc[t][:, :], lhsT=lhsT(k, t), rhs=w[:, kk * 512:(kk + 1) * 512],
                                                 start=k == 0, stop=k == k_tiles - 1)
                    m.then_inc(s_used, 2)

            def half_unit_chunk(self, c, lhsT):
                acc = self.banks(c)
                w = self.unit(c // 2)
                for k in range(XA_H):
                    for t in range(NT):
                        m = nc.tensor.matmul(acc[t][:, :], lhsT=lhsT(k, t),
                                             rhs=w[:, k * 1024 + (c % 2) * 512:k * 1024 + (c % 2 + 1) * 512],
                                             start=k == 0, stop=k == XA_H - 1)
                m.then_inc(s_used, 1)

            def column_chunk(self, c, turn=0, turns=(0, 0), tiles=4):
                acc = self.banks(c, turn, turns[0])
                w = [self.unit(int(c * self.per) + j, turn, turns[1]) for j in range(2)]
                for i in range(tiles):
                    for k in range(KD):
                        kk = k % UNIT_K
                        m = nc.tensor.matmul(acc[i // 2][:, (i % 2) * S:(i % 2 + 1) * S],
                                             lhsT=w[k // UNIT_K][:, kk * 512 + i * P:kk * 512 + (i + 1) * P],
                                             rhs=hT[:, k, :], start=k == 0, stop=k == KD - 1)
                        if i == tiles - 1 and kk == UNIT_K - 1 and k < KD - 1:
                            m.then_inc(s_used, 2)
                m.then_inc(s_used, 2)

        def chunk_done(name, c, turn=0, units_per_turn=0):
            per = dict((n, u) for n, _, u in GEMMS)[name]
            return turn * (2 * units_per_turn) + (2 * starts[name][1] + int(2 * per * (c + 1)))

        def chunk_banks(name, c):
            parity = (starts[name][0] + c) % 2
            return bank[2 * parity:2 * parity + 2], s_taken[parity]

        @block.sync
        def _(sp):
            sp.dma_start(const[:, :], masks).then_inc(s_load, 16)
            sp.dma_start(memx, mem_in.rearrange("(t p) d -> p t d", p=P)).then_inc(s_load, 16)
            sp.dma_start(par[:, :], small).then_inc(s_load, 16)

            def load(u, slot):
                sp.dma_start(ring[:, slot, :], stream[u]).then_inc(s_unit[slot], 16)

            for slot in range(RING):
                load(slot, slot)
            sp.dma_start(x[:, :, :], x_in.rearrange("(t p) d -> p t d", p=P)).then_inc(s_load, 16)
            with sp.Fori(1, n_loaded // RING) as turn:
                for slot in range(RING):
                    sp.wait_ge(s_used, turn * (2 * RING) + 2 * (slot - RING + 1))
                    load(turn * RING + slot, slot)
            for u in range(n_loaded // RING * RING, n_loaded):
                sp.wait_ge(s_used, 2 * (u - RING + 1))
                load(u, u % RING)
            wait_chunks_taken(sp, n_chunks)
            sp.dma_start(x_out.rearrange("(t p) d -> p t d", p=P), x[:, :, :]).then_inc(s_out, 16)
            sp.wait_ge(s_out, 16)

        def pe_norm(pe, name, before=()):
            n = NORM_NO[name]
            pe.wait_ge(s_xn, 2 * n + 2)
            for sem_, value in before:
                pe.wait_ge(sem_, value)
            for b in range(8):
                if b >= 4:
                    pe.wait_ge((s_hT_a, s_hT_d)[b % 2], 4 * n + (b - 4) // 2 + 1)
                for i in range(2):
                    for t in range(NT):
                        k = 2 * b + i
                        m = nc.tensor.transpose(aux[b % 4][:, (2 * i + t) * P:(2 * i + t + 1) * P],
                                                xn[:, t, k * P:(k + 1) * P], ident)
                m.then_inc(s_tr, 1)

        def gain_out(eng_is_act, name, b, n):
            for i in range(2):
                k = 2 * b + i
                src = aux[b % 4][:, i * S:(i + 1) * S]
                g = par[:, Q[f"g_{name}"].start + k:Q[f"g_{name}"].start + k + 1]
                if eng_is_act:
                    m = nc.scalar.activation(hT[:, k, :], src, ACT.Copy, scale=g)
                else:
                    m = nc.vector.tensor_scalar(hT[:, k, :], src, g, None, MULT)
            m.then_inc(s_hT_a if eng_is_act else s_hT_d, 1)

        def act_norm(act, name, src, hT_free):
            n = NORM_NO[name]
            if n:
                act.wait_ge(s_tr, 8 * n)
            nc.scalar.activation(xn[:, 0, :], src[:, 0, :], ACT.Square, accum_out=ss[:, 0:1]).then_inc(s_sq, 1)
            act.wait_ge(s_ms, n + 1)
            nc.scalar.activation(sdv, msq, ACT.Sqrt).then_inc(s_sd, 1)
            act.wait_ge(s_rstd, n + 1)
            nc.scalar.activation(xn[:, 0, :], src[:, 0, :], ACT.Copy, scale=rstd[:, 0:1]).then_inc(s_xn, 1)
            act.wait_ge(s_used, hT_free)
            for b in range(0, 8, 2):
                act.wait_ge(s_tr, 8 * n + b + 1)
                gain_out(True, name, b, n)

        def dve_norm(dve, name, src, hT_free):
            n = NORM_NO[name]
            if n:
                dve.wait_ge(s_tr, 8 * n)
            dve_step(nc.vector.tensor_tensor_reduce(out=xn[:, 1, :], in0=src[:, 1, :], in1=src[:, 1, :], scale=1.0,
                                                    scalar=0.0, op0=MULT, op1=ADD, accum_out=ss[:, 1:2]))
            dve.wait_ge(s_sq, n + 1)
            nc.vector.tensor_scalar(msq, ss, 1.0 / D, RMS_EPS, MULT, ADD).then_inc(s_ms, 1)
            dve.wait_ge(s_sd, n + 1)
            nc.vector.reciprocal(rstd, sdv).then_inc(s_rstd, 1)
            dve.wait_ge(s_rstd, n + 1)
            nc.vector.tensor_scalar(xn[:, 1, :], src[:, 1, :], rstd[:, 1:2], None, MULT).then_inc(s_xn, 1)
            dve.wait_ge(s_used, hT_free)
            for b in range(1, 8, 2):
                dve.wait_ge(s_tr, 8 * n + b + 1)
                gain_out(False, name, b, n)

        def pe_hT(pe, name):
            n = NORM_NO[name]
            pe.wait_ge(s_hT_a, 4 * n + 4)
            pe.wait_ge(s_hT_d, 4 * n + 4)

        mk = W(0, NT, XA_H * P)
        mk_sq = W(1024, NT, XA_H * P)

        def heads8(ap):
            return ap.rearrange("p t (h e) -> p (t h) e", e=P)

        def lanes(ap, n):
            return ap.unsqueeze(2).broadcast_to([P, ap.shape[1], n])

        def hT_tile(k, t):
            return hT[:, k, t * P:(t + 1) * P]

        def pe_memory(pe, l):
            pe_hT(pe, f"mem{l}")
            Gemm(pe, f"mem_k{l}").row_chunk(0, hT_tile)
            Gemm(pe, f"mem_v{l}").row_chunk(0, hT_tile)
            pe.wait_ge(s_mk, l + 1)
            for h in range(XA_H):
                for t in range(NT):
                    m = nc.tensor.transpose(aux[h // 2][:, ((h % 2) * NT + t) * P:((h % 2) * NT + t + 1) * P],
                                            mk[:, t, h * P:(h + 1) * P], ident)
                if h % 2:
                    m.then_inc(s_mk_tr, 1)

        def take_row_chunk(act, name, c, dst):
            banks, taken = chunk_banks(name, c)
            act.wait_ge(s_used, chunk_done(name, c))
            for t in range(NT):
                nc.scalar.activation(dst(t), banks[t][:, :], ACT.Copy).then_inc(taken, 1)

        def act_memory(act, l):
            take_row_chunk(act, f"mem_k{l}", 0, lambda t: mk[:, t, :])
            take_row_chunk(act, f"mem_v{l}", 0, lambda t: mem_v[l][:, t, :])
            act.wait_ge(s_mk_ms, l + 1)
            nc.scalar.activation(mk_sd, mk_ms, ACT.Sqrt).then_inc(s_mk_sd, 1)
            for b in range(2):
                act.wait_ge(s_mk_tr, 2 * l + b + 1)
                nc.scalar.activation(mem_kT[l][:, 2 * b:2 * b + 2, :], aux[b][:, :].rearrange("p (h s) -> p h s", s=S),
                                     ACT.Copy).then_inc(s_mkT, 1)

        def dve_memory(dve, l):
            parity = starts[f"mem_k{l}"][0] % 2
            dve.wait_ge(s_taken[parity], 2 * (starts[f"mem_k{l}"][0] // 2 + 1))
            dve_step(nc.vector.tensor_tensor(mk_sq, mk, mk, MULT))
            dve_step(nc.vector.reduce_sum(mk_ss, heads8(mk_sq), AX_X))
            nc.vector.tensor_scalar(mk_ms, mk_ss, 1.0 / P, RMS_EPS, MULT, ADD).then_inc(s_mk_ms, 1)
            dve.wait_ge(s_mk_sd, l + 1)
            dve_step(nc.vector.reciprocal(mk_r, mk_sd))
            nc.vector.tensor_tensor(heads8(mk), heads8(mk), lanes(mk_r, P), MULT).then_inc(s_mk, 1)

        xq_sq, xqT = W(0, XA_H, S), W(1024, XA_H, S)
        xp = W(2048, NT, XA_H, S)
        xpT = W(4096, NT, XA_H, S)
        xoT = W(6144, XA_H, S)

        def pe_cross(pe, l):
            pe_hT(pe, f"xattn{l}")
            Gemm(pe, f"xa_q{l}").column_chunk(0)
            pe.wait_ge(s_xq, l + 1)
            for t in range(NT):
                for h in range(XA_H):
                    m = nc.tensor.matmul(aux[0][:, t * XA_H + h:t * XA_H + h + 1],
                                         lhsT=xq_sq[:, h, t * P:(t + 1) * P], rhs=ones_col, start=True, stop=True)
            m.then_inc(s_xss, 1)
            for b in list(range(1, 4)) + [0]:
                t, hp = b // 2, b % 2
                if b == 0:
                    pe.wait_ge(s_xms, l + 1)
                for i in range(2):
                    h = 2 * hp + i
                    m = nc.tensor.matmul(aux[b][:, i * S:(i + 1) * S], lhsT=xqT[:, h, t * P:(t + 1) * P],
                                         rhs=mem_kT[l][:, h, :], start=True, stop=True)
                m.then_inc(s_xlog, 1)
            for n, b in enumerate(XB):
                t, hp = b // 2, b % 2
                pe.wait_ge(s_xp, 4 * l + n + 1)
                for i in range(2):
                    for mt in range(NT):
                        m = nc.tensor.transpose(aux[b][:, (2 * i + mt) * P:(2 * i + mt + 1) * P],
                                                xp[:, t, 2 * hp + i, mt * P:(mt + 1) * P], ident)
                m.then_inc(s_xpt, 1)
            pe.wait_ge(s_xpt_a, 2 * l + 2)
            pe.wait_ge(s_xpt_d, 2 * l + 2)
            for h in range(XA_H):
                for mt in range(NT):
                    m = nc.tensor.matmul(aux[h // 2][:, (h % 2) * S:(h % 2 + 1) * S],
                                         lhsT=mem_v[l][:, mt, h * P:(h + 1) * P], rhs=xpT[:, mt, h, :],
                                         start=mt == 0, stop=mt == NT - 1)
                if h % 2:
                    m.then_inc(s_xo, 1)
            pe.wait_ge(s_xoT, 2 * l + 2)
            for c in range(4):
                Gemm(pe, f"xa_o{l}").half_unit_chunk(c, lambda k, t: xoT[:, k, t * P:(t + 1) * P])

        XB = [1, 2, 3, 0]

        def pt_out(b):
            t, hp = b // 2, b % 2
            dst = xpT[:, :, 2 * hp:2 * hp + 2, t * P:(t + 1) * P].rearrange("p m i s -> p i m s")
            return dst, aux[b][:, :].rearrange("p (i m s) -> p i m s", i=2, s=P)

        def act_cross(act, l):
            name = f"xa_q{l}"
            banks, taken = chunk_banks(name, 0)
            act.wait_ge(s_used, chunk_done(name, 0))
            act.wait_ge(s_gqk, 1)
            for b in range(2):
                v = banks[b][:, :].rearrange("p (h s) -> p h s", s=S)
                nc.scalar.activation(xq_sq[:, 2 * b:2 * b + 2, :], v, ACT.Square)
                m = nc.scalar.activation(xqT[:, 2 * b:2 * b + 2, :], v, ACT.Copy, scale=gqk[:, l:l + 1])
                m.then_inc(taken, 1)
            act.wait_ge(taken, 2 * (starts[name][0] // 2 + 1))
            act.sem_inc(s_xq, 1)
            act.wait_ge(s_xms, l + 1)
            nc.scalar.activation(xa_sd, xa_ms, ACT.Sqrt).then_inc(s_xsd, 1)
            for n, b in enumerate(XB):
                t, hp = b // 2, b % 2
                act.wait_ge(s_xnm, 4 * l + n + 1)
                for i in range(2):
                    j = t * XA_H + 2 * hp + i
                    nc.scalar.activation(xp[:, t, 2 * hp + i, :], aux[b][:, i * S:(i + 1) * S], ACT.Exp,
                                         bias=xa_nm[:, j:j + 1], scale=xa_rq[:, j:j + 1],
                                         accum_out=xa_sum[:, j:j + 1]).then_inc(s_xexp, 1)
            for n, b in enumerate(XB):
                if b >= 2:
                    continue
                act.wait_ge(s_xpt, 4 * l + n + 1)
                dst, src = pt_out(b)
                for i in range(2):
                    m = nc.scalar.activation(dst[:, i], src[:, i], ACT.Copy)
                m.then_inc(s_xpt_a, 1)
            for b in range(2):
                act.wait_ge(s_xo, 2 * l + b + 1)
                nc.scalar.activation(xoT[:, 2 * b:2 * b + 2, :], aux[b][:, :].rearrange("p (h s) -> p h s", s=S),
                                     ACT.Copy).then_inc(s_xoT, 1)

        def dve_cross(dve, l):
            dve.wait_ge(s_xss, l + 1)
            nc.vector.tensor_scalar(xa_ms, aux[0][:, 0:8], 1.0 / P, RMS_EPS, MULT, ADD).then_inc(s_xms, 1)
            dve.wait_ge(s_xsd, l + 1)
            dve_step(nc.vector.reciprocal(xa_r, xa_sd))
            dve_step(nc.vector.tensor_scalar(xa_rq, xa_r, HEAD_SCALE, None, MULT))
            for n, b in enumerate(XB):
                t, hp = b // 2, b % 2
                j = slice(t * XA_H + 2 * hp, t * XA_H + 2 * hp + 2)
                dve.wait_ge(s_xlog, 4 * l + n + 1)
                dve_step(nc.vector.reduce_max(xa_mx[:, j], aux[b][:, :].rearrange("p (i m) -> p i m", i=2), AX_X))
                nc.vector.scalar_tensor_tensor(out=xa_nm[:, j], in0=xa_mx[:, j], scalar=-1.0, in1=xa_rq[:, j],
                                               op0=MULT, op1=MULT).then_inc(s_xnm, 1)
            for n, b in enumerate(XB):
                t, hp = b // 2, b % 2
                j = slice(t * XA_H + 2 * hp, t * XA_H + 2 * hp + 2)
                dve.wait_ge(s_xexp, 8 * l + 2 * n + 2)
                dve_step(nc.vector.reciprocal(xa_rs[:, j], xa_sum[:, j]))
                pv = xp[:, t, 2 * hp:2 * hp + 2, :]
                nc.vector.tensor_tensor(pv, pv, lanes(xa_rs[:, j], S), MULT).then_inc(s_xp, 1)
            for n, b in enumerate(XB):
                if b < 2:
                    continue
                dve.wait_ge(s_xpt, 4 * l + n + 1)
                dst, src = pt_out(b)
                nc.vector.tensor_copy(dst, src).then_inc(s_xpt_d, 1)
            for c in range(4):
                dve_add_to_x(dve, f"xa_o{l}", c)

        def dve_add_to_x(dve, name, c, turn=0, turns=(0, 0)):
            banks, taken = chunk_banks(name, c)
            dve.wait_ge(s_used, chunk_done(name, c, turn, turns[1]))
            for t in range(NT):
                cols = x[:, t, bass.ds((turn * turns[0] + c) * 512, 512)]
                nc.vector.tensor_tensor(cols, cols, banks[t][:, :], ADD).then_inc(taken, 1)

        uT = W(0, F_FF // P, S)

        def pe_ffn(pe, l):
            pe_hT(pe, f"ffn{l}")
            up, down = Gemm(pe, f"ffn_up{l}"), Gemm(pe, f"ffn_down{l}")
            with pe.Fori(0, 8) as turn:
                for c in range(2):
                    up.column_chunk(c, turn, (2, 4))
            pe.wait_ge(s_u, 32 * (l + 1))
            with pe.Fori(0, 2) as turn:
                for c in range(2):
                    down.row_chunk(c, lambda k, t: uT[:, k, t * P:(t + 1) * P], F_FF // P, turn, (2, 16))

        def u_view(turn, c, b):
            return work[:, bass.ds((turn * 2 + c) * 1024 + b * 512, 512)]

        def act_ffn(act, l):
            name = f"ffn_up{l}"
            with act.Fori(0, 8) as turn:
                for c in range(2):
                    banks, taken = chunk_banks(name, c)
                    act.wait_ge(s_used, chunk_done(name, c, turn, 4))
                    for b in range(2):
                        nc.scalar.activation(u_view(turn, c, b), banks[b][:, :], ACT.Relu).then_inc(taken, 1)

        def dve_ffn(dve, l):
            g0 = starts[f"ffn_up{l}"][0]
            with dve.Fori(0, 8) as turn:
                for c in range(2):
                    taken = s_taken[(g0 + c) % 2]
                    for b in range(2):
                        dve.wait_ge(taken, turn * 2 + ((g0 + c) // 2 * 2 + b + 1))
                        u = u_view(turn, c, b)
                        nc.vector.tensor_tensor(u, u, u, MULT).then_inc(s_u, 1)
            with dve.Fori(0, 2) as turn:
                for c in range(2):
                    dve_add_to_x(dve, f"ffn_down{l}", c, turn, (2, 16))

        def inv_views(base, nbuf=2):
            T, Tt, Pm = (W(base + 1024 * i, 2, 4, P) for i in range(3))
            MT = [W(base + 3072 + 1024 * i, 2, 4, P) for i in range(nbuf)]
            return T, Tt, Pm, MT

        def side_of(ap, level, right):
            size = 1 << level
            if len(ap.shape) == 3:
                return ap.rearrange("p m (n two s) -> p m n two s", two=2, s=size)[:, :, :, int(right)]
            return ap.rearrange("p (n two s) -> p n two s", two=2, s=size)[:, :, int(right)]

        def level_mask(d, level):
            i = C["level"].start + (d * LEVELS + level) * P
            return const[:, i:i + P].unsqueeze(1).broadcast_to([P, 4, P])

        def pool_inv_mask(pool, group, AT, views, level, d):
            MT = views[3]
            if level >= len(MT):
                pool.wait_ge(iv_p, (group * LEVELS + level - len(MT)) * 2 + d + 1)
                if level == len(MT):
                    pool.wait_ge(iv_t, group * LEVELS * 2 + d + 1)
            nc.gpsimd.tensor_tensor(MT[level % len(MT)][:, d], AT[d], level_mask(d, level), MULT).then_inc(iv_mt, 1)

        def pe_inv(pe, group, views):
            T, Tt, Pm, MT = views
            for level in range(LEVELS):
                for d in range(2):
                    n = (group * LEVELS + level) * 2 + d
                    pe.wait_ge(iv_mt, n + 1)
                    if level:
                        pe.wait_ge(iv_t, n - 2 + 1)
                    for m in range(4):
                        out = aux[d][:, m * P:(m + 1) * P]
                        if level == 0:
                            i = nc.tensor.transpose(out, MT[0][:, d, m], ident)
                        else:
                            i = nc.tensor.matmul(out, lhsT=MT[level % len(MT)][:, d, m], rhs=T[:, d, m],
                                                 start=True, stop=True)
                    i.then_inc(iv_p, 1)
                if level == 0:
                    continue
                for d in range(2):
                    pe.wait_ge(iv_ps, (group * (LEVELS - 1) + level - 1) * 2 + d + 1)
                    for m in range(4):
                        for j, (lhsT, rhs) in enumerate((
                                (Tt[:, d, m], side_of(Pm[:, d, m], level, d == 1)),
                                (Pm[:, d, m], side_of(Tt[:, d, m], level, d == 0)))):
                            if level == LEVELS - 1 and j == 0:
                                continue
                            at = (4 * j + m) * 64
                            out = aux[2 + d][:, at:at + 64].rearrange("p (n s) -> p n s", s=1 << level)
                            i = nc.tensor.matmul(out, lhsT=lhsT, rhs=rhs, start=True, stop=True)
                    i.then_inc(iv_q, 1)

        def act_inv(act, group, views):
            Pm = views[2]
            for level in range(1, LEVELS):
                for d in range(2):
                    act.wait_ge(iv_p, (group * LEVELS + level) * 2 + d + 1)
                    if level > 1:
                        act.wait_ge(iv_q, (group * (LEVELS - 1) + level - 2) * 2 + d + 1)
                    nc.scalar.activation(Pm[:, d], four(aux[d]), ACT.Copy).then_inc(iv_ps, 1)

        def dve_inv(dve, group, views):
            T, Tt, Pm, MT = views
            for level in range(LEVELS):
                for d in range(2):
                    if level == 0:
                        dve.wait_ge(iv_p, group * LEVELS * 2 + d + 1)
                        eye = ident.unsqueeze(1).broadcast_to([P, 4, P])
                        nc.vector.tensor_tensor(Tt[:, d], eye, MT[0][:, d], SUB)
                        i = nc.vector.tensor_tensor(T[:, d], eye, four(aux[d]), SUB)
                    else:
                        dve.wait_ge(iv_q, (group * (LEVELS - 1) + level - 1) * 2 + d + 1)
                        for j, (dst, right) in enumerate(((T, d == 1), (Tt, d == 0))):
                            if level == LEVELS - 1 and j == 0:
                                continue
                            v = side_of(dst[:, d], level, right)
                            got = aux[2 + d][:, j * 256:(j + 1) * 256].rearrange(
                                "p (m n s) -> p m n s", m=4, s=1 << level)
                            i = nc.vector.tensor_tensor(v, v, got, SUB)
                    i.then_inc(iv_t, 1)

        dn_qT, dn_kT = W(0, DN_H, S), W(2048, DN_H, S)
        dn_k, dn_v = W(4096, NT, DN_W), W(6144, NT, DN_W)
        gate = W(8192, NT, DN_W)
        yscT = W(10240, 8, S)
        G = 12288
        stage = [W(G + 1032 * i, 4, S + 2) for i in range(2)]
        conv = [W(G + 2064 + 1024 * i, 4, S) for i in range(2)]
        dn_vT = W(G + 4112, DN_H, S)
        cgate = W(G + 6160, 4, S)
        dn_AT = W(G, 2, 4, P)
        dn_inv = inv_views(G + 1024)
        QKT = W(G + 6144, 2, 4, P)
        qTg, eg = W(G + 7168, 2, 2, P), W(G + 7680, 2, 2, P)
        Dm, DB = W(G + 8192, 2, 4, P), W(G + 9216, 2, 4, P)
        vb1, vb2 = W(G + 8192, 2, 2, P), W(G + 8704, 2, 2, P)
        kd1, vn1 = W(G + 9216, 2, 2, P), W(G + 9728, 2, 2, P)
        S1 = W(G + 10240, 2, 2, P)
        vn2 = W(G + 3072, 2, 2, P)
        o_tok = hT[:, 8:16, :].rearrange("p k s -> p (k s)").rearrange("p (t h e) -> p t h e", t=NT, e=P)
        o_sq = W(G, NT, DN_H, P)
        y_tok = W(G + 2048, NT, DN_H, P)

        def stat(at, n=32):
            return st[:, 128 + at:128 + at + n].rearrange("p (t n) -> p t n", t=NT)

        abv, beta, xb, ax, soft, decay_g = stat(0, 64), stat(64), stat(96), stat(128), stat(160), stat(192)
        ea = st[:, 128 + 224:128 + 240]
        cum, ecum = stat(240, 64), stat(304, 64)
        dn_ms, dn_sd, dn_rn = stat(368), stat(400), stat(432)
        rq = stat(464, 16)
        brk, nbe, kds = stat(480), stat(512), stat(544)
        o_ss, o_ms, o_sd, o_r = (st[:, 128 + 576 + 16 * i:128 + 592 + 16 * i] for i in range(4))
        FIRST = (0, 1)
        N_SC = 6

        def conv_w(name, tile, tap):
            i = Q[name].start + 3 * tile + tap
            return par[:, i:i + 1]

        def per_dir(v, t, d, hp):
            return v[:, t, 8 * d + 2 * hp:8 * d + 2 * hp + 2]

        def pe_even(pe):
            pe_hT(pe, "mix0")
            for t in range(NT):
                for k in range(KD):
                    i = Q["ab_w"].start + 32 * k
                    m = nc.tensor.matmul(aux[0][:, 32 * t:32 * t + 32], lhsT=hT_tile(k, t), rhs=par[:, i:i + 32],
                                         start=k == 0, stop=k == KD - 1)
            m.then_inc(s_ab, 1)
            with pe.Fori(0, 3) as turn:
                for c in range(2):
                    Gemm(pe, "ev_qkv").column_chunk(c, turn, (2, 4))
            for c in range(2):
                Gemm(pe, "ev_gate").row_chunk(c, hT_tile)
            for c in range(N_SC):
                Gemm(pe, "ev_sc").column_chunk(c)
            pe.wait_ge(s_silu, 6)
            wait_chunks_taken(pe, after("ev_sc"))
            pe.wait_ge(s_abv, 1)
            for b in range(8):
                for t in range(NT):
                    for i in range(2):
                        src = (dn_kT, dn_vT)[b // 4][:, 2 * (b % 4) + i, t * P:(t + 1) * P]
                        m = nc.tensor.transpose(bank[b][:, (2 * t + i) * P:(2 * t + i + 1) * P], src, ident)
                m.then_inc(s_kvt, 1)
            pe.wait_ge(s_g, 1)
            pe.wait_ge(s_kv_a, 2)
            for t in range(NT):
                for kind, masks_ in enumerate(((1, 3), (2, 0))):
                    for d in range(2):
                        at = t * 32 + kind * 16 + 8 * d
                        m = nc.tensor.matmul(bank[1][:, at:at + 8], lhsT=const_of("causal", masks_[d]),
                                             rhs=decay_g[:, t, 8 * d:8 * d + 8], start=True, stop=True)
            m.then_inc(s_cum, 1)
            pe.wait_ge(s_dsq, 2)
            for t in range(NT):
                for h in range(2 * DN_H):
                    m = nc.tensor.matmul(bank[0][:, 16 * t + h:16 * t + h + 1], lhsT=hT[:, h, t * P:(t + 1) * P],
                                         rhs=ones_col, start=True, stop=True)
            m.then_inc(s_dss, 1)
            pe.wait_ge(s_stats, 1)
            pe.wait_ge(s_kv_a, 4)
            pe.wait_ge(s_kv_d, 4)
            for hp in range(4):
                pe_delta_group(pe, hp)
            pe.wait_ge(s_y, 1)
            for b in range(4):
                for i in range(2):
                    for t in range(NT):
                        m = nc.tensor.transpose(aux[b][:, (2 * i + t) * P:(2 * i + t + 1) * P],
                                                y_tok[:, t, 2 * b + i, :], ident)
                m.then_inc(s_yt, 1)
            pe.wait_ge(s_yT, 4)
            out = Gemm(pe, "ev_out")
            for c in range(4):
                out.row_chunk(c, lambda k, t: hT_tile(k, t) if k < 8 else yscT[:, k - 8, t * P:(t + 1) * P])

        def pe_delta_group(pe, hp):
            T, Tt, Pm, MT = dn_inv
            if hp:
                pe.wait_ge(s_os, hp)
            for d in range(2):
                b = bank[4 * d:4 * d + 4]
                for i in range(2):
                    for t in range(NT):
                        h, cols = 2 * hp + i, slice((2 * i + t) * P, (2 * i + t + 1) * P)
                        tile = slice(t * P, (t + 1) * P)
                        g_col = decay_g[:, t, 8 * d + h:8 * d + h + 1].broadcast_to([P, P])
                        b_col = brk[:, t, 8 * d + h:8 * d + h + 1].broadcast_to([P, P])
                        for bk, lhsT, rhs in ((b[0], g_col, const_of("causal", 2 * d + 1)), (b[1], b_col, ident),
                                              (b[2], dn_kT[:, h, tile], dn_kT[:, h, tile]),
                                              (b[3], dn_kT[:, h, tile], dn_qT[:, h, tile])):
                            m = nc.tensor.matmul(bk[:, cols], lhsT=lhsT, rhs=rhs, start=True, stop=True)
                m.then_inc(s_pre, 1)
            pe.wait_ge(s_eg, 2 * hp + 2)
            pe.wait_ge(s_AT, 2 * hp + 2)
            pe_inv(pe, hp, dn_inv)
            pe.wait_ge(s_vb, hp + 1)
            pe.wait_ge(iv_t, (hp + 1) * LEVELS * 2)
            for d in range(2):
                for i in range(2):
                    m = nc.tensor.matmul(bank[0][:, (2 * d + i) * P:(2 * d + i + 1) * P],
                                         lhsT=Tt[:, d, 2 * i + FIRST[d]], rhs=vb1[:, d, i], start=True, stop=True)
            m.then_inc(s_vn1, 1)
            pe.wait_ge(s_vn1s, hp + 1)
            for d in range(2):
                for i in range(2):
                    m = nc.tensor.matmul(bank[1][:, (2 * d + i) * P:(2 * d + i + 1) * P],
                                         lhsT=kd1[:, d, i], rhs=vn1[:, d, i], start=True, stop=True)
            m.then_inc(s_S, 1)
            pe.wait_ge(s_Ss, hp + 1)
            for d in range(2):
                t2 = 1 - FIRST[d]
                for i in range(2):
                    m = nc.tensor.matmul(bank[2][:, (2 * d + i) * P:(2 * d + i + 1) * P],
                                         lhsT=dn_kT[:, 2 * hp + i, t2 * P:(t2 + 1) * P], rhs=S1[:, d, i],
                                         start=True, stop=True)
            m.then_inc(s_kS, 1)
            pe.wait_ge(s_R, hp + 1)
            for d in range(2):
                for i in range(2):
                    m = nc.tensor.matmul(bank[3][:, (2 * d + i) * P:(2 * d + i + 1) * P],
                                         lhsT=Tt[:, d, 2 * i + 1 - FIRST[d]], rhs=vb2[:, d, i], start=True, stop=True)
            m.then_inc(s_vn2, 1)
            pe.wait_ge(s_vn2s, hp + 1)
            pe.wait_ge(s_qtg, 2 * hp + 2)
            for t in range(NT):
                d1, d2 = (0, 1) if t == 0 else (1, 0)
                for i in range(2):
                    out = bank[0][:, (2 * t + i) * P:(2 * t + i + 1) * P]
                    nc.tensor.matmul(out, lhsT=QKT[:, d1, 2 * i + t], rhs=vn1[:, d1, i], start=True, stop=False)
                    nc.tensor.matmul(out, lhsT=QKT[:, d2, 2 * i + t], rhs=vn2[:, d2, i], start=False, stop=False)
                    m = nc.tensor.matmul(out, lhsT=qTg[:, d2, i], rhs=S1[:, d2, i], start=False, stop=True)
            m.then_inc(s_o, 1)

        def act_even(act):
            act.wait_ge(s_abv, 1)
            nc.scalar.activation(beta, abv[:, :, 0:16], ACT.Sigmoid)
            act.wait_ge(s_ax, 1)
            act_step(nc.scalar.activation(soft, ax, ACT.Exp, scale=-1.0))
            nc.scalar.activation(ea, par[:, Q["a_log"]], ACT.Exp)
            nc.scalar.activation(soft, soft, ACT.Ln, bias=1.0).then_inc(s_sp, 1)

            def silu(c):
                act.wait_ge(s_cv, c + 1)
                dst = (dn_qT, dn_kT, dn_vT)[c // 2][:, 4 * (c % 2):4 * (c % 2) + 4, :]
                nc.scalar.activation(dst, conv[c % 2], ACT.Silu).then_inc(s_silu, 1)

            for c in range(6):
                banks, taken = chunk_banks("ev_qkv", c)
                act.wait_ge(s_used, chunk_done("ev_qkv", c))
                if c >= 2:
                    act.wait_ge(s_cv, c - 1)
                for b in range(2):
                    nc.scalar.activation(stage[c % 2][:, 2 * b:2 * b + 2, 1:S + 1],
                                         banks[b][:, :].rearrange("p (h s) -> p h s", s=S), ACT.Copy).then_inc(taken, 1)
                if c:
                    silu(c - 1)
            silu(5)
            for c in range(2):
                banks, taken = chunk_banks("ev_gate", c)
                act.wait_ge(s_used, chunk_done("ev_gate", c))
                for t in range(NT):
                    nc.scalar.activation(gate[:, t, c * 512:(c + 1) * 512], banks[t][:, :], ACT.Silu).then_inc(taken, 1)
            for half in range(2):
                c = 3 * half
                banks, taken = chunk_banks("ev_sc", c)
                act.wait_ge(s_used, chunk_done("ev_sc", c))
                if half:
                    wait_chunks_taken(act, starts["ev_sc"][0] + 2)
                for b in range(2):
                    nc.scalar.activation(cgate[:, 2 * b:2 * b + 2, :], banks[b][:, :].rearrange("p (h s) -> p h s", s=S),
                                         ACT.Copy).then_inc(taken, 1)
            act.wait_ge(s_used, chunk_done("ev_sc", 5))
            nc.scalar.activation(hT[:, 0:8, :], dn_qT, ACT.Square).then_inc(s_dsq, 1)
            nc.scalar.activation(hT[:, 8:16, :], dn_kT, ACT.Square).then_inc(s_dsq, 1)
            for b in range(4):
                act.wait_ge(s_kvt, b + 1)
                dst = dn_k.rearrange("p t (h e) -> p t h e", e=P)[:, :, 2 * b:2 * b + 2, :]
                nc.scalar.activation(dst, bank[b][:, :].rearrange("p (t h e) -> p t h e", t=NT, e=P),
                                     ACT.Copy).then_inc(s_kv_a, 1)
            act.wait_ge(s_cumv, 1)
            nc.scalar.activation(ecum, cum, ACT.Exp).then_inc(s_dE, 1)
            act.wait_ge(s_dms, 1)
            nc.scalar.activation(dn_sd, dn_ms, ACT.Sqrt).then_inc(s_dsd, 1)
            for hp in range(4):
                for d in range(2):
                    act.wait_ge(s_diff, 2 * hp + d + 1)
                    nc.scalar.activation(Dm[:, d], Dm[:, d], ACT.Exp).then_inc(s_D, 1)
                    if hp:
                        act.wait_ge(s_qtg, 2 * hp)
                    src = bank[4 * d][:, :].rearrange("p (i t s) -> p i t s", t=NT, s=P)[:, :, 1 - FIRST[d], :]
                    nc.scalar.activation(eg[:, d], src, ACT.Exp).then_inc(s_eg, 1)
                act_inv(act, hp, dn_inv)
                for n, (ready, src, dst, done) in enumerate(((s_vn1, 0, vn1, s_vn1s), (s_S, 1, S1, s_Ss), (s_vn2, 3, vn2, s_vn2s))):
                    act.wait_ge(ready, hp + 1)
                    nc.scalar.activation(dst.rearrange("p d i e -> p (d i) e"), four(bank[src]), ACT.Copy).then_inc(done, 1)
            act.wait_ge(s_oms, 1)
            nc.scalar.activation(o_sd, o_ms, ACT.Sqrt).then_inc(s_osd, 1)
            for b in range(0, 4, 2):
                act.wait_ge(s_yt, b + 1)
                nc.scalar.activation(hT[:, 2 * b:2 * b + 2, :], aux[b][:, :].rearrange("p (h s) -> p h s", s=S),
                                     ACT.Copy).then_inc(s_yT, 1)

        def dve_conv(dve, src, dst, name, tile0, done):
            for i in range(4):
                m = nc.vector.tensor_scalar(dst[:, i], src[:, i, 1:S + 1], conv_w(name, tile0 + i, 1), None, MULT)
            dve_step(m)
            for tap, at in ((0, 0), (2, 2)):
                for i in range(4):
                    m = nc.vector.scalar_tensor_tensor(out=dst[:, i], in0=src[:, i, at:at + S],
                                                       scalar=conv_w(name, tile0 + i, tap), in1=dst[:, i],
                                                       op0=MULT, op1=ADD)
                if tap == 0:
                    dve_step(m)
            if done is None:
                dve_step(m)
            else:
                m.then_inc(done, 1)

        def dve_even(dve):
            for s_ in stage:
                nc.vector.memset(s_[:, :, 0:1], 0.0)
                m = nc.vector.memset(s_[:, :, S + 1:S + 2], 0.0)
            dve_step(m)
            dve.wait_ge(s_ab, 1)
            nc.vector.tensor_copy(abv, aux[0][:, 0:64].rearrange("p (t n) -> p t n", t=NT)).then_inc(s_abv, 1)
            dve.wait_ge(s_abv, 1)
            dt = par[:, Q["dt_bias"]].unsqueeze(1).broadcast_to([P, NT, 16])
            dve_step(nc.vector.tensor_tensor(xb, abv[:, :, 16:32], dt, ADD))
            nc.vector.scalar_tensor_tensor(out=ax, in0=xb, scalar=-1.0, in1=xb, op0=MULT, op1=MAX).then_inc(s_ax, 1)
            dve.wait_ge(s_sp, 1)
            dve_step(nc.vector.scalar_tensor_tensor(out=xb, in0=xb, scalar=0.0, in1=soft, op0=MAX, op1=ADD))
            nc.vector.scalar_tensor_tensor(out=decay_g, in0=xb, scalar=-1.0, in1=ea.unsqueeze(1).broadcast_to([P, NT, 16]),
                                           op0=MULT, op1=MULT).then_inc(s_g, 1)
            for c in range(6):
                _, taken = chunk_banks("ev_qkv", c)
                dve.wait_ge(taken, 2 * ((starts["ev_qkv"][0] + c) // 2 + 1))
                if c >= 2:
                    dve.wait_ge(s_silu, c - 1)
                dve_conv(dve, stage[c % 2], conv[c % 2], "dn_conv", 4 * c, s_cv)
            wait_chunks_taken(dve, after("ev_gate"))
            gain = par[:, Q["dn_norm"]].unsqueeze(1).broadcast_to([P, NT * DN_H, P])
            gv = gate.rearrange("p t (h e) -> p (t h) e", e=P)
            nc.vector.tensor_tensor(gv, gv, gain, MULT)
            dve.wait_ge(s_silu, 6)
            for half in range(2):
                c = 3 * half + 1
                banks, taken = chunk_banks("ev_sc", c)
                wait_chunks_taken(dve, starts["ev_sc"][0] + c)
                dve.wait_ge(s_used, chunk_done("ev_sc", c))
                for b in range(2):
                    nc.vector.tensor_tensor(stage[0][:, 2 * b:2 * b + 2, 1:S + 1], cgate[:, 2 * b:2 * b + 2, :],
                                            banks[b][:, :].rearrange("p (h s) -> p h s", s=S), MULT).then_inc(taken, 1)
                dve.wait_ge(taken, 2 * ((starts["ev_sc"][0] + c) // 2 + 1))
                dve_conv(dve, stage[0], conv[0], "sc_conv", 4 * half, None)
                banks, taken = chunk_banks("ev_sc", c + 1)
                dve.wait_ge(s_used, chunk_done("ev_sc", c + 1))
                for b in range(2):
                    nc.vector.tensor_tensor(yscT[:, 4 * half + 2 * b:4 * half + 2 * b + 2, :],
                                            conv[0][:, 2 * b:2 * b + 2, :],
                                            banks[b][:, :].rearrange("p (h s) -> p h s", s=S), MULT).then_inc(taken, 1)
            for b in range(4):
                dve.wait_ge(s_kvt, 4 + b + 1)
                dst = dn_v.rearrange("p t (h e) -> p t h e", e=P)[:, :, 2 * b:2 * b + 2, :]
                nc.vector.tensor_copy(dst, bank[4 + b][:, :].rearrange("p (t h e) -> p t h e", t=NT, e=P)).then_inc(s_kv_d, 1)
            dve.wait_ge(s_cum, 1)
            nc.vector.tensor_copy(cum, bank[1][:, 0:64].rearrange("p (t n) -> p t n", t=NT)).then_inc(s_cumv, 1)
            dve.wait_ge(s_dss, 1)
            nc.vector.tensor_scalar(dn_ms, bank[0][:, 0:32].rearrange("p (t n) -> p t n", t=NT), 1e-6, None, ADD).then_inc(s_dms, 1)
            dve.wait_ge(s_dsd, 1)
            dve_step(nc.vector.reciprocal(dn_rn, dn_sd))
            nc.vector.tensor_scalar(rq, dn_rn[:, :, 0:8], HEAD_SCALE, None, MULT)
            rk2 = dn_rn[:, :, 8:16].unsqueeze(2).broadcast_to([P, NT, 2, 8])
            two = lambda v: v.rearrange("p t (d h) -> p t d h", d=2)
            dve_step(nc.vector.tensor_tensor(two(brk), two(beta), rk2, MULT))
            dve.wait_ge(s_dE, 1)
            nc.vector.scalar_tensor_tensor(out=nbe, in0=brk, scalar=-1.0, in1=ecum[:, :, 0:16], op0=MULT, op1=MULT)
            nc.vector.tensor_tensor(two(kds), two(ecum[:, :, 16:32]), rk2, MULT).then_inc(s_stats, 1)
            dve.wait_ge(s_stats, 1)
            for hp in range(4):
                dve_delta_group(dve, hp)
            dve.wait_ge(s_os, 4)
            dve_step(nc.vector.tensor_tensor(o_sq, o_tok, o_tok, MULT))
            dve_step(nc.vector.reduce_sum(o_ss, o_sq.rearrange("p t h e -> p (t h) e"), AX_X))
            nc.vector.tensor_scalar(o_ms, o_ss, 1.0 / P, RMS_EPS, MULT, ADD).then_inc(s_oms, 1)
            dve.wait_ge(s_osd, 1)
            dve_step(nc.vector.reciprocal(o_r, o_sd))
            flat = lambda v: v.rearrange("p t h e -> p (t h) e")
            dve_step(nc.vector.tensor_tensor(flat(y_tok), flat(o_tok), lanes(o_r, P), MULT))
            nc.vector.tensor_tensor(flat(y_tok), flat(y_tok), gv, MULT).then_inc(s_y, 1)
            for b in range(1, 4, 2):
                dve.wait_ge(s_yt, b + 1)
                nc.vector.tensor_copy(hT[:, 2 * b:2 * b + 2, :], aux[b][:, :].rearrange("p (h s) -> p h s", s=S)).then_inc(s_yT, 1)
            for c in range(4):
                dve_add_to_x(dve, "ev_out", c)

        def dve_delta_group(dve, hp):
            if hp:
                dve.wait_ge(s_o, hp)
            for d in range(2):
                b = bank[4 * d:4 * d + 4]
                dve.wait_ge(s_pre, 2 * hp + d + 1)
                each = [(2 * i + t, t, 8 * d + 2 * hp + i, 8 + 2 * hp + i) for i in range(2) for t in range(NT)]
                for m, t, j, _ in each:
                    i_ = nc.vector.scalar_tensor_tensor(out=Dm[:, d, m], in0=b[0][:, m * P:(m + 1) * P],
                                                        scalar=cum[:, t, j:j + 1], in1=const_of("neg", d), op0=SUB, op1=ADD)
                i_.then_inc(s_diff, 1)
                dve.wait_ge(s_D, 2 * hp + d + 1)
                dve_step(nc.vector.tensor_tensor(DB[:, d], Dm[:, d], four(b[1]), MULT))
                for m, t, _, kh in each:
                    nc.vector.scalar_tensor_tensor(out=QKT[:, d, m], in0=b[3][:, m * P:(m + 1) * P],
                                                   scalar=dn_rn[:, t, kh:kh + 1], in1=Dm[:, d, m], op0=MULT, op1=MULT)
                for m, t, _, kh in each:
                    i_ = nc.vector.scalar_tensor_tensor(out=dn_AT[:, d, m], in0=b[2][:, m * P:(m + 1) * P],
                                                        scalar=dn_rn[:, t, kh:kh + 1], in1=DB[:, d, m], op0=MULT, op1=MULT)
                i_.then_inc(s_AT, 1)
            dve_inv(dve, hp, dn_inv)
            dve.wait_ge(s_kS, hp + 1)
            dve.wait_ge(s_vb, hp + 1)
            for d in range(2):
                for i in range(2):
                    j = 8 * d + 2 * hp + i
                    m = nc.vector.scalar_tensor_tensor(out=vb2[:, d, i], in0=bank[2][:, (2 * d + i) * P:(2 * d + i + 1) * P],
                                                       scalar=nbe[:, 1 - FIRST[d], j:j + 1], in1=vb2[:, d, i],
                                                       op0=MULT, op1=ADD)
            m.then_inc(s_R, 1)
            dve.wait_ge(s_o, hp + 1)
            for t in range(NT):
                m = nc.vector.tensor_tensor(o_tok[:, t, 2 * hp:2 * hp + 2, :],
                                            bank[0][:, t * 256:(t + 1) * 256].rearrange("p (i e) -> p i e", e=P),
                                            lanes(rq[:, t, 2 * hp:2 * hp + 2], P), MULT)
            m.then_inc(s_os, 1)

        def pool_even(pool):
            views = dn_inv
            pool.wait_ge(s_stats, 1)
            for hp in range(4):
                for d in range(2):
                    pool.wait_ge(s_AT, 2 * hp + d + 1)
                    pool_inv_mask(pool, hp, [dn_AT[:, 0], dn_AT[:, 1]], views, 0, d)
                for d in range(2):
                    pool_inv_mask(pool, hp, [dn_AT[:, 0], dn_AT[:, 1]], views, 1, d)
                for d in range(2):
                    t1, t2 = FIRST[d], 1 - FIRST[d]
                    pool.wait_ge(s_eg, 2 * hp + d + 1)
                    nc.gpsimd.tensor_tensor(qTg[:, d], dn_qT[:, 2 * hp:2 * hp + 2, t2 * P:(t2 + 1) * P], eg[:, d],
                                            MULT).then_inc(s_qtg, 1)
                    for dst, src, t, w in ((vb1, dn_v, t1, beta), (vb2, dn_v, t2, beta), (kd1, dn_k, t1, kds)):
                        v = src[:, t, 2 * hp * P:(2 * hp + 2) * P].rearrange("p (i e) -> p i e", e=P)
                        m = nc.gpsimd.tensor_tensor(dst[:, d], v, lanes(per_dir(w, t, d, hp), P), MULT)
                m.then_inc(s_vb, 1)
                for level in range(2, LEVELS):
                    for d in range(2):
                        pool_inv_mask(pool, hp, [dn_AT[:, 0], dn_AT[:, 1]], views, level, d)

        NB = N_BUCKETS + 1
        btab = W(2048, DSA_G, 512)[0:NB]
        rel = st[0:NB, 112:112 + DSA_H]
        brow = W(16384, DSA_H, 512)

        def pe_bias(pe):
            pe.wait_ge(s_bt_in, 32)
            pe.wait_ge(s_neg, 1)
            for h in range(DSA_H):
                if h >= 4:
                    pe.wait_ge(s_bias_s, h - 3)
                nc.tensor.matmul(aux[h % 4][:, :], lhsT=rel[:, h:h + 1].broadcast_to([NB, P]),
                                 rhs=btab[:, h // DSA_HG, :], start=True, stop=True).then_inc(s_bias_m, 1)

        def act_bias(act):
            act.dma_start(rel[0:N_BUCKETS], rel_bias).then_inc(s_bt_in, 16)
            act.dma_start(btab, bias_table.rearrange("b (g n) -> b g n", g=DSA_G)).then_inc(s_bt_in, 16)
            for h in range(DSA_H):
                act.wait_ge(s_bias_m, h + 1)
                nc.scalar.activation(brow[:, h, :], aux[h % 4][:, :], ACT.Copy).then_inc(s_bias_s, 1)
            act.wait_ge(s_bias_s, DSA_H)
            act.dma_start(bias_rows.rearrange("h p n -> p h n"), brow).then_inc(s_bias_out, 16)

        oq, ok, ov, okT = W(0, DSA_H, S), W(3072, NT, DSA_H * P), W(6144, NT, DSA_H * P), W(9216, DSA_H, S)
        bias = W(12288, NT, DSA_H, S)
        osc = W(18432, 2, DSA_G, S)
        oq_sq = W(19968, 2, 4, S)
        ok_sq = W(18432, NT, 512)
        oPT = W(3072, 2, 6, P)
        ycT = mem_kT[0]
        o_sum = lambda i: st[:, 124 + i:125 + i]
        ost = lambda i: st[:, 128 + 24 * i:152 + 24 * i]
        oms, osd, orq0, orq, kss, kms, ksd, krs = (ost(i) for i in range(8))
        omx, onm, osum, ors = (st[:, 320 + 2 * i:322 + 2 * i] for i in range(4))
        gca = st[:, 328:329]
        ITEMS = [(hg, t) for hg in range(DSA_HG) for t in range(NT)]

        def taken_of(eng, name, c):
            g = starts[name][0] + c
            eng.wait_ge(s_taken[g % 2], 2 * (g // 2 + 1))

        def pe_window(pe):
            pe_hT(pe, "mix1")
            q, k, v = (Gemm(pe, n) for n in ("od_q", "od_k", "od_v"))

            def ssq(c):
                taken_of(pe, "od_q", c)
                for t in range(NT):
                    for i in range(4):
                        at = t * DSA_H + 4 * c + i
                        m = nc.tensor.matmul(aux[0][:, at:at + 1], lhsT=oq_sq[:, c % 2, i, t * P:(t + 1) * P],
                                             rhs=ones_col, start=True, stop=True)
                m.then_inc(s_oss, 1)

            q.column_chunk(0)
            q.column_chunk(1)
            ssq(0)
            q.column_chunk(2)
            ssq(1)
            k.row_chunk(0, hT_tile)
            ssq(2)
            k.row_chunk(1, hT_tile)
            k.row_chunk(2, hT_tile)
            for c in range(3):
                v.row_chunk(c, hT_tile)
            pe.wait_ge(s_ok, 1)
            pe.wait_ge(s_oms0, 1)
            for b in range(6):
                if b >= 4:
                    pe.wait_ge((s_okT_a, s_okT_d)[b % 2], (b - 4) // 2 + 1)
                for i in range(2):
                    for t in range(NT):
                        h = 2 * b + i
                        m = nc.tensor.transpose(aux[b % 4][:, (2 * i + t) * P:(2 * i + t + 1) * P],
                                                ok[:, t, h * P:(h + 1) * P], ident)
                m.then_inc(s_okt, 1)
            pe.wait_ge(s_okT_a, 3)
            pe.wait_ge(s_okT_d, 3)
            wait_chunks_taken(pe, after("od_v"))

            def scores(n):
                hg, t = ITEMS[n]
                p = n % 2
                if n >= 2:
                    pe.wait_ge(s_opt_a, n - 1)
                    pe.wait_ge(s_opt_d, n - 1)
                for g in range(DSA_G):
                    h = g * DSA_HG + hg
                    m = nc.tensor.matmul(aux[2 * p + g // 2][:, (g % 2) * S:(g % 2 + 1) * S],
                                         lhsT=oq[:, h, t * P:(t + 1) * P], rhs=okT[:, h, :], start=True, stop=True)
                m.then_inc(s_ol, 1)

            scores(0)
            for n, (hg, t) in enumerate(ITEMS):
                p = n % 2
                if n + 1 < len(ITEMS):
                    scores(n + 1)
                pe.wait_ge(s_op, n + 1)
                for g in range(DSA_G):
                    for mt in range(NT):
                        j = 2 * g + mt
                        m = nc.tensor.transpose(aux[2 * p + j // 4][:, (j % 4) * P:(j % 4 + 1) * P],
                                                osc[:, p, g, mt * P:(mt + 1) * P], ident)
                m.then_inc(s_opt, 1)
                pe.wait_ge(s_opt_a, n + 1)
                pe.wait_ge(s_opt_d, n + 1)
                if n >= 2:
                    pe.wait_ge(s_oyc, n - 1)
                for g in range(DSA_G):
                    for mt in range(NT):
                        h = g * DSA_HG + hg
                        m = nc.tensor.matmul(bank[p][:, 0:P], lhsT=ov[:, mt, h * P:(h + 1) * P],
                                             rhs=oPT[:, p, 2 * g + mt, :], start=g + mt == 0, stop=g + mt == 3)
                m.then_inc(s_opv, 1)

        def act_window(act):
            act.wait_ge(s_used, chunk_done("ffn_down0", 3))
            act.wait_ge(s_bias_out, 16)
            for t in range(NT):
                src = bass.AP(bias_rows.tensor, S - 1 - P * t, [[511, P], [P * 512, DSA_H], [1, S]])
                act.dma_start(bias[:, t], src).then_inc(s_bias_in, 16)
            act.wait_ge(s_gca, 1)
            for c in range(3):
                banks, taken = chunk_banks("od_q", c)
                act.wait_ge(s_used, chunk_done("od_q", c))
                if c == 2:
                    act.wait_ge(s_oss, 1)
                for b in range(2):
                    v = banks[b][:, :].rearrange("p (h s) -> p h s", s=S)
                    nc.scalar.activation(oq_sq[:, c % 2, 2 * b:2 * b + 2, :], v, ACT.Square)
                    nc.scalar.activation(oq[:, 4 * c + 2 * b:4 * c + 2 * b + 2, :], v, ACT.Copy, scale=gca).then_inc(taken, 1)
            for name, dst in (("od_k", ok), ("od_v", ov)):
                for c in range(3):
                    take_row_chunk(act, name, c, lambda t: dst[:, t, c * 512:(c + 1) * 512])
                    if name == "od_k" and c == 2:
                        act.wait_ge(s_oms0, 1)
                        nc.scalar.activation(osd, oms, ACT.Sqrt).then_inc(s_osd0, 1)
                        act.wait_ge(s_kms, 1)
                        nc.scalar.activation(ksd, kms, ACT.Sqrt).then_inc(s_ksd, 1)
            for b in range(0, 6, 2):
                act.wait_ge(s_okt, b + 1)
                nc.scalar.activation(okT[:, 2 * b:2 * b + 2, :], aux[b % 4][:, :].rearrange("p (h s) -> p h s", s=S),
                                     ACT.Copy).then_inc(s_okT_a, 1)
            def exps(n):
                p = n % 2
                act.wait_ge(s_onm, n + 1)
                v = osc[:, p].rearrange("p g m -> p (g m)")
                nc.scalar.activation(v, v, ACT.Exp, bias=onm[:, p:p + 1], accum_out=osum[:, p:p + 1]).then_inc(s_oexp, 1)

            exps(0)
            for n, (hg, t) in enumerate(ITEMS):
                p = n % 2
                if n + 1 < len(ITEMS):
                    exps(n + 1)
                act.wait_ge(s_opt, n + 1)
                nc.scalar.activation(oPT[:, p, 0:4, :], four(aux[2 * p]), ACT.Copy).then_inc(s_opt_a, 1)
                act.wait_ge(s_opv, n + 1)
                nc.scalar.activation(ycT[:, hg, t * P:(t + 1) * P], bank[p][:, 0:P], ACT.Copy).then_inc(s_oyc, 1)

        def dve_window(dve):
            nc.vector.tensor_tensor(gca, par[:, Q["ca_qn"]], par[:, Q["ca_kn"]], MULT).then_inc(s_gca, 1)
            for c in range(3):
                taken_of(dve, "od_k", c)
                dve_step(nc.vector.tensor_tensor(ok_sq, ok[:, :, c * 512:(c + 1) * 512], ok[:, :, c * 512:(c + 1) * 512], MULT))
                for t in range(NT):
                    m = nc.vector.reduce_sum(kss[:, t * DSA_H + 4 * c:t * DSA_H + 4 * c + 4],
                                             ok_sq[:, t, :].rearrange("p (h e) -> p h e", e=P), AX_X)
                dve_step(m)
            dve.wait_ge(s_oss, 3)
            nc.vector.tensor_scalar(oms, aux[0][:, 0:24], 1.0 / P, RMS_EPS, MULT, ADD).then_inc(s_oms0, 1)
            nc.vector.tensor_scalar(kms, kss, 1.0 / P, RMS_EPS, MULT, ADD).then_inc(s_kms, 1)
            dve.wait_ge(s_osd0, 1)
            dve_step(nc.vector.reciprocal(orq0, osd))
            nc.vector.tensor_scalar(orq, orq0, HEAD_SCALE, None, MULT).then_inc(s_orq, 1)
            dve.wait_ge(s_ksd, 1)
            dve_step(nc.vector.reciprocal(krs, ksd))
            kv = ok.rearrange("p t (h e) -> p (t h) e", e=P)
            nc.vector.tensor_tensor(kv, kv, lanes(krs, P), MULT).then_inc(s_ok, 1)
            for b in range(1, 6, 2):
                dve.wait_ge(s_okt, b + 1)
                nc.vector.tensor_copy(okT[:, 2 * b:2 * b + 2, :], aux[b % 4][:, :].rearrange("p (h s) -> p h s", s=S)).then_inc(s_okT_d, 1)
            dve.wait_ge(s_bias_in, 32)
            dve.wait_ge(s_orq, 1)

            def scores(n):
                hg, t = ITEMS[n]
                p = n % 2
                dve.wait_ge(s_ol, n + 1)
                if n >= 2:
                    dve.wait_ge(s_opt, n - 1)
                for g in range(DSA_G):
                    h = g * DSA_HG + hg
                    m = nc.vector.scalar_tensor_tensor(out=osc[:, p, g, :], in0=aux[2 * p + g // 2][:, (g % 2) * S:(g % 2 + 1) * S],
                                                       scalar=orq[:, t * DSA_H + h:t * DSA_H + h + 1], in1=bias[:, t, h, :],
                                                       op0=MULT, op1=ADD)
                dve_step(m)
                dve_step(nc.vector.reduce_max(omx[:, p:p + 1], osc[:, p].rearrange("p g m -> p (g m)"), AX_X))
                nc.vector.tensor_scalar(onm[:, p:p + 1], omx[:, p:p + 1], -1.0, None, MULT).then_inc(s_onm, 1)

            scores(0)
            for n, (hg, t) in enumerate(ITEMS):
                p = n % 2
                if n + 1 < len(ITEMS):
                    scores(n + 1)
                dve.wait_ge(s_oexp, n + 1)
                dve_step(nc.vector.reciprocal(ors[:, p:p + 1], osum[:, p:p + 1]))
                v = osc[:, p].rearrange("p g m -> p (g m)")
                nc.vector.tensor_scalar(v, v, ors[:, p:p + 1], None, MULT).then_inc(s_op, 1)
                dve.wait_ge(s_opt, n + 1)
                nc.vector.tensor_copy(oPT[:, p, 4:6, :], aux[2 * p + 1][:, 0:256].rearrange("p (m s) -> p m s", s=P)).then_inc(s_opt_d, 1)

        R = 12288
        rT, krT, kkT, rv = W(0, RW_F, S), W(1024, RW_F, S), W(2048, RW_F, S), W(3072, NT, RW_W)
        lw, gout = W(4096, NT, 2, RW_W), W(6144, NT, RW_W)
        kdT, aT = W(7168, 2, RW_F, S), W(9216, 2, RW_F, S)
        ln_wb = W(11264, 2, RW_W)
        rstage = [W(R + 1032 * i, 4, S + 2) for i in range(2)]
        vrT, wagT = W(R + 2064, RW_F, S), W(R + 3088, 3, S)
        wide_w = W(R + 3856, 2560)
        w2, a2, g2, w0 = (wide_w[:, WD[n]] for n in ("w2", "a2", "g2", "w0"))
        rtmp = W(R + 6416, RW_F, S)
        rpr = W(R + 7440, RW_F, S)
        rtmp2 = W(R + 8464, RW_F, S)
        MAT = W(R, 2, 4, 4, P)
        rw_inv = inv_views(R + 4096)
        Z1, U1, Z2, U2 = (W(R + 9216 + 256 * i, 2, 2, RW_N) for i in range(4))
        SD = W(R + 10240, 2, P)
        hflat = hT[:, :, :].rearrange("p k s -> p (k s)")
        Fx = hflat[:, 0:1536].rearrange("p (d t k s) -> p d t k s", d=2, t=NT, k=3)
        RA = hflat[:, 1536:2560].rearrange("p (d t k s) -> p d t k s", d=2, t=NT, k=2)
        btl = hflat[:, 2560:3072].rearrange("p (d t s) -> p d t s", d=2, t=NT)
        ktl = hflat[:, 3072:3584].rearrange("p (d t s) -> p d t s", d=2, t=NT)
        BK = hflat[:, 3584:4096].rearrange("p (d k c) -> p d k c", d=2, k=2)
        Ytok = mem_v[0]
        mid_w, side_w = st[:, 336:351], st[:, 352:367]
        one_ka = st[:, 368:372]
        bon = st[:, 376:392].rearrange("p (t h) -> p t h", t=NT)
        sc0, scl = st[:, 392:394], st[:, 394:396]
        gsum, gmean, gvar, gms, gsd, grs = (st[:, 400 + 16 * i:416 + 16 * i] for i in range(6))

        def f_cols(v, f):
            return v[:, f, :].rearrange("p (t s) -> p t s", s=P)

        def pe_rwkv(pe):
            pe.wait_ge(s_oyc, len(ITEMS))
            rw = Gemm(pe, "od_rw")
            for c in range(4):
                rw.column_chunk(c, tiles=3 if c == 3 else 4)
            wait_chunks_taken(pe, after("od_rw"))
            pe.wait_ge(s_wide, 32)
            pe.wait_ge(s_rtanh, 1)
            for d in range(2):
                for t in range(NT):
                    nc.tensor.matmul(bank[2 * d + t][:, :], lhsT=wagT[64 * d:64 * d + 64, 0, t * P:(t + 1) * P],
                                     rhs=w2[64 * d:64 * d + 64, :], start=True, stop=True).then_inc(s_rwm, 1)
            for t in range(NT):
                nc.tensor.matmul(bank[4 + t][:, :], lhsT=wagT[:, 2, t * P:(t + 1) * P], rhs=g2,
                                 start=True, stop=True).then_inc(s_rgm, 1)
            for b in range(2):
                for t in range(NT):
                    for i in range(2):
                        m = nc.tensor.transpose(bank[6 + b][:, (2 * t + i) * P:(2 * t + i + 1) * P],
                                                vrT[:, 2 * b + i, t * P:(t + 1) * P], ident)
                m.then_inc(s_rvt, 1)
            for d in range(2):
                for fp in range(2):
                    pe.wait_ge(s_rlw0, 2 * d + fp + 1)
                    for i in range(2):
                        f = 2 * fp + i
                        m = nc.tensor.matmul(bank[2 * d + fp][:, i * S:(i + 1) * S],
                                             lhsT=a2[64 * d:64 * d + 64, f * P:(f + 1) * P],
                                             rhs=wagT[64 * d:64 * d + 64, 1, :], start=True, stop=True)
                    m.then_inc(s_ram, 1)
            pe.wait_ge(s_kksq, 1)
            pe.wait_ge(s_rgs, 2)
            for b in range(2):
                for i in range(2):
                    m = nc.tensor.matmul(bank[4 + b][:, i * S:(i + 1) * S], lhsT=const[:, C["halves"]],
                                         rhs=rtmp[:, 2 * b + i, :], start=True, stop=True)
                m.then_inc(s_kkm, 1)
            pe.wait_ge(s_pr, 1)
            pe.wait_ge(s_rv, 2)
            for t in range(NT):
                for f in range(RW_F):
                    m = nc.tensor.matmul(bank[6][:, t * RW_H + 2 * f:t * RW_H + 2 * f + 2],
                                         lhsT=rpr[:, f, t * P:(t + 1) * P], rhs=const[:, C["half_cols"]],
                                         start=True, stop=True)
            m.then_inc(s_prm, 1)
            pe.wait_ge(s_lw, 1)
            pe.wait_ge(s_ra, 8)
            pe.wait_ge(s_kkms, 1)
            pe.wait_ge(s_bon, 1)
            for f in range(RW_F):
                pe_rwkv_group(pe, f)
            pe.wait_ge(s_ry, 1)
            for b in range(2):
                for i in range(2):
                    for t in range(NT):
                        m = nc.tensor.transpose(aux[b][:, (2 * i + t) * P:(2 * i + t + 1) * P],
                                                Ytok[:, t, (2 * b + i) * P:(2 * b + i + 1) * P], ident)
                m.then_inc(s_ryt, 1)
            pe.wait_ge(s_ryT, 2)
            out = Gemm(pe, "od_out")
            for c in range(4):
                out.row_chunk(c, lambda k, t: ycT[:, k, t * P:(t + 1) * P] if k < 4 else hT_tile(k - 4, t), k_tiles=8)

        def pe_rwkv_group(pe, f):
            T, Tt, Pm, MT = rw_inv
            tile = lambda t: slice(t * P, (t + 1) * P)
            if f:
                pe.wait_ge(s_os, f + 4)
            for d in range(2):
                i0 = C["cum_mid"].start + 256 * d
                for t in range(NT):
                    m = nc.tensor.matmul(bank[d][:, t * S:(t + 1) * S], lhsT=lw[:, t, d, f * P:(f + 1) * P],
                                         rhs=const[:, i0:i0 + 256], start=True, stop=True)
                m.then_inc(s_rc, 1)
            for d in range(2):
                pe.wait_ge(s_rRA, 2 * f + d + 1)
                pe.wait_ge(s_rbk, 2 * f + d + 1)
                if d == 1:
                    pe.wait_ge(s_rF, 2 * f + 2)
                for i in range(2):
                    for t in range(NT):
                        m_ = 2 * i + t
                        bk = bank[(4 + m_) if d == 0 else m_]
                        rows = slice(64 * i, 64 * i + 64)
                        for j, lhs in enumerate((btl, ktl)):
                            m = nc.tensor.matmul(bk[:, j * 256:(j + 1) * 256], lhsT=lhs[rows, d, t, :],
                                                 rhs=RA[rows, d, t].rearrange("p k s -> p (k s)"), start=True, stop=True)
                        m.then_inc(s_rM, 1)
            pe.wait_ge(s_rMAT, 8 * f + 8)
            for d in range(2):
                for j, src in enumerate((btl, ktl)):
                    m = nc.tensor.transpose(bank[2][:, (2 * d + j) * P:(2 * d + j + 1) * P], src[:, d, FIRST_T[d], :], ident)
            m.then_inc(s_rbt, 1)
            for d in range(2):
                for i in range(2):
                    t1 = FIRST_T[d]
                    h = 2 * f + i
                    m = nc.tensor.matmul(bank[3][:, (2 * d + i) * RW_N:(2 * d + i + 1) * RW_N],
                                         lhsT=MAT[:, d, 2 * i + t1, 2], rhs=rv[:, t1, h * RW_N:(h + 1) * RW_N],
                                         start=True, stop=True)
            m.then_inc(s_rz1, 1)
            pe_inv(pe, 4 + f, rw_inv)
            pe.wait_ge(iv_t, (5 + f) * LEVELS * 2)
            pe.wait_ge(s_rz1s, f + 1)
            for d in range(2):
                for i in range(2):
                    m = nc.tensor.matmul(bank[3][:, (2 * d + i) * RW_N:(2 * d + i + 1) * RW_N],
                                         lhsT=Tt[:, d, 2 * i + FIRST_T[d]], rhs=Z1[:, d, i], start=True, stop=True)
            m.then_inc(s_vn1, 1)
            pe.wait_ge(s_rBK, f + 1)
            pe.wait_ge(s_vn1s, f + 5)
            for d in range(2):
                out = bank[2][:, d * P:(d + 1) * P]
                nc.tensor.matmul(out, lhsT=BK[:, d, 1], rhs=rv[:, FIRST_T[d], f * P:(f + 1) * P], start=True, stop=False)
                m = nc.tensor.matmul(out, lhsT=BK[:, d, 0], rhs=U1[:, d].rearrange("p i e -> p (i e)"), start=False, stop=True)
            m.then_inc(s_S, 1)
            pe.wait_ge(s_Ss, f + 5)
            for d in range(2):
                t2 = 1 - FIRST_T[d]
                nc.tensor.matmul(bank[3][:, d * P:(d + 1) * P], lhsT=RA[:, d, t2, 0], rhs=SD[:, d], start=True, stop=False)
                for i in range(2):
                    h = 2 * f + i
                    m = nc.tensor.matmul(bank[3][:, (2 * d + i) * RW_N:(2 * d + i + 1) * RW_N],
                                         lhsT=MAT[:, d, 2 * i + t2, 2], rhs=rv[:, t2, h * RW_N:(h + 1) * RW_N],
                                         start=False, stop=i == 1)
            m.then_inc(s_kS, 1)
            pe.wait_ge(s_R, f + 5)
            for d in range(2):
                for i in range(2):
                    m = nc.tensor.matmul(bank[2][:, (2 * d + i) * RW_N:(2 * d + i + 1) * RW_N],
                                         lhsT=Tt[:, d, 2 * i + 1 - FIRST_T[d]], rhs=Z2[:, d, i], start=True, stop=True)
            m.then_inc(s_vn2, 1)
            pe.wait_ge(s_vn2s, f + 5)
            for t in range(NT):
                d2 = 1 if t == 0 else 0
                nc.tensor.matmul(bank[0][:, t * P:(t + 1) * P], lhsT=RA[:, d2, t, 1], rhs=SD[:, d2], start=True, stop=False)
                for d in range(2):
                    U = U1 if t == FIRST_T[d] else U2
                    for i in range(2):
                        h = 2 * f + i
                        out = bank[0][:, t * P + i * RW_N:t * P + (i + 1) * RW_N]
                        nc.tensor.matmul(out, lhsT=MAT[:, d, 2 * i + t, 3], rhs=rv[:, t, h * RW_N:(h + 1) * RW_N],
                                         start=False, stop=False)
                        m = nc.tensor.matmul(out, lhsT=MAT[:, d, 2 * i + t, 1], rhs=U[:, d, i], start=False,
                                             stop=d == 1 and i == 1)
            m.then_inc(s_o, 1)

        FIRST_T = (0, 1)

        def act_rwkv(act):
            act.dma_start(ln_wb.rearrange("p a n -> p (a n)"), wide[:, 2560:3584]).then_inc(s_wide, 16)
            act.dma_start(wide_w, wide[:, 0:2560]).then_inc(s_wide, 16)
            act.wait_ge(s_rw, 1)
            for c in range(4):
                banks, taken = chunk_banks("od_rw", c)
                act.wait_ge(s_used, chunk_done("od_rw", c))
                if c >= 2:
                    act.wait_ge(s_rw, c)
                for b in range(2):
                    n = 1 if (c, b) == (3, 1) else 2
                    nc.scalar.activation(rstage[c % 2][:, 2 * b:2 * b + n, 1:S + 1],
                                         banks[b][:, 0:n * S].rearrange("p (h s) -> p h s", s=S), ACT.Copy).then_inc(taken, 1)
            act.wait_ge(s_kk0, 1)
            nc.scalar.activation(rtmp, kkT, ACT.Square).then_inc(s_kksq, 1)
            act.wait_ge(s_rw, 5)
            nc.scalar.activation(wagT[:, 0, :], wagT[:, 0, :], ACT.Tanh)
            nc.scalar.activation(wagT[:, 2, :], wagT[:, 2, :], ACT.Sigmoid).then_inc(s_rtanh, 1)
            for t in range(NT):
                act.wait_ge(s_rgm, t + 1)
                nc.scalar.activation(gout[:, t, :], bank[4 + t][:, :], ACT.Copy).then_inc(s_rgs, 1)
            act.wait_ge(s_rlw0, 4)
            nc.scalar.activation(lw, lw, ACT.Sigmoid).then_inc(s_lw, 1)
            for d in range(2):
                for fp in range(2):
                    act.wait_ge(s_ram, 2 * d + fp + 1)
                    for i in range(2):
                        f = 2 * fp + i
                        j = Q["rw_a0"].start + 4 * d + f
                        nc.scalar.activation(aT[:, d, f, :], bank[2 * d + fp][:, i * S:(i + 1) * S], ACT.Sigmoid,
                                             bias=par[:, j:j + 1]).then_inc(s_ra, 1)
            act.wait_ge(s_kkms, 1)
            nc.scalar.activation(rtmp, rtmp2, ACT.Sqrt).then_inc(s_kksd, 1)
            for f in range(RW_F):
                for d in range(2):
                    act.wait_ge(s_rc, 2 * f + d + 1)
                    v = bank[d][:, :].rearrange("p (t k s) -> p t k s", t=NT, k=2)
                    nc.scalar.activation(Fx[:, d, :, 0:2, :], v, ACT.Exp, scale=-KAPPA)
                    nc.scalar.activation(Fx[:, d, :, 2, :], v[:, :, 0, :], ACT.Exp, scale=KAPPA).then_inc(s_rF, 1)
                act.wait_ge(s_rbt, f + 1)
                nc.scalar.activation(BK.rearrange("p d k c -> p (d k) c"), four(bank[2]), ACT.Copy).then_inc(s_rBK, 1)
                act.wait_ge(s_rz1, f + 1)
                c4 = lambda v: v.rearrange("p d i e -> p (d i e)")
                nc.scalar.activation(c4(Z1), bank[3][:, 0:256], ACT.Copy).then_inc(s_rz1s, 1)
                act_inv(act, 4 + f, rw_inv)
                for ready, src, dst, scale, done in ((s_vn1, 3, U1, -1.0, s_vn1s), (s_kS, 3, Z2, 1.0, s_R),
                                                     (s_vn2, 2, U2, -1.0, s_vn2s)):
                    act.wait_ge(ready, f + 5)
                    nc.scalar.activation(c4(dst), bank[src][:, 0:256], ACT.Copy, scale=scale).then_inc(done, 1)
            act.wait_ge(s_gms, 1)
            nc.scalar.activation(gsd, gms, ACT.Sqrt).then_inc(s_gsd, 1)
            act.wait_ge(s_ryt, 1)
            nc.scalar.activation(hT[:, 0:2, :], aux[0][:, :].rearrange("p (h s) -> p h s", s=S), ACT.Copy).then_inc(s_ryT, 1)

        def dve_shift(dve, src, dst, tile0, n):
            for i in range(n):
                m = nc.vector.tensor_scalar(dst[:, i], src[:, i, 1:S + 1], mid_w[:, tile0 + i:tile0 + i + 1], None, MULT)
            dve_step(m)
            for at in (0, 2):
                for i in range(n):
                    m = nc.vector.scalar_tensor_tensor(out=dst[:, i], in0=src[:, i, at:at + S],
                                                       scalar=side_w[:, tile0 + i:tile0 + i + 1], in1=dst[:, i],
                                                       op0=MULT, op1=ADD)
                if at == 0:
                    dve_step(m)
            m.then_inc(s_rw, 1)

        def dve_rwkv(dve):
            mu = par[:, Q["rw_mu"]]
            ka = par[:, Q["rw_ka"]]
            nc.vector.tensor_scalar(mid_w, mu, -1.0, 1.0, MULT, ADD)
            nc.vector.tensor_scalar(side_w, mu, 0.5, None, MULT)
            nc.vector.tensor_scalar(one_ka, ka, -1.0, 1.0, MULT, ADD)
            dve.wait_ge(s_oyc, len(ITEMS))
            for s_ in rstage:
                nc.vector.memset(s_[:, :, 0:1], 0.0)
                m = nc.vector.memset(s_[:, :, S + 1:S + 2], 0.0)
            m.then_inc(s_rw, 1)
            dve.wait_ge(s_rw, 1)
            for c, dst in enumerate((rT, krT, vrT, wagT)):
                taken_of(dve, "od_rw", c)
                dve_shift(dve, rstage[c % 2], dst, 4 * c, 3 if c == 3 else 4)
                if c == 1:
                    dve.wait_ge(s_rw, 3)
                    for f in range(RW_F):
                        j = Q["rw_kk"].start + f
                        m = nc.vector.tensor_scalar(kkT[:, f, :], krT[:, f, :], par[:, j:j + 1], None, MULT)
                    m.then_inc(s_kk0, 1)
            w0v = w0.rearrange("p (d n) -> p d n", d=2)
            for d in range(2):
                for t in range(NT):
                    dve.wait_ge(s_rwm, 2 * d + t + 1)
                    nc.vector.tensor_tensor(lw[:, t, d, :], bank[2 * d + t][:, :], w0v[:, d], ADD).then_inc(s_rlw0, 1)
            for b in range(2):
                dve.wait_ge(s_rvt, b + 1)
                nc.vector.tensor_copy(rv[:, :, 2 * b * P:(2 * b + 2) * P],
                                      bank[6 + b][:, :].rearrange("p (t n) -> p t n", t=NT)).then_inc(s_rv, 1)
            for b in range(2):
                dve.wait_ge(s_kkm, b + 1)
                m = nc.vector.tensor_scalar(rtmp2[:, 2 * b:2 * b + 2, :], bank[4 + b][:, :].rearrange("p (h s) -> p h s", s=S),
                                            1e-6, None, ADD)
            m.then_inc(s_kkms, 1)
            for d in range(2):
                for f in range(RW_F):
                    dve.wait_ge(s_ra, 4 * d + f + 1)
                    j = Q["rw_ka"].start + f
                    m = nc.vector.tensor_scalar(kdT[:, d, f, :], aT[:, d, f, :], par[:, j:j + 1], one_ka[:, f:f + 1], MULT, ADD)
                dve_step(m)
                m = nc.vector.tensor_tensor(kdT[:, d], kdT[:, d], krT, MULT)
            m.then_inc(s_kd, 1)
            dve.wait_ge(s_kksd, 1)
            dve_step(nc.vector.reciprocal(rtmp2, rtmp))
            nc.vector.tensor_tensor(kkT, kkT, rtmp2, MULT).then_inc(s_kk, 1)
            dve.wait_ge(s_kd, 1)
            dve_step(nc.vector.tensor_tensor(rpr, kdT[:, 0], kdT[:, 1], ADD))
            for f in range(RW_F):
                j = Q["rw_rk"].start + f
                m = nc.vector.scalar_tensor_tensor(out=rpr[:, f, :], in0=rpr[:, f, :], scalar=par[:, j:j + 1],
                                                   in1=rT[:, f, :], op0=MULT, op1=MULT)
            m.then_inc(s_pr, 1)
            dve.wait_ge(s_prm, 1)
            nc.vector.tensor_copy(bon, bank[6][:, 0:16].rearrange("p (t h) -> p t h", t=NT)).then_inc(s_bon, 1)
            dve.wait_ge(s_kk, 1)
            for f in range(RW_F):
                dve_rwkv_group(dve, f)
            dve.wait_ge(s_os, RW_F + 4)
            y16 = Ytok[:, :, :].rearrange("p t (h e) -> p (t h) e", e=RW_N)
            z = W(R, NT, RW_W)
            z16 = z.rearrange("p t (h e) -> p (t h) e", e=RW_N)
            dve_step(nc.vector.reduce_sum(gsum, y16, AX_X))
            dve_step(nc.vector.tensor_scalar(gmean, gsum, 1.0 / RW_N, None, MULT))
            dve_step(nc.vector.tensor_tensor(y16, y16, lanes(gmean, RW_N), SUB))
            dve_step(nc.vector.tensor_tensor(z16, y16, y16, MULT))
            dve_step(nc.vector.reduce_sum(gvar, z16, AX_X))
            nc.vector.tensor_scalar(gms, gvar, 1.0 / RW_N, GN_EPS, MULT, ADD).then_inc(s_gms, 1)
            dve_step(nc.vector.tensor_tensor(z16, rv.rearrange("p t (h e) -> p (t h) e", e=RW_N),
                                             lanes(bon.rearrange("p t h -> p (t h)"), RW_N), MULT))
            dve.wait_ge(s_gsd, 1)
            dve_step(nc.vector.reciprocal(grs, gsd))
            dve_step(nc.vector.tensor_tensor(y16, y16, lanes(grs, RW_N), MULT))
            row = lambda j: ln_wb[:, j].unsqueeze(1).broadcast_to([P, NT, RW_W])
            dve_step(nc.vector.tensor_tensor(Ytok[:, :, :], Ytok[:, :, :], row(0), MULT))
            dve_step(nc.vector.tensor_tensor(Ytok[:, :, :], Ytok[:, :, :], row(1), ADD))
            dve_step(nc.vector.tensor_tensor(Ytok[:, :, :], Ytok[:, :, :], z, ADD))
            nc.vector.tensor_tensor(Ytok[:, :, :], Ytok[:, :, :], gout, MULT).then_inc(s_ry, 1)
            dve.wait_ge(s_ryt, 2)
            nc.vector.tensor_copy(hT[:, 2:4, :], aux[1][:, :].rearrange("p (h s) -> p h s", s=S)).then_inc(s_ryT, 1)
            for c in range(4):
                dve_add_to_x(dve, "od_out", c)

        def dve_rwkv_group(dve, f):
            for d in range(2):
                dve.wait_ge(s_rF, 2 * f + d + 1)
                nc.vector.tensor_tensor(RA[:, d, :, 0, :], f_cols(kkT, f), Fx[:, d, :, 1, :], MULT)
                nc.vector.tensor_tensor(RA[:, d, :, 1, :], f_cols(rT, f), Fx[:, d, :, 0, :], MULT).then_inc(s_rRA, 1)
            for d in range(2):
                t1, last, first = FIRST_T[d], (P - 1, 0)[d], (0, P - 1)[d]
                dve_step(nc.vector.reciprocal(sc0[:, d:d + 1], Fx[:, d, 1 - t1, 1, first:first + 1]))
                m = nc.vector.tensor_tensor(scl[:, d:d + 1], sc0[:, d:d + 1], Fx[:, d, t1, 0, last:last + 1], MULT)
            dve_step(m)
            for d in range(2):
                for m_ in range(4):
                    n = 4 * d + m_
                    dve.wait_ge(s_rM, 8 * f + n + 1)
                    bk = bank[(4 + m_) if d == 0 else m_]
                    i0 = C["causal"].start + 256 * d
                    mask = const[:, i0:i0 + 256].unsqueeze(1).broadcast_to([P, 2, 256])
                    nc.vector.tensor_tensor(MAT[:, d, m_].rearrange("p (two k) s -> p two (k s)", two=2),
                                            bk[:, :].rearrange("p (two k) -> p two k", two=2), mask, MULT).then_inc(s_rMAT, 1)
            dve_inv(dve, 4 + f, rw_inv)
            dve.wait_ge(s_S, f + 5)
            for d in range(2):
                m = nc.vector.scalar_tensor_tensor(out=SD[:, d], in0=bank[2][:, d * P:(d + 1) * P], scalar=scl[:, d:d + 1],
                                                   in1=const[:, C["halves"]], op0=MULT, op1=MULT)
            m.then_inc(s_Ss, 1)
            dve.wait_ge(s_o, f + 5)
            nc.vector.tensor_copy(Ytok[:, :, f * P:(f + 1) * P],
                                  bank[0][:, 0:256].rearrange("p (t n) -> p t n", t=NT)).then_inc(s_os, 1)

        def pool_odd(pool):
            pool.wait_ge(s_kk, 1)
            pool.wait_ge(s_kd, 1)
            for d in range(2):
                m = nc.gpsimd.tensor_tensor(aT[:, d], aT[:, d], kkT, MULT)
            m.then_inc(s_b, 1)
            pool.wait_ge(s_b, 1)
            for f in range(RW_F):
                for d in range(2):
                    pool.wait_ge(s_rF, 2 * f + d + 1)
                    nc.gpsimd.tensor_tensor(btl[:, d], f_cols(aT[:, d], f), Fx[:, d, :, 2, :], MULT)
                    nc.gpsimd.tensor_tensor(ktl[:, d], f_cols(kdT[:, d], f), Fx[:, d, :, 2, :], MULT).then_inc(s_rbk, 1)
                AT = [MAT[:, d, :, 0, :] for d in range(2)]
                for level in range(LEVELS):
                    for d in range(2):
                        if level == 0:
                            pool.wait_ge(s_rMAT, 8 * f + 4 * d + 4)
                        pool_inv_mask(pool, 4 + f, AT, rw_inv, level, d)

        def pe_odd(pe):
            pe_window(pe)
            pe_rwkv(pe)

        def act_odd(act):
            act_window(act)
            act_rwkv(act)

        def dve_odd(dve):
            dve_window(dve)
            dve_rwkv(dve)

        def norm_src(name):
            return memx if name.startswith("mem") else x

        HT_FREE = {"mem0": 0, "mem1": chunk_done("mem_v0", 0), "mix0": chunk_done("mem_v1", 0),
                   "xattn0": chunk_done("ev_out", 3), "ffn0": chunk_done("xa_q0", 0),
                   "mix1": chunk_done("ffn_up0", 15), "xattn1": chunk_done("od_out", 3),
                   "ffn1": chunk_done("xa_q1", 0)}

        def after(name):
            return starts[name][0] + dict((n, c) for n, c, _ in GEMMS)[name]

        X_READY = {"xattn0": after("ev_out"), "ffn0": after("xa_o0"), "mix1": after("ffn_down0"),
                   "xattn1": after("od_out"), "ffn1": after("xa_o1")}

        def run_norm(eng, norm, name):
            if name in X_READY:
                wait_chunks_taken(eng, X_READY[name])
            norm(eng, name, norm_src(name), HT_FREE[name])

        @block.tensor
        def _(pe):
            pe.wait_ge(s_load, 64)
            pe_bias(pe)
            pe_norm(pe, "mem0", before=[(s_bias_s, DSA_H)])
            pe_memory(pe, 0)
            pe_norm(pe, "mem1", before=[(s_mkT, 2)])
            pe_memory(pe, 1)
            pe_norm(pe, "mix0", before=[(s_mkT, 4)])
            pe_even(pe)
            for l in range(2):
                if l:
                    pe_norm(pe, "mix1", before=[(s_xoT, 2)])
                    pe_odd(pe)
                pe_norm(pe, f"xattn{l}")
                pe_cross(pe, l)
                pe_norm(pe, f"ffn{l}")
                pe_ffn(pe, l)

        @block.scalar
        def _(act):
            act_bias(act)
            act.wait_ge(s_load, 64)
            for l in range(2):
                run_norm(act, act_norm, f"mem{l}")
                act_memory(act, l)
            run_norm(act, act_norm, "mix0")
            act.wait_ge(s_bias_out, 16)
            act_even(act)
            for l in range(2):
                if l:
                    run_norm(act, act_norm, "mix1")
                    act_odd(act)
                run_norm(act, act_norm, f"xattn{l}")
                act_cross(act, l)
                run_norm(act, act_norm, f"ffn{l}")
                act_ffn(act, l)

        @block.vector
        def _(dve):
            dve.wait_ge(s_load, 64)
            nc.vector.tensor_tensor(gqk, par[:, Q["xa_qn"]], par[:, Q["xa_kn"]], MULT).then_inc(s_gqk, 1)
            for l in range(2):
                run_norm(dve, dve_norm, f"mem{l}")
                dve_memory(dve, l)
            run_norm(dve, dve_norm, "mix0")
            dve.wait_ge(s_bias_out, 16)
            dve_even(dve)
            for l in range(2):
                if l:
                    run_norm(dve, dve_norm, "mix1")
                    dve_odd(dve)
                run_norm(dve, dve_norm, f"xattn{l}")
                dve_cross(dve, l)
                run_norm(dve, dve_norm, f"ffn{l}")
                dve_ffn(dve, l)

        @block.gpsimd
        def _(pool):
            nc.gpsimd.memset(rel[N_BUCKETS:NB], NEG).then_inc(s_neg, 1)
            pool.wait_ge(s_load, 64)
            pool_even(pool)
            pool_odd(pool)


def constants():
    import math

    import numpy as np

    at, n = columns(CONST_COLS)
    c = np.zeros((P, n), np.float32)
    s, t = np.arange(P)[:, None], np.arange(P)[None, :]
    c[:, at["ident"]] = s == t
    level = np.zeros((P, 2, LEVELS, P), np.float32)
    for n_, size in enumerate(1 << np.arange(LEVELS)):
        pair = (s // (2 * size)) == (t // (2 * size))
        level[:, 0, n_] = pair & (s // size < t // size)
        level[:, 1, n_] = pair & (s // size > t // size)
    c[:, at["level"]] = level.reshape(P, -1)
    c[:, at["neg"]] = np.where(np.hstack([s <= t, s >= t]), 0.0, NEG)
    low, high = s < P // 2, s >= P // 2
    mid = [(s <= t) * 1.0 - low, (s < t) * 1.0 - low, (s >= t) * 1.0 - high, (s > t) * 1.0 - high]
    c[:, at["cum_mid"]] = np.hstack(mid)
    c[:, at["causal"]] = np.hstack([s < t, s <= t, s > t, s >= t])
    c[:, at["halves"]] = (s // RW_N) == (t // RW_N)
    c[:, at["ones"]] = 1.0
    c[:, at["half_cols"]] = np.hstack([low, high])

    table = np.zeros((N_BUCKETS + 1, DSA_G, 512), np.float32)
    half = N_BUCKETS // 2
    exact = half // 2
    for g, dil in enumerate(DILATIONS):
        rel = np.arange(512) - (S - 1)
        inside = (rel % dil == 0) & (np.abs(rel) <= N_SIDE * dil)
        dist = np.abs(rel)
        ratio = np.maximum(dist, exact).astype(np.float32) / np.float32(exact)
        scaled = np.log(ratio) / np.float32(math.log(MAX_DIST / exact))
        large = np.minimum(exact + (scaled * np.float32(half - exact)).astype(np.int32), half - 1)
        bucket = np.where(rel > 0, half, 0) + np.where(dist < exact, dist, large)
        for n_ in range(512):
            table[bucket[n_] if inside[n_] else N_BUCKETS, g, n_] = 1.0
    return c, table.reshape(N_BUCKETS + 1, -1)


def kernel(**inputs):
    import numpy as np
    import concourse.bacc as bacc
    from concourse.bass_utils import run_bass_kernel_spmd

    a = {name: np.asarray(value) for name, value in inputs.items()}

    sc = a["ev_w_in"][0][:, 4 * DN_W + 4 * DN_H:]
    sc_order = [(part, half) for half in range(2) for part in (1, 2, 0)]
    rw = a["od_w_in"][0][:, 3 * DSA_H * P:]
    matrices = {
        "ev_qkv": a["ev_w_in"][0][:, :3 * DN_W],
        "ev_gate": a["ev_w_in"][0][:, 3 * DN_W:4 * DN_W],
        "ev_sc": np.hstack([sc[:, p * 1024 + h * 512:p * 1024 + h * 512 + 512] for p, h in sc_order]),
        "ev_out": a["ev_w_out"][0],
        "od_q": a["od_w_in"][0][:, :DSA_H * P],
        "od_k": a["od_w_in"][0][:, DSA_H * P:2 * DSA_H * P],
        "od_v": a["od_w_in"][0][:, 2 * DSA_H * P:3 * DSA_H * P],
        "od_rw": np.pad(rw, ((0, 0), (0, 2048 - rw.shape[1]))),
        "od_out": a["od_w_out"][0],
    }
    for l in range(2):
        matrices[f"mem_k{l}"], matrices[f"mem_v{l}"] = a["xa_wk"][l], a["xa_wv"][l]
        matrices[f"xa_q{l}"], matrices[f"xa_o{l}"] = a["xa_wq"][l], a["xa_wo"][l]
        matrices[f"ffn_up{l}"], matrices[f"ffn_down{l}"] = a["ffn_w1"][l], a["ffn_w2"][l]
    starts, _, n_units = gemm_starts()
    stream = np.zeros((n_units, P, UNIT), np.float32)
    for name, chunks, per in GEMMS:
        w, u = matrices[name], starts[name][1]
        k, n = w.shape
        width = 1024 if per == 0.5 else 512
        kt = min(k // P, UNIT // width)
        got = w.reshape(k // (kt * P), kt, P, n // width, width).transpose(3, 0, 2, 1, 4)
        stream[u:u + int(chunks * per)] = got.reshape(-1, P, UNIT)

    tiles = lambda v: np.ascontiguousarray(v.reshape(-1, P).T)
    rows = lambda v: np.broadcast_to(v.reshape(1, -1), (P, v.size))
    at, n = columns(PARAM_COLS)
    small = np.zeros((P, n), np.float32)
    for l in range(2):
        for name, source in (("mix", "norm_mix"), ("xattn", "norm_xattn"), ("mem", "norm_mem"), ("ffn", "norm_ffn")):
            small[:, at[f"g_{name}{l}"]] = tiles(a[source][l])
    small[:, at["xa_qn"]], small[:, at["xa_kn"]] = a["xa_qn"].T, a["xa_kn"].T
    small[:, at["dn_conv"]] = a["dn_conv"][0].reshape(24, P, 3).transpose(1, 0, 2).reshape(P, 72)
    small[:, at["sc_conv"]] = a["sc_conv"][0].reshape(8, P, 3).transpose(1, 0, 2).reshape(P, 24)
    small[:, at["dn_norm"]] = rows(a["dn_norm"][0])
    small[:, at["a_log"]], small[:, at["dt_bias"]] = rows(a["dn_a_log"][0]), rows(a["dn_dt_bias"][0])
    small[:, at["ab_w"]] = (a["ev_w_in"][0][:, 4 * DN_W:4 * DN_W + 4 * DN_H]
                            .reshape(KD, P, 4 * DN_H).transpose(1, 0, 2).reshape(P, 512))
    small[:, at["ca_qn"]], small[:, at["ca_kn"]] = a["ca_qn"].T, a["ca_kn"].T
    small[:, at["rw_mu"]] = tiles(a["rw_mu"][0])
    small[:, at["rw_a0"]] = tiles(a["rw_a0"][0])
    small[:, at["rw_kk"]], small[:, at["rw_ka"]] = tiles(a["rw_k_k"][0]), tiles(a["rw_k_a"][0])
    small[:, at["rw_rk"]] = tiles(a["rw_r_k"][0])
    at, n = columns(WIDE_COLS)
    wide = np.zeros((P, n), np.float32)
    wide[:, at["w2"]], wide[:, at["a2"]] = a["rw_w2"][0].reshape(P, RW_W), a["rw_a2"][0].reshape(P, RW_W)
    wide[:, at["g2"]] = a["rw_g2"][0]
    wide[:, at["w0"]] = rows(a["rw_w0"][0])
    wide[:, at["ln_w"]], wide[:, at["ln_b"]] = rows(a["rw_ln_w"][0]), rows(a["rw_ln_b"][0])

    masks, table = constants()
    sent = {
        "x": a["x"][0], "mem": a["mem"][0], "stream": stream, "small": small, "wide": wide,
        "masks": masks, "bias_table": table, "rel_bias": a["rel_bias"],
    }
    nc = bacc.Bacc("TRN2", target_bir_lowering=False, num_devices=1, dynamic_dma_scratch_size=1024)
    arrays = {f"in_{name}": np.ascontiguousarray(v) for name, v in sent.items()}
    aps = [nc.dram_tensor(name, v.shape, mybir.dt.from_np(v.dtype), kind="ExternalInput").ap()
           for name, v in arrays.items()]
    out = nc.dram_tensor("out", (S, D), F32, kind="ExternalOutput").ap()
    scratch = nc.dram_tensor("bias_rows", (DSA_H, P, 512), F32, kind="Internal").ap()
    build(nc, *aps, scratch, out)
    r = run_bass_kernel_spmd(nc, [arrays], core_ids=[0])
    return r.results[0]["out"].reshape(1, S, D)
```

```python
from contextlib import ExitStack

import concourse.bass as bass
from concourse import mybir

P = 128
D = 2048
S = 256
NT = S // P
KD = D // P
RAW = 4
SPLIT = 4
AHEAD = SPLIT
UNIT = 1024
BLOCK = 2 * UNIT
WORK = 19200
F_FF = 4 * D
RMS_EPS = 1e-6

ALU = mybir.AluOpType
ACT = mybir.ActivationFunctionType
F32 = mybir.dt.float32
F32R = mybir.dt.float32r
AX_X = mybir.AxisListType.X

MULT, ADD, SUB, MAX = ALU.mult, ALU.add, ALU.subtract, ALU.max

DN_H = 8
DN_W = DN_H * P
DSA_G = 3
DSA_HG = 4
DSA_H = DSA_G * DSA_HG
DILATIONS = (1, 4, 16)
N_SIDE = 64
N_BUCKETS = 32
MAX_DIST = 1024
NEG = -1e30
RW_H = 8
RW_N = 64
RW_W = RW_H * RW_N
RW_F = RW_W // P
KAPPA = 0.6065306597126334
GN_EPS = 64e-5
XA_H = 4
HEAD_SCALE = float(P) ** -0.5
LEVELS = 7

FF_TURNS = 4
FF_CHUNKS = 8
FF_UNITS = 64
GEMMS = [
    ("mem_k0", 1, 8), ("mem_v0", 1, 8), ("mem_k1", 1, 8), ("mem_v1", 1, 8),
    ("ev_qkv", 6, 8), ("ev_gate", 2, 8), ("ev_sc", 6, 8), ("ev_out", 4, 8),
    ("xa_q0", 1, 8), ("xa_o0", 4, 2), ("ffn0", FF_TURNS * FF_CHUNKS, 8),
    ("od_q", 3, 8), ("od_k", 3, 8), ("od_v", 3, 8), ("od_rw", 4, 8), ("od_out", 4, 4),
    ("xa_q1", 1, 8), ("xa_o1", 4, 2), ("ffn1", FF_TURNS * FF_CHUNKS, 8),
]
UNITS_OF = {name: units for name, _, units in GEMMS}


def gemm_starts():
    at, chunk, unit = {}, 0, 0
    for name, chunks, units in GEMMS:
        at[name] = (chunk, unit)
        chunk += chunks
        unit += chunks * units
    return at, chunk, unit


CONST_COLS = [
    ("ident", P), ("level", 2 * LEVELS * P),
    ("neg", 2 * P), ("cum_mid", 4 * P), ("causal", 4 * P), ("halves", P), ("ones", 1), ("half_cols", 2),
]
PARAM_COLS = [
    ("g_mix0", 16), ("g_mix1", 16), ("g_xattn0", 16), ("g_xattn1", 16),
    ("g_mem0", 16), ("g_mem1", 16), ("g_ffn0", 16), ("g_ffn1", 16),
    ("xa_qn", 2), ("xa_kn", 2), ("dn_conv", 72), ("sc_conv", 24), ("dn_norm", P),
    ("a_log", 16), ("dt_bias", 16), ("ab_w", 512),
    ("ca_qn", 1), ("ca_kn", 1), ("rw_mu", 15), ("rw_a0", 8), ("rw_kk", 4), ("rw_ka", 4), ("rw_rk", 4),
]
WIDE_COLS = [("w2", 512), ("a2", 512), ("g2", 512), ("w0", 1024), ("ln_w", 512), ("ln_b", 512)]


def columns(table):
    at, n = {}, 0
    for name, width in table:
        at[name] = slice(n, n + width)
        n += width
    return at, n


class Chain:

    def __init__(self, engine, sem):
        self.engine, self.sem, self.n = engine, sem, 0

    def __call__(self, instruction):
        self.n += 1
        instruction.then_inc(self.sem, 1)
        self.engine.wait_ge(self.sem, self.n)


def build(nc, x_in, mem_in, stream, small, wide, masks, bias_table, rel_bias, bias_rows, x_out):
    starts, n_chunks, n_units = gemm_starts()
    C, n_const = columns(CONST_COLS)
    Q, n_param = columns(PARAM_COLS)
    WD, n_wide = columns(WIDE_COLS)

    ctx = ExitStack()
    with ctx:
        def sem(name):
            return ctx.enter_context(nc.semaphore(name))

        at = [1152]

        def place(name, shape, dtype=F32, offset=None):
            n = 4
            for d in shape[1:]:
                n *= d
            if offset is None:
                offset = at[0]
                at[0] += (n + 31) // 32 * 32
            return nc.alloc_sbuf_tensor_at(name, shape, dtype, offset=offset)

        x = place("x", [P, NT, D])
        const = place("const", [P, n_const])
        par = place("par", [P, n_param])
        mem_kT = [place(f"mem_kT{l}", [P, XA_H, S]) for l in range(2)]
        mem_v = [place(f"mem_v{l}", [P, NT, XA_H * P]) for l in range(2)]
        st = place("st", [P, 768])
        raw = place("raw", [P, RAW, BLOCK])
        split_hi = place("split_hi", [P, SPLIT, UNIT], F32R)
        split_lo = place("split_lo", [P, SPLIT, UNIT], F32R)
        hT_at = at[0]
        hT_hi = place("hT_hi", [P, KD, S], F32R)
        hT_lo = place("hT_lo", [P, KD, S], F32R)
        hwork = place("hwork", [P, 2 * KD * S], offset=hT_at)
        work_at = at[0]
        work = place("work", [P, WORK])
        u_hi = place("u_hi", [P, 16, S], F32R, offset=work_at)
        u_lo = place("u_lo", [P, 16, S], F32R, offset=work_at + 4 * 4096)
        ab_hi = place("ab_hi", [P, 512], F32R, offset=work_at + 4 * 16384)
        ab_lo = place("ab_lo", [P, 512], F32R, offset=work_at + 4 * 16896)
        bank = [ctx.enter_context(nc.psum_tensor(f"bank{i}", [P, 512], F32)) for i in range(8)]
        aux = bank[4:]

        def view(area, at, *shape):
            n = 1
            for d in shape:
                n *= d
            v = area[:, at:at + n]
            if len(shape) == 1:
                return v
            names = "abcd"[:len(shape)]
            return v.rearrange(f"p ({' '.join(names)}) -> p {' '.join(names)}",
                               **dict(zip(names[1:], shape[1:])))

        def W(at, *shape):
            return view(work, at, *shape)

        def H(at, *shape):
            return view(hwork, at, *shape)

        def four(ap):
            return ap[:, :].rearrange("p (m n) -> p m n", n=P)

        def const_of(name, i, width=P):
            return const[:, C[name].start + i * width:C[name].start + (i + 1) * width]

        ident = const[:, C["ident"]]
        ones_col = const[:, C["ones"]]

        s_load = sem("s_load")
        s_raw = [sem(f"s_raw{i}") for i in range(RAW)]
        s_hi, s_lo = sem("s_hi"), sem("s_lo")
        s_used = sem("s_used")
        s_taken = [sem(f"s_taken{i}") for i in range(2)]
        s_dve, s_act, s_pool = sem("s_dve"), sem("s_act"), sem("s_pool")
        s_sq = sem("s_sq")
        s_ms = sem("s_ms")
        s_sd = sem("s_sd")
        s_rstd = sem("s_rstd")
        s_xn = sem("s_xn")
        s_tr = sem("s_tr")
        s_hTh, s_hTl = sem("s_hTh"), sem("s_hTl")
        s_mk_ms, s_mk_sd, s_mk = sem("s_mk_ms"), sem("s_mk_sd"), sem("s_mk")
        s_mk_tr, s_mkT = sem("s_mk_tr"), sem("s_mkT")
        s_xq, s_xss, s_xms, s_xsd = (sem(n) for n in ("s_xq", "s_xss", "s_xms", "s_xsd"))
        s_xlog, s_xnm, s_xexp, s_xp = sem("s_xlog"), sem("s_xnm"), sem("s_xexp"), sem("s_xp")
        s_xpt, s_xpt_a, s_xpt_d = sem("s_xpt"), sem("s_xpt_a"), sem("s_xpt_d")
        s_xo, s_xoh, s_xoT = sem("s_xo"), sem("s_xoh"), sem("s_xoT")
        s_uh, s_u = sem("s_uh"), sem("s_u")
        s_ysp, s_abw = sem("s_ysp"), sem("s_abw")
        s_gqk = sem("s_gqk")
        s_out = sem("s_out")
        iv_mt, iv_p, iv_ps, iv_q, iv_t = (sem(n) for n in ("iv_mt", "iv_p", "iv_ps", "iv_q", "iv_t"))
        s_ab, s_abv, s_ax, s_sp, s_g = (sem(n) for n in ("s_ab", "s_abv", "s_ax", "s_sp", "s_g"))
        s_cv, s_silu = sem("s_cv"), sem("s_silu")
        s_dsq, s_kvt, s_kv_a, s_kv_d = sem("s_dsq"), sem("s_kvt"), sem("s_kv_a"), sem("s_kv_d")
        s_dss, s_cum, s_cumv, s_dms, s_dsd, s_dE, s_stats = (
            sem(n) for n in ("s_dss", "s_cum", "s_cumv", "s_dms", "s_dsd", "s_dE", "s_stats"))
        s_pre, s_diff, s_D, s_eg, s_AT, s_qtg, s_vb = (
            sem(n) for n in ("s_pre", "s_diff", "s_D", "s_eg", "s_AT", "s_qtg", "s_vb"))
        s_vn1, s_vn1s, s_S, s_Ss, s_kS, s_R, s_vn2, s_vn2s, s_o, s_os = (
            sem(n) for n in ("s_vn1", "s_vn1s", "s_S", "s_Ss", "s_kS", "s_R", "s_vn2", "s_vn2s", "s_o", "s_os"))
        s_oms, s_osd, s_y, s_yt, s_yT = (sem(n) for n in ("s_oms", "s_osd", "s_y", "s_yt", "s_yT"))
        s_bt_in, s_bias_m, s_bias_s, s_bias_out, s_bias_in = (
            sem(n) for n in ("s_bt_in", "s_bias_m", "s_bias_s", "s_bias_out", "s_bias_in"))
        s_neg = sem("s_neg")
        s_oss, s_oms0, s_osd0 = (sem(n) for n in ("s_oss", "s_oms0", "s_osd0"))
        s_ok, s_okt, s_okT_a, s_okT_d = (
            sem(n) for n in ("s_ok", "s_okt", "s_okT_a", "s_okT_d"))
        s_ol, s_onm, s_oexp, s_op, s_opt, s_opt_a, s_opt_d, s_opv, s_oyc = (
            sem(n) for n in ("s_ol", "s_onm", "s_oexp", "s_op", "s_opt", "s_opt_a", "s_opt_d", "s_opv", "s_oyc"))
        s_wide, s_rw, s_rtanh, s_rwm, s_rlw0, s_lw, s_rgm, s_rgs, s_ram, s_ra, s_rvt, s_rv = (
            sem(n) for n in ("s_wide", "s_rw", "s_rtanh", "s_rwm", "s_rlw0", "s_lw", "s_rgm", "s_rgs", "s_ram", "s_ra", "s_rvt", "s_rv"))
        s_kk0, s_kksq, s_kkm, s_kkms, s_kksd, s_kk, s_kd, s_pr, s_prm, s_bon = (
            sem(n) for n in ("s_kk0", "s_kksq", "s_kkm", "s_kkms", "s_kksd", "s_kk", "s_kd", "s_pr", "s_prm", "s_bon"))
        s_rc, s_rF, s_rRA, s_rbk, s_rM, s_rMAT, s_rbt, s_rBK, s_rz1, s_rz1s = (
            sem(n) for n in ("s_rc", "s_rF", "s_rRA", "s_rbk", "s_rM", "s_rMAT", "s_rbt", "s_rBK", "s_rz1", "s_rz1s"))
        s_gms, s_gsd, s_ry, s_ryt = (sem(n) for n in ("s_gms", "s_gsd", "s_ry", "s_ryt"))
        block = ctx.enter_context(nc.Block())

        NORMS = ["mem0", "mem1", "mix0", "xattn0", "ffn0", "mix1", "xattn1", "ffn1"]
        NORM_NO = {name: i for i, name in enumerate(NORMS)}
        xn = W(8192, NT, D)
        memx = W(12288, NT, D)

        dve_chain, act_chain, pool_chain = Chain(nc.vector, s_dve), Chain(nc.scalar, s_act), Chain(nc.gpsimd, s_pool)
        dve_step, act_step, pool_step = dve_chain, act_chain, pool_chain

        def wait_chunks_taken(eng, chunk):
            for parity in range(2):
                n = (chunk + 1 - parity) // 2
                if n:
                    eng.wait_ge(s_taken[parity], 2 * n)

        ss, msq, sdv, rstd = st[:, 0:2], st[:, 2:4], st[:, 4:6], st[:, 6:8]
        mk_ss, mk_ms, mk_sd, mk_r = (st[:, 8 + 8 * i:16 + 8 * i] for i in range(4))
        xa_ms, xa_sd, xa_r, xa_rq = (st[:, 40 + 8 * i:48 + 8 * i] for i in range(4))
        xa_mx, xa_nm, xa_sum, xa_rs = (st[:, 72 + 8 * i:80 + 8 * i] for i in range(4))
        gqk = st[:, 104:106]

        def f32(ap):
            return ap.bitcast(F32)

        def write_hi(act, u, turn=0):
            b = u // 2
            if u % 2 == 0:
                act.wait_ge(s_raw[b % RAW], turn * (FF_UNITS // 2 // RAW * 16) + (b // RAW + 1) * 16)
            if u >= SPLIT:
                act.wait_ge(s_used, turn * FF_UNITS + (u - SPLIT + 1))
            nc.scalar.activation(split_hi[:, u % SPLIT], raw[:, b % RAW, (u % 2) * UNIT:(u % 2 + 1) * UNIT],
                                 ACT.Copy).then_inc(s_hi, 1)

        def write_lo(dve, u, turn=0):
            b = u // 2
            dve.wait_ge(s_hi, turn * FF_UNITS + (u + 1))
            nc.vector.tensor_tensor(split_lo[:, u % SPLIT], raw[:, b % RAW, (u % 2) * UNIT:(u % 2 + 1) * UNIT],
                                    f32(split_hi[:, u % SPLIT]), SUB).then_inc(s_lo, 1)

        next_hi, next_lo = [0], [0]

        def hi_upto(act, n):
            while next_hi[0] < min(n, n_units):
                write_hi(act, next_hi[0])
                next_hi[0] += 1

        def lo_upto(dve, n):
            while next_lo[0] < min(n, n_units):
                write_lo(dve, next_lo[0])
                next_lo[0] += 1

        class Gemm:

            def __init__(self, pe, name, turn=0, turns=(FF_CHUNKS, FF_UNITS)):
                self.pe, self.turn, self.turns = pe, turn, turns
                self.chunk0, self.unit0 = starts[name]
                self.per = UNITS_OF[name]

            def unit(self, n):
                u = self.unit0 + n
                self.pe.wait_ge(s_lo, self.turn * self.turns[1] + (u + 1))
                return split_hi[:, u % SPLIT], split_lo[:, u % SPLIT]

            def banks(self, c):
                g = self.chunk0 + c
                if g >= 2:
                    self.pe.wait_ge(s_taken[g % 2], self.turn * self.turns[0] + g // 2 * 2)
                return bank[2 * (g % 2):2 * (g % 2) + 2]

            def row_chunk(self, c, lhsT, k_tiles=KD, k_ready=None):
                acc = self.banks(c)
                for k in range(k_tiles):
                    if k_ready:
                        k_ready(k)
                    if k % 2 == 0:
                        w_hi, w_lo = self.unit(c * self.per + k // 2)
                    cols = slice((k % 2) * 512, (k % 2 + 1) * 512)
                    for t in range(NT):
                        x_hi, x_lo = lhsT(k, t)
                        out = acc[t][:, :]
                        nc.tensor.matmul(out, lhsT=x_hi, rhs=w_hi[:, cols], start=k == 0, stop=False)
                        nc.tensor.matmul(out, lhsT=x_hi, rhs=w_lo[:, cols], start=False, stop=False)
                        m = nc.tensor.matmul(out, lhsT=x_lo, rhs=w_hi[:, cols], start=False, stop=k == k_tiles - 1)
                    if k % 2:
                        m.then_inc(s_used, 1)

            def column_chunk(self, c, tiles=4):
                acc = self.banks(c)
                for i in range(tiles):
                    for j in range(2):
                        n = c * self.per + 2 * i + j
                        w_hi, w_lo = self.unit(n)
                        used = 1
                        if (i, j) == (tiles - 1, 1) and tiles < 4:
                            used += 2 * (4 - tiles)
                            self.unit(n + used - 1)
                        for kk in range(8):
                            k = 8 * j + kk
                            cols = slice(kk * P, (kk + 1) * P)
                            out = acc[i // 2][:, (i % 2) * S:(i % 2 + 1) * S]
                            nc.tensor.matmul(out, lhsT=w_hi[:, cols], rhs=hT_hi[:, k, :], start=k == 0, stop=False)
                            nc.tensor.matmul(out, lhsT=w_hi[:, cols], rhs=hT_lo[:, k, :], start=False, stop=False)
                            m = nc.tensor.matmul(out, lhsT=w_lo[:, cols], rhs=hT_hi[:, k, :], start=False, stop=k == KD - 1)
                        m.then_inc(s_used, used)

        def chunk_done(name, c):
            return starts[name][1] + UNITS_OF[name] * (c + 1)

        def chunk_banks(name, c):
            parity = (starts[name][0] + c) % 2
            return bank[2 * parity:2 * parity + 2], s_taken[parity]

        @block.sync
        def _(sp):
            sp.dma_start(const[:, :], masks).then_inc(s_load, 16)
            sp.dma_start(memx, mem_in.rearrange("(t p) d -> p t d", p=P)).then_inc(s_load, 16)
            sp.dma_start(par[:, :], small).then_inc(s_load, 16)

            def load(b, slot):
                sp.dma_start(raw[:, slot, :], stream[b]).then_inc(s_raw[slot], 16)

            for slot in range(RAW):
                load(slot, slot)
            sp.dma_start(x[:, :, :], x_in.rearrange("(t p) d -> p t d", p=P)).then_inc(s_load, 16)
            with sp.Fori(1, n_units // 2 // RAW) as turn:
                for slot in range(RAW):
                    sp.wait_ge(s_lo, turn * (2 * RAW) + 2 * (slot - RAW + 1))
                    load(turn * RAW + slot, slot)
            wait_chunks_taken(sp, n_chunks)
            sp.dma_start(x_out.rearrange("(t p) d -> p t d", p=P), x[:, :, :]).then_inc(s_out, 16)
            sp.wait_ge(s_out, 16)

        def pe_norm(pe, name, before=()):
            n = NORM_NO[name]
            pe.wait_ge(s_xn, 2 * n + 2)
            for sem_, value in before:
                pe.wait_ge(sem_, value)
            for b in range(8):
                if b >= 4:
                    pe.wait_ge(s_hTl, 8 * n + b - 3)
                for i in range(2):
                    for t in range(NT):
                        k = 2 * b + i
                        m = nc.tensor.transpose(aux[b % 4][:, (2 * i + t) * P:(2 * i + t + 1) * P],
                                                xn[:, t, k * P:(k + 1) * P], ident)
                m.then_inc(s_tr, 1)

        def gained(name, b):
            for i in range(2):
                k = 2 * b + i
                yield k, aux[b % 4][:, i * S:(i + 1) * S], par[:, Q[f"g_{name}"].start + k:Q[f"g_{name}"].start + k + 1]

        def act_norm(act, name, src, hT_free):
            n = NORM_NO[name]
            if n:
                act.wait_ge(s_tr, 8 * n)
            nc.scalar.activation(xn[:, 0, :], src[:, 0, :], ACT.Square, accum_out=ss[:, 0:1]).then_inc(s_sq, 1)
            act.wait_ge(s_ms, n + 1)
            nc.scalar.activation(sdv, msq, ACT.Sqrt).then_inc(s_sd, 1)
            act.wait_ge(s_rstd, n + 1)
            nc.scalar.activation(xn[:, 0, :], src[:, 0, :], ACT.Copy, scale=rstd[:, 0:1]).then_inc(s_xn, 1)
            act.wait_ge(s_used, hT_free)
            for b in range(8):
                act.wait_ge(s_tr, 8 * n + b + 1)
                for k, v, gain in gained(name, b):
                    m = nc.scalar.activation(hT_hi[:, k, :], v, ACT.Copy, scale=gain)
                m.then_inc(s_hTh, 1)

        def dve_norm(dve, name, src, hT_free):
            n = NORM_NO[name]
            if n:
                dve.wait_ge(s_tr, 8 * n)
            dve_step(nc.vector.tensor_tensor_reduce(out=xn[:, 1, :], in0=src[:, 1, :], in1=src[:, 1, :], scale=1.0,
                                                    scalar=0.0, op0=MULT, op1=ADD, accum_out=ss[:, 1:2]))
            dve.wait_ge(s_sq, n + 1)
            nc.vector.tensor_scalar(msq, ss, 1.0 / D, RMS_EPS, MULT, ADD).then_inc(s_ms, 1)
            dve.wait_ge(s_sd, n + 1)
            nc.vector.reciprocal(rstd, sdv).then_inc(s_rstd, 1)
            dve.wait_ge(s_rstd, n + 1)
            nc.vector.tensor_scalar(xn[:, 1, :], src[:, 1, :], rstd[:, 1:2], None, MULT).then_inc(s_xn, 1)
            for b in range(8):
                dve.wait_ge(s_hTh, 8 * n + b + 1)
                for k, v, gain in gained(name, b):
                    m = nc.vector.scalar_tensor_tensor(out=hT_lo[:, k, :], in0=v, scalar=gain, in1=f32(hT_hi[:, k, :]),
                                                       op0=MULT, op1=SUB)
                m.then_inc(s_hTl, 1)

        def pe_hT(pe, name):
            n = NORM_NO[name]
            pe.wait_ge(s_hTl, 8 * n + 8)

        mk = W(0, NT, XA_H * P)
        mk_sq = W(1024, NT, XA_H * P)

        def heads8(ap):
            return ap.rearrange("p t (h e) -> p (t h) e", e=P)

        def lanes(ap, n):
            return ap.unsqueeze(2).broadcast_to([P, ap.shape[1], n])

        def hT_tile(k, t):
            return hT_hi[:, k, t * P:(t + 1) * P], hT_lo[:, k, t * P:(t + 1) * P]

        def pe_memory(pe, l):
            pe_hT(pe, f"mem{l}")
            Gemm(pe, f"mem_k{l}").row_chunk(0, hT_tile)
            Gemm(pe, f"mem_v{l}").row_chunk(0, hT_tile)
            pe.wait_ge(s_mk, l + 1)
            for h in range(XA_H):
                for t in range(NT):
                    m = nc.tensor.transpose(aux[h // 2][:, ((h % 2) * NT + t) * P:((h % 2) * NT + t + 1) * P],
                                            mk[:, t, h * P:(h + 1) * P], ident)
                if h % 2:
                    m.then_inc(s_mk_tr, 1)

        def take_row_chunk(act, name, c, dst):
            banks, taken = chunk_banks(name, c)
            hi_upto(act, chunk_done(name, c) + AHEAD)
            act.wait_ge(s_used, chunk_done(name, c))
            for t in range(NT):
                nc.scalar.activation(dst(t), banks[t][:, :], ACT.Copy).then_inc(taken, 1)

        def act_memory(act, l):
            take_row_chunk(act, f"mem_k{l}", 0, lambda t: mk[:, t, :])
            take_row_chunk(act, f"mem_v{l}", 0, lambda t: mem_v[l][:, t, :])
            act.wait_ge(s_mk_ms, l + 1)
            nc.scalar.activation(mk_sd, mk_ms, ACT.Sqrt).then_inc(s_mk_sd, 1)
            for b in range(2):
                act.wait_ge(s_mk_tr, 2 * l + b + 1)
                nc.scalar.activation(mem_kT[l][:, 2 * b:2 * b + 2, :], aux[b][:, :].rearrange("p (h s) -> p h s", s=S),
                                     ACT.Copy).then_inc(s_mkT, 1)

        def dve_memory(dve, l):
            lo_upto(dve, chunk_done(f"mem_k{l}", 0) + AHEAD)
            parity = starts[f"mem_k{l}"][0] % 2
            dve.wait_ge(s_taken[parity], 2 * (starts[f"mem_k{l}"][0] // 2 + 1))
            dve_step(nc.vector.tensor_tensor(mk_sq, mk, mk, MULT))
            dve_step(nc.vector.reduce_sum(mk_ss, heads8(mk_sq), AX_X))
            nc.vector.tensor_scalar(mk_ms, mk_ss, 1.0 / P, RMS_EPS, MULT, ADD).then_inc(s_mk_ms, 1)
            lo_upto(dve, chunk_done(f"mem_v{l}", 0) + AHEAD)
            dve.wait_ge(s_mk_sd, l + 1)
            dve_step(nc.vector.reciprocal(mk_r, mk_sd))
            nc.vector.tensor_tensor(heads8(mk), heads8(mk), lanes(mk_r, P), MULT).then_inc(s_mk, 1)

        xq_sq, xqT = W(0, XA_H, S), W(1024, XA_H, S)
        xp = W(2048, NT, XA_H, S)
        xpT = W(4096, NT, XA_H, S)

        def pe_cross(pe, l):
            pe_hT(pe, f"xattn{l}")
            Gemm(pe, f"xa_q{l}").column_chunk(0)
            pe.wait_ge(s_xq, l + 1)
            for t in range(NT):
                for h in range(XA_H):
                    m = nc.tensor.matmul(aux[0][:, t * XA_H + h:t * XA_H + h + 1],
                                         lhsT=xq_sq[:, h, t * P:(t + 1) * P], rhs=ones_col, start=True, stop=True)
            m.then_inc(s_xss, 1)
            for b in list(range(1, 4)) + [0]:
                t, hp = b // 2, b % 2
                if b == 0:
                    pe.wait_ge(s_xms, l + 1)
                for i in range(2):
                    h = 2 * hp + i
                    m = nc.tensor.matmul(aux[b][:, i * S:(i + 1) * S], lhsT=xqT[:, h, t * P:(t + 1) * P],
                                         rhs=mem_kT[l][:, h, :], start=True, stop=True)
                m.then_inc(s_xlog, 1)
            for n, b in enumerate(XB):
                t, hp = b // 2, b % 2
                pe.wait_ge(s_xp, 4 * l + n + 1)
                for i in range(2):
                    for mt in range(NT):
                        m = nc.tensor.transpose(aux[b][:, (2 * i + mt) * P:(2 * i + mt + 1) * P],
                                                xp[:, t, 2 * hp + i, mt * P:(mt + 1) * P], ident)
                m.then_inc(s_xpt, 1)
            pe.wait_ge(s_xpt_a, 2 * l + 2)
            pe.wait_ge(s_xpt_d, 2 * l + 2)
            for h in range(XA_H):
                for mt in range(NT):
                    m = nc.tensor.matmul(aux[h // 2][:, (h % 2) * S:(h % 2 + 1) * S],
                                         lhsT=mem_v[l][:, mt, h * P:(h + 1) * P], rhs=xpT[:, mt, h, :],
                                         start=mt == 0, stop=mt == NT - 1)
                if h % 2:
                    m.then_inc(s_xo, 1)
            pe.wait_ge(s_xoT, 2 * l + 2)
            for c in range(4):
                Gemm(pe, f"xa_o{l}").row_chunk(c, hT_tile, k_tiles=XA_H)

        XB = [1, 2, 3, 0]

        def pt_out(b):
            t, hp = b // 2, b % 2
            dst = xpT[:, :, 2 * hp:2 * hp + 2, t * P:(t + 1) * P].rearrange("p m i s -> p i m s")
            return dst, aux[b][:, :].rearrange("p (i m s) -> p i m s", i=2, s=P)

        def act_cross(act, l):
            name = f"xa_q{l}"
            banks, taken = chunk_banks(name, 0)
            hi_upto(act, chunk_done(name, 0) + AHEAD)
            act.wait_ge(s_used, chunk_done(name, 0))
            act.wait_ge(s_gqk, 1)
            for b in range(2):
                v = banks[b][:, :].rearrange("p (h s) -> p h s", s=S)
                nc.scalar.activation(xq_sq[:, 2 * b:2 * b + 2, :], v, ACT.Square)
                m = nc.scalar.activation(xqT[:, 2 * b:2 * b + 2, :], v, ACT.Copy, scale=gqk[:, l:l + 1])
                m.then_inc(taken, 1)
            act.wait_ge(taken, 2 * (starts[name][0] // 2 + 1))
            act.sem_inc(s_xq, 1)
            act.wait_ge(s_xms, l + 1)
            nc.scalar.activation(xa_sd, xa_ms, ACT.Sqrt).then_inc(s_xsd, 1)
            for n, b in enumerate(XB):
                t, hp = b // 2, b % 2
                act.wait_ge(s_xnm, 4 * l + n + 1)
                for i in range(2):
                    j = t * XA_H + 2 * hp + i
                    nc.scalar.activation(xp[:, t, 2 * hp + i, :], aux[b][:, i * S:(i + 1) * S], ACT.Exp,
                                         bias=xa_nm[:, j:j + 1], scale=xa_rq[:, j:j + 1],
                                         accum_out=xa_sum[:, j:j + 1]).then_inc(s_xexp, 1)
            for n, b in enumerate(XB):
                if b >= 2:
                    continue
                act.wait_ge(s_xpt, 4 * l + n + 1)
                dst, src = pt_out(b)
                for i in range(2):
                    m = nc.scalar.activation(dst[:, i], src[:, i], ACT.Copy)
                m.then_inc(s_xpt_a, 1)
            for b in range(2):
                act.wait_ge(s_xo, 2 * l + b + 1)
                nc.scalar.activation(hT_hi[:, 2 * b:2 * b + 2, :], aux[b][:, :].rearrange("p (h s) -> p h s", s=S),
                                     ACT.Copy).then_inc(s_xoh, 1)
            for c in range(4):
                hi_upto(act, chunk_done(f"xa_o{l}", c) + AHEAD)

        def dve_cross(dve, l):
            lo_upto(dve, chunk_done(f"xa_q{l}", 0) + AHEAD)
            dve.wait_ge(s_xss, l + 1)
            nc.vector.tensor_scalar(xa_ms, aux[0][:, 0:8], 1.0 / P, RMS_EPS, MULT, ADD).then_inc(s_xms, 1)
            dve.wait_ge(s_xsd, l + 1)
            dve_step(nc.vector.reciprocal(xa_r, xa_sd))
            dve_step(nc.vector.tensor_scalar(xa_rq, xa_r, HEAD_SCALE, None, MULT))
            for n, b in enumerate(XB):
                t, hp = b // 2, b % 2
                j = slice(t * XA_H + 2 * hp, t * XA_H + 2 * hp + 2)
                dve.wait_ge(s_xlog, 4 * l + n + 1)
                dve_step(nc.vector.reduce_max(xa_mx[:, j], aux[b][:, :].rearrange("p (i m) -> p i m", i=2), AX_X))
                nc.vector.scalar_tensor_tensor(out=xa_nm[:, j], in0=xa_mx[:, j], scalar=-1.0, in1=xa_rq[:, j],
                                               op0=MULT, op1=MULT).then_inc(s_xnm, 1)
            for n, b in enumerate(XB):
                t, hp = b // 2, b % 2
                j = slice(t * XA_H + 2 * hp, t * XA_H + 2 * hp + 2)
                dve.wait_ge(s_xexp, 8 * l + 2 * n + 2)
                dve_step(nc.vector.reciprocal(xa_rs[:, j], xa_sum[:, j]))
                pv = xp[:, t, 2 * hp:2 * hp + 2, :]
                nc.vector.tensor_tensor(pv, pv, lanes(xa_rs[:, j], S), MULT).then_inc(s_xp, 1)
            for n, b in enumerate(XB):
                if b < 2:
                    continue
                dve.wait_ge(s_xpt, 4 * l + n + 1)
                dst, src = pt_out(b)
                nc.vector.tensor_copy(dst, src).then_inc(s_xpt_d, 1)
            for b in range(2):
                dve.wait_ge(s_xoh, 2 * l + b + 1)
                nc.vector.tensor_tensor(hT_lo[:, 2 * b:2 * b + 2, :], aux[b][:, :].rearrange("p (h s) -> p h s", s=S),
                                        f32(hT_hi[:, 2 * b:2 * b + 2, :]), SUB).then_inc(s_xoT, 1)
            for c in range(4):
                dve_add_to_x(dve, f"xa_o{l}", c)

        def dve_add_to_x(dve, name, c):
            banks, taken = chunk_banks(name, c)
            lo_upto(dve, chunk_done(name, c) + AHEAD)
            dve.wait_ge(s_used, chunk_done(name, c))
            for t in range(NT):
                cols = x[:, t, c * 512:(c + 1) * 512]
                nc.vector.tensor_tensor(cols, cols, banks[t][:, :], ADD).then_inc(taken, 1)

        relu = W(16384, 2, UNIT)
        usq = W(12288, 4, UNIT)

        def u_tile(k, t):
            return u_hi[:, k, t * P:(t + 1) * P], u_lo[:, k, t * P:(t + 1) * P]

        def pe_ffn(pe, l):
            pe_hT(pe, f"ffn{l}")
            with pe.Fori(0, FF_TURNS) as turn:
                mlp = Gemm(pe, f"ffn{l}", turn)
                for c in range(4):
                    mlp.column_chunk(c)

                def u_ready(k):
                    if k % 4 == 0:
                        pe.wait_ge(s_u, turn * 4 + (4 * FF_TURNS * l + k // 4 + 1))

                for c in range(4, 8):
                    mlp.row_chunk(c, u_tile, k_ready=u_ready if c == 4 else None)

        def split_in_turn(write, eng, l, c, turn, last):
            u0 = starts[f"ffn{l}"][1] + AHEAD + 8 * c
            for u in range(u0, u0 + 8):
                if not last or u + (FF_TURNS - 1) * FF_UNITS < n_units:
                    write(eng, u, turn)

        def act_ffn(act, l):
            name = f"ffn{l}"
            hi_upto(act, starts[name][1] + AHEAD)

            def one_turn(turn, last):
                for c in range(FF_CHUNKS):
                    split_in_turn(write_hi, act, l, c, turn, last)
                    if c >= 4:
                        continue
                    banks, taken = chunk_banks(name, c)
                    g = starts[name][0] + c
                    act.wait_ge(s_used, turn * FF_UNITS + chunk_done(name, c))
                    for b in range(2):
                        nc.scalar.activation(relu[:, c % 2, b * 512:(b + 1) * 512], banks[b][:, :], ACT.Relu).then_inc(taken, 1)
                    act.wait_ge(taken, turn * FF_CHUNKS + (g // 2 + 1) * 2)
                    nc.scalar.activation(usq[:, c], relu[:, c % 2], ACT.Square)
                    nc.scalar.activation(u_hi[:, 4 * c:4 * c + 4, :].rearrange("p k s -> p (k s)"), relu[:, c % 2],
                                         ACT.Square).then_inc(s_uh, 1)

            run_turns(act, l, one_turn)
            next_hi[0] += FF_TURNS * FF_UNITS

        def run_turns(eng, l, one_turn):
            with eng.Fori(0, FF_TURNS - l) as turn:
                one_turn(turn, False)
            if l:
                one_turn(FF_TURNS - 1, True)

        def dve_ffn(dve, l):
            name = f"ffn{l}"
            lo_upto(dve, starts[name][1] + AHEAD)

            def one_turn(turn, last):
                for c in range(FF_CHUNKS):
                    split_in_turn(write_lo, dve, l, c, turn, last)
                    if c < 4:
                        dve.wait_ge(s_uh, turn * 4 + (4 * FF_TURNS * l + c + 1))
                        nc.vector.tensor_tensor(u_lo[:, 4 * c:4 * c + 4, :].rearrange("p k s -> p (k s)"), usq[:, c],
                                                f32(u_hi[:, 4 * c:4 * c + 4, :].rearrange("p k s -> p (k s)")), SUB).then_inc(s_u, 1)
                        continue
                    banks, taken = chunk_banks(name, c)
                    dve.wait_ge(s_used, turn * FF_UNITS + chunk_done(name, c))
                    for t in range(NT):
                        cols = x[:, t, (c - 4) * 512:(c - 3) * 512]
                        nc.vector.tensor_tensor(cols, cols, banks[t][:, :], ADD).then_inc(taken, 1)

            run_turns(dve, l, one_turn)
            next_lo[0] += FF_TURNS * FF_UNITS

        def inv_views(base, nbuf=2):
            T, Tt, Pm = (W(base + 1024 * i, 2, 4, P) for i in range(3))
            MT = [W(base + 3072 + 1024 * i, 2, 4, P) for i in range(nbuf)]
            return T, Tt, Pm, MT

        def side_of(ap, level, right):
            size = 1 << level
            if len(ap.shape) == 3:
                return ap.rearrange("p m (n two s) -> p m n two s", two=2, s=size)[:, :, :, int(right)]
            return ap.rearrange("p (n two s) -> p n two s", two=2, s=size)[:, :, int(right)]

        def level_mask(d, level):
            i = C["level"].start + (d * LEVELS + level) * P
            return const[:, i:i + P].unsqueeze(1).broadcast_to([P, 4, P])

        def pool_inv_mask(pool, group, AT, views, level, d):
            MT = views[3]
            if level >= len(MT):
                pool.wait_ge(iv_p, (group * LEVELS + level - len(MT)) * 2 + d + 1)
                if level == len(MT):
                    pool.wait_ge(iv_t, group * LEVELS * 2 + d + 1)
            nc.gpsimd.tensor_tensor(MT[level % len(MT)][:, d], AT[d], level_mask(d, level), MULT).then_inc(iv_mt, 1)

        def pe_inv(pe, group, views):
            T, Tt, Pm, MT = views
            for level in range(LEVELS):
                for d in range(2):
                    n = (group * LEVELS + level) * 2 + d
                    pe.wait_ge(iv_mt, n + 1)
                    if level:
                        pe.wait_ge(iv_t, n - 2 + 1)
                    for m in range(4):
                        out = aux[d][:, m * P:(m + 1) * P]
                        if level == 0:
                            i = nc.tensor.transpose(out, MT[0][:, d, m], ident)
                        else:
                            i = nc.tensor.matmul(out, lhsT=MT[level % len(MT)][:, d, m], rhs=T[:, d, m],
                                                 start=True, stop=True)
                    i.then_inc(iv_p, 1)
                if level == 0:
                    continue
                for d in range(2):
                    pe.wait_ge(iv_ps, (group * (LEVELS - 1) + level - 1) * 2 + d + 1)
                    for m in range(4):
                        for j, (lhsT, rhs) in enumerate((
                                (Tt[:, d, m], side_of(Pm[:, d, m], level, d == 1)),
                                (Pm[:, d, m], side_of(Tt[:, d, m], level, d == 0)))):
                            if level == LEVELS - 1 and j == 0:
                                continue
                            at = (4 * j + m) * 64
                            out = aux[2 + d][:, at:at + 64].rearrange("p (n s) -> p n s", s=1 << level)
                            i = nc.tensor.matmul(out, lhsT=lhsT, rhs=rhs, start=True, stop=True)
                    i.then_inc(iv_q, 1)

        def act_inv(act, group, views):
            Pm = views[2]
            for level in range(1, LEVELS):
                for d in range(2):
                    act.wait_ge(iv_p, (group * LEVELS + level) * 2 + d + 1)
                    if level > 1:
                        act.wait_ge(iv_q, (group * (LEVELS - 1) + level - 2) * 2 + d + 1)
                    nc.scalar.activation(Pm[:, d], four(aux[d]), ACT.Copy).then_inc(iv_ps, 1)

        def dve_inv(dve, group, views):
            T, Tt, Pm, MT = views
            for level in range(LEVELS):
                for d in range(2):
                    if level == 0:
                        dve.wait_ge(iv_p, group * LEVELS * 2 + d + 1)
                        eye = ident.unsqueeze(1).broadcast_to([P, 4, P])
                        nc.vector.tensor_tensor(Tt[:, d], eye, MT[0][:, d], SUB)
                        i = nc.vector.tensor_tensor(T[:, d], eye, four(aux[d]), SUB)
                    else:
                        dve.wait_ge(iv_q, (group * (LEVELS - 1) + level - 1) * 2 + d + 1)
                        for j, (dst, right) in enumerate(((T, d == 1), (Tt, d == 0))):
                            if level == LEVELS - 1 and j == 0:
                                continue
                            v = side_of(dst[:, d], level, right)
                            got = aux[2 + d][:, j * 256:(j + 1) * 256].rearrange(
                                "p (m n s) -> p m n s", m=4, s=1 << level)
                            i = nc.vector.tensor_tensor(v, v, got, SUB)
                    i.then_inc(iv_t, 1)

        dn_qT, dn_kT = W(0, DN_H, S), W(2048, DN_H, S)
        dn_k, dn_v = W(4096, NT, DN_W), W(6144, NT, DN_W)
        gate = W(8192, NT, DN_W)
        yscT = W(10240, 8, S)
        G = 12288
        stage = [W(G + 1032 * i, 4, S + 2) for i in range(2)]
        conv = [W(G + 2064 + 1024 * i, 4, S) for i in range(2)]
        cgate = W(G + 4112, 4, S)
        dn_vT = W(6144, DN_H, S)
        qk_sq = H(0, 2 * DN_H, S)
        dn_AT = W(G, 2, 4, P)
        dn_inv = inv_views(G + 1024)
        QKT = H(0, 2, 4, P)
        qTg, eg = H(1024, 2, 2, P), H(1536, 2, 2, P)
        Dm, DB = H(2048, 2, 4, P), H(3072, 2, 4, P)
        vb1, vb2 = H(2048, 2, 2, P), H(2560, 2, 2, P)
        kd1, vn1 = H(3072, 2, 2, P), H(3584, 2, 2, P)
        o_tok = H(4096, NT, DN_H, P)
        S1 = H(6144, 2, 2, P)
        vn2 = W(G + 3072, 2, 2, P)
        o_sq = W(G, NT, DN_H, P)
        y_tok = W(G + 2048, NT, DN_H, P)

        def stat(at, n=32):
            return st[:, 128 + at:128 + at + n].rearrange("p (t n) -> p t n", t=NT)

        abv, beta, xb, ax, soft, decay_g = stat(0, 64), stat(64), stat(96), stat(128), stat(160), stat(192)
        ea = st[:, 128 + 224:128 + 240]
        cum, ecum = stat(240, 64), stat(304, 64)
        dn_ms, dn_sd, dn_rn = stat(368), stat(400), stat(432)
        rq = stat(464, 16)
        brk, nbe, kds = stat(480), stat(512), stat(544)
        o_ss, o_ms, o_sd, o_r = (st[:, 128 + 576 + 16 * i:128 + 592 + 16 * i] for i in range(4))
        FIRST = (0, 1)
        N_SC = 6

        def conv_w(name, tile, tap):
            i = Q[name].start + 3 * tile + tap
            return par[:, i:i + 1]

        def per_dir(v, t, d, hp):
            return v[:, t, 8 * d + 2 * hp:8 * d + 2 * hp + 2]

        def pe_even(pe):
            pe_hT(pe, "mix0")
            pe.wait_ge(s_abw, 2)
            for t in range(NT):
                for k in range(KD):
                    cols = slice(32 * k, 32 * k + 32)
                    x_hi, x_lo = hT_tile(k, t)
                    out = aux[0][:, 32 * t:32 * t + 32]
                    nc.tensor.matmul(out, lhsT=x_hi, rhs=ab_hi[:, cols], start=k == 0, stop=False)
                    nc.tensor.matmul(out, lhsT=x_hi, rhs=ab_lo[:, cols], start=False, stop=False)
                    m = nc.tensor.matmul(out, lhsT=x_lo, rhs=ab_hi[:, cols], start=False, stop=k == KD - 1)
            m.then_inc(s_ab, 1)
            with pe.Fori(0, 3) as turn:
                for c in range(2):
                    Gemm(pe, "ev_qkv", turn, (2, 16)).column_chunk(c)
            for c in range(2):
                Gemm(pe, "ev_gate").row_chunk(c, hT_tile)
            for c in range(N_SC):
                Gemm(pe, "ev_sc").column_chunk(c)
            pe.wait_ge(s_silu, 6)
            wait_chunks_taken(pe, after("ev_sc"))
            pe.wait_ge(s_abv, 1)
            for b in range(8):
                for t in range(NT):
                    for i in range(2):
                        src = (dn_kT, dn_vT)[b // 4][:, 2 * (b % 4) + i, t * P:(t + 1) * P]
                        m = nc.tensor.transpose(bank[b][:, (2 * t + i) * P:(2 * t + i + 1) * P], src, ident)
                m.then_inc(s_kvt, 1)
            pe.wait_ge(s_g, 1)
            pe.wait_ge(s_kv_a, 2)
            for t in range(NT):
                for kind, masks_ in enumerate(((1, 3), (2, 0))):
                    for d in range(2):
                        at = t * 32 + kind * 16 + 8 * d
                        m = nc.tensor.matmul(bank[1][:, at:at + 8], lhsT=const_of("causal", masks_[d]),
                                             rhs=decay_g[:, t, 8 * d:8 * d + 8], start=True, stop=True)
            m.then_inc(s_cum, 1)
            pe.wait_ge(s_dsq, 2)
            for t in range(NT):
                for h in range(2 * DN_H):
                    m = nc.tensor.matmul(bank[0][:, 16 * t + h:16 * t + h + 1], lhsT=qk_sq[:, h, t * P:(t + 1) * P],
                                         rhs=ones_col, start=True, stop=True)
            m.then_inc(s_dss, 1)
            pe.wait_ge(s_stats, 1)
            pe.wait_ge(s_kv_a, 4)
            pe.wait_ge(s_kv_d, 4)
            for hp in range(4):
                pe_delta_group(pe, hp)
            pe.wait_ge(s_y, 1)
            for b in range(4):
                for i in range(2):
                    for t in range(NT):
                        m = nc.tensor.transpose(aux[b][:, (2 * i + t) * P:(2 * i + t + 1) * P],
                                                y_tok[:, t, 2 * b + i, :], ident)
                m.then_inc(s_yt, 1)
            pe.wait_ge(s_yT, 5)
            for c in range(4):
                Gemm(pe, "ev_out").row_chunk(c, hT_tile)

        def pe_delta_group(pe, hp):
            T, Tt, Pm, MT = dn_inv
            if hp:
                pe.wait_ge(s_os, hp)
            for d in range(2):
                b = bank[4 * d:4 * d + 4]
                for i in range(2):
                    for t in range(NT):
                        h, cols = 2 * hp + i, slice((2 * i + t) * P, (2 * i + t + 1) * P)
                        tile = slice(t * P, (t + 1) * P)
                        g_col = decay_g[:, t, 8 * d + h:8 * d + h + 1].broadcast_to([P, P])
                        b_col = brk[:, t, 8 * d + h:8 * d + h + 1].broadcast_to([P, P])
                        for bk, lhsT, rhs in ((b[0], g_col, const_of("causal", 2 * d + 1)), (b[1], b_col, ident),
                                              (b[2], dn_kT[:, h, tile], dn_kT[:, h, tile]),
                                              (b[3], dn_kT[:, h, tile], dn_qT[:, h, tile])):
                            m = nc.tensor.matmul(bk[:, cols], lhsT=lhsT, rhs=rhs, start=True, stop=True)
                m.then_inc(s_pre, 1)
            pe.wait_ge(s_eg, 2 * hp + 2)
            pe.wait_ge(s_AT, 2 * hp + 2)
            pe_inv(pe, hp, dn_inv)
            pe.wait_ge(s_vb, hp + 1)
            pe.wait_ge(iv_t, (hp + 1) * LEVELS * 2)
            for d in range(2):
                for i in range(2):
                    m = nc.tensor.matmul(bank[0][:, (2 * d + i) * P:(2 * d + i + 1) * P],
                                         lhsT=Tt[:, d, 2 * i + FIRST[d]], rhs=vb1[:, d, i], start=True, stop=True)
            m.then_inc(s_vn1, 1)
            pe.wait_ge(s_vn1s, hp + 1)
            for d in range(2):
                for i in range(2):
                    m = nc.tensor.matmul(bank[1][:, (2 * d + i) * P:(2 * d + i + 1) * P],
                                         lhsT=kd1[:, d, i], rhs=vn1[:, d, i], start=True, stop=True)
            m.then_inc(s_S, 1)
            pe.wait_ge(s_Ss, hp + 1)
            for d in range(2):
                t2 = 1 - FIRST[d]
                for i in range(2):
                    m = nc.tensor.matmul(bank[2][:, (2 * d + i) * P:(2 * d + i + 1) * P],
                                         lhsT=dn_kT[:, 2 * hp + i, t2 * P:(t2 + 1) * P], rhs=S1[:, d, i],
                                         start=True, stop=True)
            m.then_inc(s_kS, 1)
            pe.wait_ge(s_R, hp + 1)
            for d in range(2):
                for i in range(2):
                    m = nc.tensor.matmul(bank[3][:, (2 * d + i) * P:(2 * d + i + 1) * P],
                                         lhsT=Tt[:, d, 2 * i + 1 - FIRST[d]], rhs=vb2[:, d, i], start=True, stop=True)
            m.then_inc(s_vn2, 1)
            pe.wait_ge(s_vn2s, hp + 1)
            pe.wait_ge(s_qtg, 2 * hp + 2)
            for t in range(NT):
                d1, d2 = (0, 1) if t == 0 else (1, 0)
                for i in range(2):
                    out = bank[0][:, (2 * t + i) * P:(2 * t + i + 1) * P]
                    nc.tensor.matmul(out, lhsT=QKT[:, d1, 2 * i + t], rhs=vn1[:, d1, i], start=True, stop=False)
                    nc.tensor.matmul(out, lhsT=QKT[:, d2, 2 * i + t], rhs=vn2[:, d2, i], start=False, stop=False)
                    m = nc.tensor.matmul(out, lhsT=qTg[:, d2, i], rhs=S1[:, d2, i], start=False, stop=True)
            m.then_inc(s_o, 1)

        def act_even(act):
            nc.scalar.activation(ab_hi[:, :], par[:, Q["ab_w"]], ACT.Copy).then_inc(s_abw, 1)
            act.wait_ge(s_abv, 1)
            nc.scalar.activation(beta, abv[:, :, 0:16], ACT.Sigmoid)
            act.wait_ge(s_ax, 1)
            act_step(nc.scalar.activation(soft, ax, ACT.Exp, scale=-1.0))
            nc.scalar.activation(ea, par[:, Q["a_log"]], ACT.Exp)
            nc.scalar.activation(soft, soft, ACT.Ln, bias=1.0).then_inc(s_sp, 1)

            def silu(c):
                act.wait_ge(s_cv, c + 1)
                dst = (dn_qT, dn_kT, dn_vT)[c // 2][:, 4 * (c % 2):4 * (c % 2) + 4, :]
                nc.scalar.activation(dst, conv[c % 2], ACT.Silu).then_inc(s_silu, 1)

            for c in range(6):
                banks, taken = chunk_banks("ev_qkv", c)
                hi_upto(act, chunk_done("ev_qkv", c) + AHEAD)
                act.wait_ge(s_used, chunk_done("ev_qkv", c))
                if c >= 2:
                    act.wait_ge(s_cv, c - 1)
                for b in range(2):
                    nc.scalar.activation(stage[c % 2][:, 2 * b:2 * b + 2, 1:S + 1],
                                         banks[b][:, :].rearrange("p (h s) -> p h s", s=S), ACT.Copy).then_inc(taken, 1)
                if c:
                    silu(c - 1)
            silu(5)
            for c in range(2):
                banks, taken = chunk_banks("ev_gate", c)
                hi_upto(act, chunk_done("ev_gate", c) + AHEAD)
                act.wait_ge(s_used, chunk_done("ev_gate", c))
                for t in range(NT):
                    nc.scalar.activation(gate[:, t, c * 512:(c + 1) * 512], banks[t][:, :], ACT.Silu).then_inc(taken, 1)
            for half in range(2):
                c = 3 * half
                banks, taken = chunk_banks("ev_sc", c)
                hi_upto(act, chunk_done("ev_sc", c) + AHEAD)
                act.wait_ge(s_used, chunk_done("ev_sc", c))
                if half:
                    wait_chunks_taken(act, starts["ev_sc"][0] + 2)
                for b in range(2):
                    nc.scalar.activation(cgate[:, 2 * b:2 * b + 2, :], banks[b][:, :].rearrange("p (h s) -> p h s", s=S),
                                         ACT.Copy).then_inc(taken, 1)
                for i in (c + 1, c + 2):
                    hi_upto(act, chunk_done("ev_sc", i) + AHEAD)
            act.wait_ge(s_used, chunk_done("ev_sc", 5))
            nc.scalar.activation(qk_sq[:, 0:8, :], dn_qT, ACT.Square).then_inc(s_dsq, 1)
            nc.scalar.activation(qk_sq[:, 8:16, :], dn_kT, ACT.Square).then_inc(s_dsq, 1)
            for b in range(4):
                act.wait_ge(s_kvt, b + 1)
                dst = dn_k.rearrange("p t (h e) -> p t h e", e=P)[:, :, 2 * b:2 * b + 2, :]
                nc.scalar.activation(dst, bank[b][:, :].rearrange("p (t h e) -> p t h e", t=NT, e=P),
                                     ACT.Copy).then_inc(s_kv_a, 1)
            act.wait_ge(s_cumv, 1)
            nc.scalar.activation(ecum, cum, ACT.Exp).then_inc(s_dE, 1)
            act.wait_ge(s_dms, 1)
            nc.scalar.activation(dn_sd, dn_ms, ACT.Sqrt).then_inc(s_dsd, 1)
            for hp in range(4):
                for d in range(2):
                    act.wait_ge(s_diff, 2 * hp + d + 1)
                    nc.scalar.activation(Dm[:, d], Dm[:, d], ACT.Exp).then_inc(s_D, 1)
                    if hp:
                        act.wait_ge(s_qtg, 2 * hp)
                    src = bank[4 * d][:, :].rearrange("p (i t s) -> p i t s", t=NT, s=P)[:, :, 1 - FIRST[d], :]
                    nc.scalar.activation(eg[:, d], src, ACT.Exp).then_inc(s_eg, 1)
                act_inv(act, hp, dn_inv)
                for n, (ready, src, dst, done) in enumerate(((s_vn1, 0, vn1, s_vn1s), (s_S, 1, S1, s_Ss), (s_vn2, 3, vn2, s_vn2s))):
                    act.wait_ge(ready, hp + 1)
                    nc.scalar.activation(dst.rearrange("p d i e -> p (d i) e"), four(bank[src]), ACT.Copy).then_inc(done, 1)
            act.wait_ge(s_oms, 1)
            nc.scalar.activation(o_sd, o_ms, ACT.Sqrt).then_inc(s_osd, 1)
            act.wait_ge(s_o, 4)
            nc.scalar.activation(hT_hi[:, 8:16, :], yscT, ACT.Copy).then_inc(s_ysp, 1)
            for b in range(4):
                act.wait_ge(s_yt, b + 1)
                nc.scalar.activation(hT_hi[:, 2 * b:2 * b + 2, :], aux[b][:, :].rearrange("p (h s) -> p h s", s=S),
                                     ACT.Copy).then_inc(s_ysp, 1)
            for c in range(4):
                hi_upto(act, chunk_done("ev_out", c) + AHEAD)

        def dve_conv(dve, src, dst, name, tile0, done):
            for i in range(4):
                m = nc.vector.tensor_scalar(dst[:, i], src[:, i, 1:S + 1], conv_w(name, tile0 + i, 1), None, MULT)
            dve_step(m)
            for tap, at in ((0, 0), (2, 2)):
                for i in range(4):
                    m = nc.vector.scalar_tensor_tensor(out=dst[:, i], in0=src[:, i, at:at + S],
                                                       scalar=conv_w(name, tile0 + i, tap), in1=dst[:, i],
                                                       op0=MULT, op1=ADD)
                if tap == 0:
                    dve_step(m)
            if done is None:
                dve_step(m)
            else:
                m.then_inc(done, 1)

        def dve_even(dve):
            for s_ in stage:
                nc.vector.memset(s_[:, :, 0:1], 0.0)
                m = nc.vector.memset(s_[:, :, S + 1:S + 2], 0.0)
            dve_step(m)
            dve.wait_ge(s_abw, 1)
            nc.vector.tensor_tensor(ab_lo[:, :], par[:, Q["ab_w"]], f32(ab_hi[:, :]), SUB).then_inc(s_abw, 1)
            dve.wait_ge(s_ab, 1)
            nc.vector.tensor_copy(abv, aux[0][:, 0:64].rearrange("p (t n) -> p t n", t=NT)).then_inc(s_abv, 1)
            dve.wait_ge(s_abv, 1)
            dt = par[:, Q["dt_bias"]].unsqueeze(1).broadcast_to([P, NT, 16])
            dve_step(nc.vector.tensor_tensor(xb, abv[:, :, 16:32], dt, ADD))
            nc.vector.scalar_tensor_tensor(out=ax, in0=xb, scalar=-1.0, in1=xb, op0=MULT, op1=MAX).then_inc(s_ax, 1)
            dve.wait_ge(s_sp, 1)
            dve_step(nc.vector.scalar_tensor_tensor(out=xb, in0=xb, scalar=0.0, in1=soft, op0=MAX, op1=ADD))
            nc.vector.scalar_tensor_tensor(out=decay_g, in0=xb, scalar=-1.0, in1=ea.unsqueeze(1).broadcast_to([P, NT, 16]),
                                           op0=MULT, op1=MULT).then_inc(s_g, 1)
            for c in range(6):
                _, taken = chunk_banks("ev_qkv", c)
                lo_upto(dve, chunk_done("ev_qkv", c) + AHEAD)
                dve.wait_ge(taken, 2 * ((starts["ev_qkv"][0] + c) // 2 + 1))
                if c >= 2:
                    dve.wait_ge(s_silu, c - 1)
                dve_conv(dve, stage[c % 2], conv[c % 2], "dn_conv", 4 * c, s_cv)
            for c in range(2):
                lo_upto(dve, chunk_done("ev_gate", c) + AHEAD)
            wait_chunks_taken(dve, after("ev_gate"))
            gain = par[:, Q["dn_norm"]].unsqueeze(1).broadcast_to([P, NT * DN_H, P])
            gv = gate.rearrange("p t (h e) -> p (t h) e", e=P)
            nc.vector.tensor_tensor(gv, gv, gain, MULT)
            dve.wait_ge(s_silu, 6)
            for half in range(2):
                c = 3 * half + 1
                banks, taken = chunk_banks("ev_sc", c)
                lo_upto(dve, chunk_done("ev_sc", c - 1) + AHEAD)
                lo_upto(dve, chunk_done("ev_sc", c) + AHEAD)
                wait_chunks_taken(dve, starts["ev_sc"][0] + c)
                dve.wait_ge(s_used, chunk_done("ev_sc", c))
                for b in range(2):
                    nc.vector.tensor_tensor(stage[0][:, 2 * b:2 * b + 2, 1:S + 1], cgate[:, 2 * b:2 * b + 2, :],
                                            banks[b][:, :].rearrange("p (h s) -> p h s", s=S), MULT).then_inc(taken, 1)
                dve.wait_ge(taken, 2 * ((starts["ev_sc"][0] + c) // 2 + 1))
                dve_conv(dve, stage[0], conv[0], "sc_conv", 4 * half, None)
                banks, taken = chunk_banks("ev_sc", c + 1)
                lo_upto(dve, chunk_done("ev_sc", c + 1) + AHEAD)
                dve.wait_ge(s_used, chunk_done("ev_sc", c + 1))
                for b in range(2):
                    nc.vector.tensor_tensor(yscT[:, 4 * half + 2 * b:4 * half + 2 * b + 2, :],
                                            conv[0][:, 2 * b:2 * b + 2, :],
                                            banks[b][:, :].rearrange("p (h s) -> p h s", s=S), MULT).then_inc(taken, 1)
            dve.wait_ge(s_kvt, 8)
            for b in range(4):
                dst = dn_v.rearrange("p t (h e) -> p t h e", e=P)[:, :, 2 * b:2 * b + 2, :]
                nc.vector.tensor_copy(dst, bank[4 + b][:, :].rearrange("p (t h e) -> p t h e", t=NT, e=P)).then_inc(s_kv_d, 1)
            dve.wait_ge(s_cum, 1)
            nc.vector.tensor_copy(cum, bank[1][:, 0:64].rearrange("p (t n) -> p t n", t=NT)).then_inc(s_cumv, 1)
            dve.wait_ge(s_dss, 1)
            nc.vector.tensor_scalar(dn_ms, bank[0][:, 0:32].rearrange("p (t n) -> p t n", t=NT), 1e-6, None, ADD).then_inc(s_dms, 1)
            dve.wait_ge(s_dsd, 1)
            dve_step(nc.vector.reciprocal(dn_rn, dn_sd))
            nc.vector.tensor_scalar(rq, dn_rn[:, :, 0:8], HEAD_SCALE, None, MULT)
            rk2 = dn_rn[:, :, 8:16].unsqueeze(2).broadcast_to([P, NT, 2, 8])
            two = lambda v: v.rearrange("p t (d h) -> p t d h", d=2)
            dve_step(nc.vector.tensor_tensor(two(brk), two(beta), rk2, MULT))
            dve.wait_ge(s_dE, 1)
            nc.vector.scalar_tensor_tensor(out=nbe, in0=brk, scalar=-1.0, in1=ecum[:, :, 0:16], op0=MULT, op1=MULT)
            nc.vector.tensor_tensor(two(kds), two(ecum[:, :, 16:32]), rk2, MULT).then_inc(s_stats, 1)
            dve.wait_ge(s_stats, 1)
            for hp in range(4):
                dve_delta_group(dve, hp)
            dve.wait_ge(s_os, 4)
            dve_step(nc.vector.tensor_tensor(o_sq, o_tok, o_tok, MULT))
            dve_step(nc.vector.reduce_sum(o_ss, o_sq.rearrange("p t h e -> p (t h) e"), AX_X))
            nc.vector.tensor_scalar(o_ms, o_ss, 1.0 / P, RMS_EPS, MULT, ADD).then_inc(s_oms, 1)
            dve.wait_ge(s_osd, 1)
            dve_step(nc.vector.reciprocal(o_r, o_sd))
            flat = lambda v: v.rearrange("p t h e -> p (t h) e")
            dve_step(nc.vector.tensor_tensor(flat(y_tok), flat(o_tok), lanes(o_r, P), MULT))
            nc.vector.tensor_tensor(flat(y_tok), flat(y_tok), gv, MULT).then_inc(s_y, 1)
            dve.wait_ge(s_ysp, 1)
            nc.vector.tensor_tensor(hT_lo[:, 8:16, :], yscT, f32(hT_hi[:, 8:16, :]), SUB).then_inc(s_yT, 1)
            for b in range(4):
                dve.wait_ge(s_ysp, b + 2)
                nc.vector.tensor_tensor(hT_lo[:, 2 * b:2 * b + 2, :], aux[b][:, :].rearrange("p (h s) -> p h s", s=S),
                                        f32(hT_hi[:, 2 * b:2 * b + 2, :]), SUB).then_inc(s_yT, 1)
            for c in range(4):
                dve_add_to_x(dve, "ev_out", c)

        def dve_delta_group(dve, hp):
            if hp:
                dve.wait_ge(s_o, hp)
            for d in range(2):
                b = bank[4 * d:4 * d + 4]
                dve.wait_ge(s_pre, 2 * hp + d + 1)
                each = [(2 * i + t, t, 8 * d + 2 * hp + i, 8 + 2 * hp + i) for i in range(2) for t in range(NT)]
                for m, t, j, _ in each:
                    i_ = nc.vector.scalar_tensor_tensor(out=Dm[:, d, m], in0=b[0][:, m * P:(m + 1) * P],
                                                        scalar=cum[:, t, j:j + 1], in1=const_of("neg", d), op0=SUB, op1=ADD)
                i_.then_inc(s_diff, 1)
                dve.wait_ge(s_D, 2 * hp + d + 1)
                dve_step(nc.vector.tensor_tensor(DB[:, d], Dm[:, d], four(b[1]), MULT))
                for m, t, _, kh in each:
                    nc.vector.scalar_tensor_tensor(out=QKT[:, d, m], in0=b[3][:, m * P:(m + 1) * P],
                                                   scalar=dn_rn[:, t, kh:kh + 1], in1=Dm[:, d, m], op0=MULT, op1=MULT)
                for m, t, _, kh in each:
                    i_ = nc.vector.scalar_tensor_tensor(out=dn_AT[:, d, m], in0=b[2][:, m * P:(m + 1) * P],
                                                        scalar=dn_rn[:, t, kh:kh + 1], in1=DB[:, d, m], op0=MULT, op1=MULT)
                i_.then_inc(s_AT, 1)
            dve_inv(dve, hp, dn_inv)
            dve.wait_ge(s_kS, hp + 1)
            dve.wait_ge(s_vb, hp + 1)
            for d in range(2):
                for i in range(2):
                    j = 8 * d + 2 * hp + i
                    m = nc.vector.scalar_tensor_tensor(out=vb2[:, d, i], in0=bank[2][:, (2 * d + i) * P:(2 * d + i + 1) * P],
                                                       scalar=nbe[:, 1 - FIRST[d], j:j + 1], in1=vb2[:, d, i],
                                                       op0=MULT, op1=ADD)
            m.then_inc(s_R, 1)
            dve.wait_ge(s_o, hp + 1)
            for t in range(NT):
                m = nc.vector.tensor_tensor(o_tok[:, t, 2 * hp:2 * hp + 2, :],
                                            bank[0][:, t * 256:(t + 1) * 256].rearrange("p (i e) -> p i e", e=P),
                                            lanes(rq[:, t, 2 * hp:2 * hp + 2], P), MULT)
            m.then_inc(s_os, 1)

        def pool_even(pool):
            views = dn_inv
            pool.wait_ge(s_stats, 1)
            for hp in range(4):
                for d in range(2):
                    pool.wait_ge(s_AT, 2 * hp + d + 1)
                    pool_inv_mask(pool, hp, [dn_AT[:, 0], dn_AT[:, 1]], views, 0, d)
                for d in range(2):
                    pool_inv_mask(pool, hp, [dn_AT[:, 0], dn_AT[:, 1]], views, 1, d)
                for d in range(2):
                    t1, t2 = FIRST[d], 1 - FIRST[d]
                    pool.wait_ge(s_eg, 2 * hp + d + 1)
                    nc.gpsimd.tensor_tensor(qTg[:, d], dn_qT[:, 2 * hp:2 * hp + 2, t2 * P:(t2 + 1) * P], eg[:, d],
                                            MULT).then_inc(s_qtg, 1)
                    for dst, src, t, w in ((vb1, dn_v, t1, beta), (vb2, dn_v, t2, beta), (kd1, dn_k, t1, kds)):
                        v = src[:, t, 2 * hp * P:(2 * hp + 2) * P].rearrange("p (i e) -> p i e", e=P)
                        m = nc.gpsimd.tensor_tensor(dst[:, d], v, lanes(per_dir(w, t, d, hp), P), MULT)
                m.then_inc(s_vb, 1)
                for level in range(2, LEVELS):
                    for d in range(2):
                        pool_inv_mask(pool, hp, [dn_AT[:, 0], dn_AT[:, 1]], views, level, d)

        NB = N_BUCKETS + 1
        btab = W(16384, DSA_G, 512)[0:NB]
        rel = st[0:NB, 112:112 + DSA_H]
        brow = W(2048, DSA_H, 512)

        def pe_bias(pe):
            pe.wait_ge(s_bt_in, 32)
            pe.wait_ge(s_neg, 1)
            for h in range(DSA_H):
                if h >= 4:
                    pe.wait_ge(s_bias_s, h - 3)
                nc.tensor.matmul(aux[h % 4][:, :], lhsT=rel[:, h:h + 1].broadcast_to([NB, P]),
                                 rhs=btab[:, h // DSA_HG, :], start=True, stop=True).then_inc(s_bias_m, 1)

        def act_bias(act):
            act.dma_start(rel[0:N_BUCKETS], rel_bias).then_inc(s_bt_in, 16)
            act.dma_start(btab, bias_table.rearrange("b (g n) -> b g n", g=DSA_G)).then_inc(s_bt_in, 16)
            for h in range(DSA_H):
                act.wait_ge(s_bias_m, h + 1)
                nc.scalar.activation(brow[:, h, :], aux[h % 4][:, :], ACT.Copy).then_inc(s_bias_s, 1)
            act.wait_ge(s_bias_s, DSA_H)
            act.dma_start(bias_rows.rearrange("h p n -> p h n"), brow).then_inc(s_bias_out, 16)

        oq, ok, ov = W(0, DSA_H, S), W(3072, NT, DSA_H * P), W(6144, NT, DSA_H * P)
        oq_sq = W(15120, 2, 4, S)
        ok_sq = W(17168, NT, 512)
        okT = W(13056, DSA_H, S)
        osc = W(16128, 2, DSA_G, S)
        bias, oPT = H(0, NT, DSA_H, S), H(6144, 2, 6, P)
        ycT = mem_kT[0][:, :, :]
        o_sum = lambda i: st[:, 124 + i:125 + i]
        ost = lambda i: st[:, 128 + 24 * i:152 + 24 * i]
        oms, osd, orq0, orq, kss, kms, ksd, krs = (ost(i) for i in range(8))
        omx, onm, osum, ors = (st[:, 320 + 2 * i:322 + 2 * i] for i in range(4))
        gca = st[:, 328:329]
        ITEMS = [(hg, t) for hg in range(DSA_HG) for t in range(NT)]

        def taken_of(eng, name, c):
            g = starts[name][0] + c
            eng.wait_ge(s_taken[g % 2], 2 * (g // 2 + 1))

        def pe_window(pe):
            pe_hT(pe, "mix1")
            q, k, v = (Gemm(pe, n) for n in ("od_q", "od_k", "od_v"))

            def ssq(c):
                taken_of(pe, "od_q", c)
                for t in range(NT):
                    for i in range(4):
                        at = t * DSA_H + 4 * c + i
                        m = nc.tensor.matmul(aux[0][:, at:at + 1], lhsT=oq_sq[:, c % 2, i, t * P:(t + 1) * P],
                                             rhs=ones_col, start=True, stop=True)
                m.then_inc(s_oss, 1)

            q.column_chunk(0)
            q.column_chunk(1)
            ssq(0)
            q.column_chunk(2)
            ssq(1)
            k.row_chunk(0, hT_tile)
            ssq(2)
            k.row_chunk(1, hT_tile)
            k.row_chunk(2, hT_tile)
            for c in range(3):
                v.row_chunk(c, hT_tile)
            rw = Gemm(pe, "od_rw")
            for c in range(4):
                rw.column_chunk(c, tiles=3 if c == 3 else 4)
            pe.wait_ge(s_ok, 1)
            pe.wait_ge(s_oms0, 1)
            for b in range(6):
                if b >= 4:
                    pe.wait_ge((s_okT_a, s_okT_d)[b % 2], (b - 4) // 2 + 1)
                for i in range(2):
                    for t in range(NT):
                        h = 2 * b + i
                        m = nc.tensor.transpose(aux[b % 4][:, (2 * i + t) * P:(2 * i + t + 1) * P],
                                                ok[:, t, h * P:(h + 1) * P], ident)
                m.then_inc(s_okt, 1)
            pe.wait_ge(s_okT_a, 3)
            pe.wait_ge(s_okT_d, 3)
            wait_chunks_taken(pe, after("od_rw"))

            def scores(n):
                hg, t = ITEMS[n]
                p = n % 2
                if n >= 2:
                    pe.wait_ge(s_opt_a, n - 1)
                    pe.wait_ge(s_opt_d, n - 1)
                for g in range(DSA_G):
                    h = g * DSA_HG + hg
                    m = nc.tensor.matmul(aux[2 * p + g // 2][:, (g % 2) * S:(g % 2 + 1) * S],
                                         lhsT=oq[:, h, t * P:(t + 1) * P], rhs=okT[:, h, :], start=True, stop=True)
                m.then_inc(s_ol, 1)

            scores(0)
            for n, (hg, t) in enumerate(ITEMS):
                p = n % 2
                if n + 1 < len(ITEMS):
                    scores(n + 1)
                pe.wait_ge(s_op, n + 1)
                for g in range(DSA_G):
                    for mt in range(NT):
                        j = 2 * g + mt
                        m = nc.tensor.transpose(aux[2 * p + j // 4][:, (j % 4) * P:(j % 4 + 1) * P],
                                                osc[:, p, g, mt * P:(mt + 1) * P], ident)
                m.then_inc(s_opt, 1)
                pe.wait_ge(s_opt_a, n + 1)
                pe.wait_ge(s_opt_d, n + 1)
                if n >= 2:
                    pe.wait_ge(s_oyc, n - 1)
                for g in range(DSA_G):
                    for mt in range(NT):
                        h = g * DSA_HG + hg
                        m = nc.tensor.matmul(bank[p][:, 0:P], lhsT=ov[:, mt, h * P:(h + 1) * P],
                                             rhs=oPT[:, p, 2 * g + mt, :], start=g + mt == 0, stop=g + mt == 3)
                m.then_inc(s_opv, 1)

        def act_window(act):
            act.wait_ge(s_gqk, 2)
            for c in range(3):
                banks, taken = chunk_banks("od_q", c)
                hi_upto(act, chunk_done("od_q", c) + AHEAD)
                act.wait_ge(s_used, chunk_done("od_q", c))
                if c == 2:
                    act.wait_ge(s_oss, 1)
                for b in range(2):
                    v = banks[b][:, :].rearrange("p (h s) -> p h s", s=S)
                    nc.scalar.activation(oq_sq[:, c % 2, 2 * b:2 * b + 2, :], v, ACT.Square)
                    nc.scalar.activation(oq[:, 4 * c + 2 * b:4 * c + 2 * b + 2, :], v, ACT.Copy, scale=gca).then_inc(taken, 1)
            for name, dst in (("od_k", ok), ("od_v", ov)):
                for c in range(3):
                    take_row_chunk(act, name, c, lambda t: dst[:, t, c * 512:(c + 1) * 512])
                    if name == "od_v" and c == 0:
                        act.wait_ge(s_oms0, 2)
                        nc.scalar.activation(osd, oms, ACT.Sqrt)
                        nc.scalar.activation(ksd, kms, ACT.Sqrt).then_inc(s_osd0, 1)
            act.dma_start(ln_wb.rearrange("p a n -> p (a n)"), wide[:, 2560:3584]).then_inc(s_wide, 16)
            act.wait_ge(s_rw, 1)
            for c in range(4):
                banks, taken = chunk_banks("od_rw", c)
                hi_upto(act, chunk_done("od_rw", c) + AHEAD)
                act.wait_ge(s_used, chunk_done("od_rw", c))
                if c >= 2:
                    act.wait_ge(s_rw, c)
                for b in range(2):
                    n = 1 if (c, b) == (3, 1) else 2
                    nc.scalar.activation(rstage[c % 2][:, 2 * b:2 * b + n, 1:S + 1],
                                         banks[b][:, 0:n * S].rearrange("p (h s) -> p h s", s=S), ACT.Copy).then_inc(taken, 1)
            for t in range(NT):
                src = bass.AP(bias_rows.tensor, S - 1 - P * t, [[511, P], [P * 512, DSA_H], [1, S]])
                act.dma_start(bias[:, t], src).then_inc(s_bias_in, 16)
            act.wait_ge(s_rw, 5)
            nc.scalar.activation(wagT[:, 0, :], wagT[:, 0, :], ACT.Tanh)
            nc.scalar.activation(wagT[:, 2, :], wagT[:, 2, :], ACT.Sigmoid).then_inc(s_rtanh, 1)
            for b in range(0, 6, 2):
                act.wait_ge(s_okt, b + 1)
                nc.scalar.activation(okT[:, 2 * b:2 * b + 2, :], aux[b % 4][:, :].rearrange("p (h s) -> p h s", s=S),
                                     ACT.Copy).then_inc(s_okT_a, 1)
            def exps(n):
                p = n % 2
                act.wait_ge(s_onm, n + 1)
                v = osc[:, p].rearrange("p g m -> p (g m)")
                nc.scalar.activation(v, v, ACT.Exp, bias=onm[:, p:p + 1], accum_out=osum[:, p:p + 1]).then_inc(s_oexp, 1)

            exps(0)
            for n, (hg, t) in enumerate(ITEMS):
                p = n % 2
                if n + 1 < len(ITEMS):
                    exps(n + 1)
                act.wait_ge(s_opt, n + 1)
                nc.scalar.activation(oPT[:, p, 0:4, :], four(aux[2 * p]), ACT.Copy).then_inc(s_opt_a, 1)
                act.wait_ge(s_opv, n + 1)
                nc.scalar.activation(ycT[:, hg, t * P:(t + 1) * P], bank[p][:, 0:P], ACT.Copy).then_inc(s_oyc, 1)

        def dve_window(dve):
            nc.vector.tensor_tensor(gca, par[:, Q["ca_qn"]], par[:, Q["ca_kn"]], MULT).then_inc(s_gqk, 1)
            nc.vector.tensor_scalar(mid_w, par[:, Q["rw_mu"]], -1.0, 1.0, MULT, ADD)
            nc.vector.tensor_scalar(side_w, par[:, Q["rw_mu"]], 0.5, None, MULT)
            nc.vector.tensor_scalar(one_ka, par[:, Q["rw_ka"]], -1.0, 1.0, MULT, ADD)
            for s_ in rstage:
                nc.vector.memset(s_[:, :, 0:1], 0.0)
                m = nc.vector.memset(s_[:, :, S + 1:S + 2], 0.0)
            m.then_inc(s_rw, 1)
            for c in range(3):
                lo_upto(dve, chunk_done("od_q", c) + AHEAD)
            for c in range(3):
                lo_upto(dve, chunk_done("od_k", c) + AHEAD)
                taken_of(dve, "od_k", c)
                dve_step(nc.vector.tensor_tensor(ok_sq, ok[:, :, c * 512:(c + 1) * 512], ok[:, :, c * 512:(c + 1) * 512], MULT))
                for t in range(NT):
                    m = nc.vector.reduce_sum(kss[:, t * DSA_H + 4 * c:t * DSA_H + 4 * c + 4],
                                             ok_sq[:, t, :].rearrange("p (h e) -> p h e", e=P), AX_X)
                dve_step(m)
            dve.wait_ge(s_oss, 3)
            nc.vector.tensor_scalar(oms, aux[0][:, 0:24], 1.0 / P, RMS_EPS, MULT, ADD).then_inc(s_oms0, 1)
            nc.vector.tensor_scalar(kms, kss, 1.0 / P, RMS_EPS, MULT, ADD).then_inc(s_oms0, 1)
            lo_upto(dve, chunk_done("od_v", 0) + AHEAD)
            dve.wait_ge(s_osd0, 1)
            dve_step(nc.vector.reciprocal(orq0, osd))
            dve_step(nc.vector.tensor_scalar(orq, orq0, HEAD_SCALE, None, MULT))
            dve_step(nc.vector.reciprocal(krs, ksd))
            kv = ok.rearrange("p t (h e) -> p (t h) e", e=P)
            nc.vector.tensor_tensor(kv, kv, lanes(krs, P), MULT).then_inc(s_ok, 1)
            for c in range(1, 3):
                lo_upto(dve, chunk_done("od_v", c) + AHEAD)
            dve.wait_ge(s_rw, 1)
            for c, dst in enumerate((rT, krT, vrT, wagT)):
                lo_upto(dve, chunk_done("od_rw", c) + AHEAD)
                taken_of(dve, "od_rw", c)
                dve_shift(dve, rstage[c % 2], dst, 4 * c, 3 if c == 3 else 4)
            dve.wait_ge(s_rw, 5)
            for b in range(1, 6, 2):
                dve.wait_ge(s_okt, b + 1)
                nc.vector.tensor_copy(okT[:, 2 * b:2 * b + 2, :], aux[b % 4][:, :].rearrange("p (h s) -> p h s", s=S)).then_inc(s_okT_d, 1)
            dve.wait_ge(s_bias_in, 32)

            def scores(n):
                hg, t = ITEMS[n]
                p = n % 2
                dve.wait_ge(s_ol, n + 1)
                if n >= 2:
                    dve.wait_ge(s_opt, n - 1)
                for g in range(DSA_G):
                    h = g * DSA_HG + hg
                    m = nc.vector.scalar_tensor_tensor(out=osc[:, p, g, :], in0=aux[2 * p + g // 2][:, (g % 2) * S:(g % 2 + 1) * S],
                                                       scalar=orq[:, t * DSA_H + h:t * DSA_H + h + 1], in1=bias[:, t, h, :],
                                                       op0=MULT, op1=ADD)
                dve_step(m)
                dve_step(nc.vector.reduce_max(omx[:, p:p + 1], osc[:, p].rearrange("p g m -> p (g m)"), AX_X))
                nc.vector.tensor_scalar(onm[:, p:p + 1], omx[:, p:p + 1], -1.0, None, MULT).then_inc(s_onm, 1)

            scores(0)
            for n, (hg, t) in enumerate(ITEMS):
                p = n % 2
                if n + 1 < len(ITEMS):
                    scores(n + 1)
                dve.wait_ge(s_oexp, n + 1)
                dve_step(nc.vector.reciprocal(ors[:, p:p + 1], osum[:, p:p + 1]))
                v = osc[:, p].rearrange("p g m -> p (g m)")
                nc.vector.tensor_scalar(v, v, ors[:, p:p + 1], None, MULT).then_inc(s_op, 1)
                dve.wait_ge(s_opt, n + 1)
                nc.vector.tensor_copy(oPT[:, p, 4:6, :], aux[2 * p + 1][:, 0:256].rearrange("p (m s) -> p m s", s=P)).then_inc(s_opt_d, 1)

        rT, krT, vrT, wagT = W(9216, RW_F, S), W(10240, RW_F, S), W(11264, RW_F, S), W(12288, 3, S)
        rstage = [W(13056 + 1032 * i, 4, S + 2) for i in range(2)]
        ln_wb = W(17664, 2, RW_W)
        kkT, rv, lw, gout = W(0, RW_F, S), W(1024, NT, RW_W), W(2048, NT, 2, RW_W), W(4096, NT, RW_W)
        kdT, aT = W(5120, 2, RW_F, S), W(7168, 2, RW_F, S)
        wide_w = W(13056, 2560)
        w2, a2, g2, w0 = (wide_w[:, WD[n]] for n in ("w2", "a2", "g2", "w0"))
        rtmp, rpr = W(15616, RW_F, S), W(16640, RW_F, S)
        rtmp2 = W(11264, RW_F, S)
        rw_inv = inv_views(10240)
        Z1, U1, Z2, U2 = (W(15360 + 256 * i, 2, 2, RW_N) for i in range(4))
        SD = W(16384, 2, P)
        Fx, RA = H(0, 2, NT, 3, P), H(1536, 2, NT, 2, P)
        btl, ktl = H(2560, 2, NT, P), H(3072, 2, NT, P)
        BK = H(3584, 2, 2, P)
        MAT = H(4096, 2, 4, 4, P)
        Ytok = mem_v[0]
        mid_w, side_w = st[:, 336:351], st[:, 352:367]
        one_ka = st[:, 368:372]
        bon = st[:, 376:392].rearrange("p (t h) -> p t h", t=NT)
        sc0, scl = st[:, 392:394], st[:, 394:396]
        gsum, gmean, gvar, gms, gsd, grs = (st[:, 400 + 16 * i:416 + 16 * i] for i in range(6))

        def f_cols(v, f):
            return v[:, f, :].rearrange("p (t s) -> p t s", s=P)

        def pe_rwkv(pe):
            pe.wait_ge(s_oyc, len(ITEMS))
            pe.wait_ge(s_wide, 32)
            pe.wait_ge(s_rtanh, 1)
            for d in range(2):
                for t in range(NT):
                    nc.tensor.matmul(bank[2 * d + t][:, :], lhsT=wagT[64 * d:64 * d + 64, 0, t * P:(t + 1) * P],
                                     rhs=w2[64 * d:64 * d + 64, :], start=True, stop=True).then_inc(s_rwm, 1)
            for t in range(NT):
                nc.tensor.matmul(bank[4 + t][:, :], lhsT=wagT[:, 2, t * P:(t + 1) * P], rhs=g2,
                                 start=True, stop=True).then_inc(s_rgm, 1)
            for b in range(2):
                for t in range(NT):
                    for i in range(2):
                        m = nc.tensor.transpose(bank[6 + b][:, (2 * t + i) * P:(2 * t + i + 1) * P],
                                                vrT[:, 2 * b + i, t * P:(t + 1) * P], ident)
                m.then_inc(s_rvt, 1)
            for d in range(2):
                for fp in range(2):
                    pe.wait_ge(s_rlw0, 2 * d + fp + 1)
                    for i in range(2):
                        f = 2 * fp + i
                        m = nc.tensor.matmul(bank[2 * d + fp][:, i * S:(i + 1) * S],
                                             lhsT=a2[64 * d:64 * d + 64, f * P:(f + 1) * P],
                                             rhs=wagT[64 * d:64 * d + 64, 1, :], start=True, stop=True)
                    m.then_inc(s_ram, 1)
            pe.wait_ge(s_kksq, 1)
            pe.wait_ge(s_rgs, 2)
            for b in range(2):
                for i in range(2):
                    m = nc.tensor.matmul(bank[4 + b][:, i * S:(i + 1) * S], lhsT=const[:, C["halves"]],
                                         rhs=rtmp[:, 2 * b + i, :], start=True, stop=True)
                m.then_inc(s_kkm, 1)
            pe.wait_ge(s_pr, 1)
            pe.wait_ge(s_rv, 2)
            for t in range(NT):
                for f in range(RW_F):
                    m = nc.tensor.matmul(bank[6][:, t * RW_H + 2 * f:t * RW_H + 2 * f + 2],
                                         lhsT=rpr[:, f, t * P:(t + 1) * P], rhs=const[:, C["half_cols"]],
                                         start=True, stop=True)
            m.then_inc(s_prm, 1)
            pe.wait_ge(s_lw, 1)
            pe.wait_ge(s_ra, 8)
            pe.wait_ge(s_kkms, 1)
            pe.wait_ge(s_bon, 1)
            for f in range(RW_F):
                pe_rwkv_group(pe, f)
            pe.wait_ge(s_ry, 1)
            for b in range(2):
                for i in range(2):
                    for t in range(NT):
                        m = nc.tensor.transpose(aux[b][:, (2 * i + t) * P:(2 * i + t + 1) * P],
                                                Ytok[:, t, (2 * b + i) * P:(2 * b + i + 1) * P], ident)
                m.then_inc(s_ryt, 1)
            pe.wait_ge(s_yT, 8)
            for c in range(4):
                Gemm(pe, "od_out").row_chunk(c, hT_tile, k_tiles=8)

        def pe_rwkv_group(pe, f):
            T, Tt, Pm, MT = rw_inv
            tile = lambda t: slice(t * P, (t + 1) * P)
            if f:
                pe.wait_ge(s_os, f + 4)
            for d in range(2):
                i0 = C["cum_mid"].start + 256 * d
                for t in range(NT):
                    m = nc.tensor.matmul(bank[d][:, t * S:(t + 1) * S], lhsT=lw[:, t, d, f * P:(f + 1) * P],
                                         rhs=const[:, i0:i0 + 256], start=True, stop=True)
                m.then_inc(s_rc, 1)
            for d in range(2):
                pe.wait_ge(s_rRA, 2 * f + d + 1)
                pe.wait_ge(s_rbk, 2 * f + d + 1)
                if d == 1:
                    pe.wait_ge(s_rF, 2 * f + 2)
                for i in range(2):
                    for t in range(NT):
                        m_ = 2 * i + t
                        bk = bank[(4 + m_) if d == 0 else m_]
                        rows = slice(64 * i, 64 * i + 64)
                        for j, lhs in enumerate((btl, ktl)):
                            m = nc.tensor.matmul(bk[:, j * 256:(j + 1) * 256], lhsT=lhs[rows, d, t, :],
                                                 rhs=RA[rows, d, t].rearrange("p k s -> p (k s)"), start=True, stop=True)
                        m.then_inc(s_rM, 1)
            pe.wait_ge(s_rMAT, 8 * f + 8)
            for d in range(2):
                for j, src in enumerate((btl, ktl)):
                    m = nc.tensor.transpose(bank[2][:, (2 * d + j) * P:(2 * d + j + 1) * P], src[:, d, FIRST_T[d], :], ident)
            m.then_inc(s_rbt, 1)
            for d in range(2):
                for i in range(2):
                    t1 = FIRST_T[d]
                    h = 2 * f + i
                    m = nc.tensor.matmul(bank[3][:, (2 * d + i) * RW_N:(2 * d + i + 1) * RW_N],
                                         lhsT=MAT[:, d, 2 * i + t1, 2], rhs=rv[:, t1, h * RW_N:(h + 1) * RW_N],
                                         start=True, stop=True)
            m.then_inc(s_rz1, 1)
            pe_inv(pe, 4 + f, rw_inv)
            pe.wait_ge(iv_t, (5 + f) * LEVELS * 2)
            pe.wait_ge(s_rz1s, f + 1)
            for d in range(2):
                for i in range(2):
                    m = nc.tensor.matmul(bank[3][:, (2 * d + i) * RW_N:(2 * d + i + 1) * RW_N],
                                         lhsT=Tt[:, d, 2 * i + FIRST_T[d]], rhs=Z1[:, d, i], start=True, stop=True)
            m.then_inc(s_vn1, 1)
            pe.wait_ge(s_rBK, f + 1)
            pe.wait_ge(s_vn1s, f + 5)
            for d in range(2):
                out = bank[2][:, d * P:(d + 1) * P]
                nc.tensor.matmul(out, lhsT=BK[:, d, 1], rhs=rv[:, FIRST_T[d], f * P:(f + 1) * P], start=True, stop=False)
                m = nc.tensor.matmul(out, lhsT=BK[:, d, 0], rhs=U1[:, d].rearrange("p i e -> p (i e)"), start=False, stop=True)
            m.then_inc(s_S, 1)
            pe.wait_ge(s_Ss, f + 5)
            for d in range(2):
                t2 = 1 - FIRST_T[d]
                nc.tensor.matmul(bank[3][:, d * P:(d + 1) * P], lhsT=RA[:, d, t2, 0], rhs=SD[:, d], start=True, stop=False)
                for i in range(2):
                    h = 2 * f + i
                    m = nc.tensor.matmul(bank[3][:, (2 * d + i) * RW_N:(2 * d + i + 1) * RW_N],
                                         lhsT=MAT[:, d, 2 * i + t2, 2], rhs=rv[:, t2, h * RW_N:(h + 1) * RW_N],
                                         start=False, stop=i == 1)
            m.then_inc(s_kS, 1)
            pe.wait_ge(s_R, f + 5)
            for d in range(2):
                for i in range(2):
                    m = nc.tensor.matmul(bank[2][:, (2 * d + i) * RW_N:(2 * d + i + 1) * RW_N],
                                         lhsT=Tt[:, d, 2 * i + 1 - FIRST_T[d]], rhs=Z2[:, d, i], start=True, stop=True)
            m.then_inc(s_vn2, 1)
            pe.wait_ge(s_vn2s, f + 5)
            for t in range(NT):
                d2 = 1 if t == 0 else 0
                nc.tensor.matmul(bank[0][:, t * P:(t + 1) * P], lhsT=RA[:, d2, t, 1], rhs=SD[:, d2], start=True, stop=False)
                for d in range(2):
                    U = U1 if t == FIRST_T[d] else U2
                    for i in range(2):
                        h = 2 * f + i
                        out = bank[0][:, t * P + i * RW_N:t * P + (i + 1) * RW_N]
                        nc.tensor.matmul(out, lhsT=MAT[:, d, 2 * i + t, 3], rhs=rv[:, t, h * RW_N:(h + 1) * RW_N],
                                         start=False, stop=False)
                        m = nc.tensor.matmul(out, lhsT=MAT[:, d, 2 * i + t, 1], rhs=U[:, d, i], start=False,
                                             stop=d == 1 and i == 1)
            m.then_inc(s_o, 1)

        FIRST_T = (0, 1)

        def act_rwkv(act):
            act.dma_start(wide_w, wide[:, 0:2560]).then_inc(s_wide, 16)
            act.wait_ge(s_kk0, 1)
            nc.scalar.activation(rtmp, kkT, ACT.Square).then_inc(s_kksq, 1)
            for t in range(NT):
                act.wait_ge(s_rgm, t + 1)
                nc.scalar.activation(gout[:, t, :], bank[4 + t][:, :], ACT.Copy).then_inc(s_rgs, 1)
            act.wait_ge(s_rlw0, 4)
            nc.scalar.activation(lw, lw, ACT.Sigmoid).then_inc(s_lw, 1)
            for d in range(2):
                for fp in range(2):
                    act.wait_ge(s_ram, 2 * d + fp + 1)
                    for i in range(2):
                        f = 2 * fp + i
                        j = Q["rw_a0"].start + 4 * d + f
                        nc.scalar.activation(aT[:, d, f, :], bank[2 * d + fp][:, i * S:(i + 1) * S], ACT.Sigmoid,
                                             bias=par[:, j:j + 1]).then_inc(s_ra, 1)
            act.wait_ge(s_kkms, 1)
            nc.scalar.activation(rtmp, rtmp2, ACT.Sqrt).then_inc(s_kksd, 1)
            for f in range(RW_F):
                for d in range(2):
                    act.wait_ge(s_rc, 2 * f + d + 1)
                    v = bank[d][:, :].rearrange("p (t k s) -> p t k s", t=NT, k=2)
                    nc.scalar.activation(Fx[:, d, :, 0:2, :], v, ACT.Exp, scale=-KAPPA)
                    nc.scalar.activation(Fx[:, d, :, 2, :], v[:, :, 0, :], ACT.Exp, scale=KAPPA).then_inc(s_rF, 1)
                act.wait_ge(s_rbt, f + 1)
                nc.scalar.activation(BK.rearrange("p d k c -> p (d k) c"), four(bank[2]), ACT.Copy).then_inc(s_rBK, 1)
                act.wait_ge(s_rz1, f + 1)
                c4 = lambda v: v.rearrange("p d i e -> p (d i e)")
                nc.scalar.activation(c4(Z1), bank[3][:, 0:256], ACT.Copy).then_inc(s_rz1s, 1)
                act_inv(act, 4 + f, rw_inv)
                for ready, src, dst, scale, done in ((s_vn1, 3, U1, -1.0, s_vn1s), (s_kS, 3, Z2, 1.0, s_R),
                                                     (s_vn2, 2, U2, -1.0, s_vn2s)):
                    act.wait_ge(ready, f + 5)
                    nc.scalar.activation(c4(dst), bank[src][:, 0:256], ACT.Copy, scale=scale).then_inc(done, 1)
            act.wait_ge(s_o, 4 + RW_F)
            nc.scalar.activation(hT_hi[:, 0:4, :], ycT, ACT.Copy).then_inc(s_ysp, 1)
            act.wait_ge(s_gms, 1)
            nc.scalar.activation(gsd, gms, ACT.Sqrt).then_inc(s_gsd, 1)
            for b in range(2):
                act.wait_ge(s_ryt, b + 1)
                nc.scalar.activation(hT_hi[:, 4 + 2 * b:6 + 2 * b, :], aux[b][:, :].rearrange("p (h s) -> p h s", s=S),
                                     ACT.Copy).then_inc(s_ysp, 1)
            for c in range(4):
                hi_upto(act, chunk_done("od_out", c) + AHEAD)

        def dve_shift(dve, src, dst, tile0, n):
            for i in range(n):
                m = nc.vector.tensor_scalar(dst[:, i], src[:, i, 1:S + 1], mid_w[:, tile0 + i:tile0 + i + 1], None, MULT)
            dve_step(m)
            for at in (0, 2):
                for i in range(n):
                    m = nc.vector.scalar_tensor_tensor(out=dst[:, i], in0=src[:, i, at:at + S],
                                                       scalar=side_w[:, tile0 + i:tile0 + i + 1], in1=dst[:, i],
                                                       op0=MULT, op1=ADD)
                if at == 0:
                    dve_step(m)
            m.then_inc(s_rw, 1)

        def dve_rwkv(dve):
            dve.wait_ge(s_oyc, len(ITEMS))
            for f in range(RW_F):
                j = Q["rw_kk"].start + f
                m = nc.vector.tensor_scalar(kkT[:, f, :], krT[:, f, :], par[:, j:j + 1], None, MULT)
            m.then_inc(s_kk0, 1)
            w0v = w0.rearrange("p (d n) -> p d n", d=2)
            for d in range(2):
                for t in range(NT):
                    dve.wait_ge(s_rwm, 2 * d + t + 1)
                    nc.vector.tensor_tensor(lw[:, t, d, :], bank[2 * d + t][:, :], w0v[:, d], ADD).then_inc(s_rlw0, 1)
            for b in range(2):
                dve.wait_ge(s_rvt, b + 1)
                nc.vector.tensor_copy(rv[:, :, 2 * b * P:(2 * b + 2) * P],
                                      bank[6 + b][:, :].rearrange("p (t n) -> p t n", t=NT)).then_inc(s_rv, 1)
            for b in range(2):
                dve.wait_ge(s_kkm, b + 1)
                m = nc.vector.tensor_scalar(rtmp2[:, 2 * b:2 * b + 2, :], bank[4 + b][:, :].rearrange("p (h s) -> p h s", s=S),
                                            1e-6, None, ADD)
            m.then_inc(s_kkms, 1)
            for d in range(2):
                for f in range(RW_F):
                    dve.wait_ge(s_ra, 4 * d + f + 1)
                    j = Q["rw_ka"].start + f
                    m = nc.vector.tensor_scalar(kdT[:, d, f, :], aT[:, d, f, :], par[:, j:j + 1], one_ka[:, f:f + 1], MULT, ADD)
                dve_step(m)
                m = nc.vector.tensor_tensor(kdT[:, d], kdT[:, d], krT, MULT)
            m.then_inc(s_kd, 1)
            dve.wait_ge(s_kksd, 1)
            dve_step(nc.vector.reciprocal(rtmp2, rtmp))
            nc.vector.tensor_tensor(kkT, kkT, rtmp2, MULT).then_inc(s_kk, 1)
            dve.wait_ge(s_kd, 1)
            dve_step(nc.vector.tensor_tensor(rpr, kdT[:, 0], kdT[:, 1], ADD))
            for f in range(RW_F):
                j = Q["rw_rk"].start + f
                m = nc.vector.scalar_tensor_tensor(out=rpr[:, f, :], in0=rpr[:, f, :], scalar=par[:, j:j + 1],
                                                   in1=rT[:, f, :], op0=MULT, op1=MULT)
            m.then_inc(s_pr, 1)
            dve.wait_ge(s_prm, 1)
            nc.vector.tensor_copy(bon, bank[6][:, 0:16].rearrange("p (t h) -> p t h", t=NT)).then_inc(s_bon, 1)
            dve.wait_ge(s_kk, 1)
            for f in range(RW_F):
                dve_rwkv_group(dve, f)
            dve.wait_ge(s_os, RW_F + 4)
            y16 = Ytok[:, :, :].rearrange("p t (h e) -> p (t h) e", e=RW_N)
            z = W(10240, NT, RW_W)
            z16 = z.rearrange("p t (h e) -> p (t h) e", e=RW_N)
            dve_step(nc.vector.reduce_sum(gsum, y16, AX_X))
            dve_step(nc.vector.tensor_scalar(gmean, gsum, 1.0 / RW_N, None, MULT))
            dve_step(nc.vector.tensor_tensor(y16, y16, lanes(gmean, RW_N), SUB))
            dve_step(nc.vector.tensor_tensor(z16, y16, y16, MULT))
            dve_step(nc.vector.reduce_sum(gvar, z16, AX_X))
            nc.vector.tensor_scalar(gms, gvar, 1.0 / RW_N, GN_EPS, MULT, ADD).then_inc(s_gms, 1)
            dve_step(nc.vector.tensor_tensor(z16, rv.rearrange("p t (h e) -> p (t h) e", e=RW_N),
                                             lanes(bon.rearrange("p t h -> p (t h)"), RW_N), MULT))
            dve.wait_ge(s_ysp, 6)
            nc.vector.tensor_tensor(hT_lo[:, 0:4, :], ycT, f32(hT_hi[:, 0:4, :]), SUB).then_inc(s_yT, 1)
            dve.wait_ge(s_gsd, 1)
            dve_step(nc.vector.reciprocal(grs, gsd))
            dve_step(nc.vector.tensor_tensor(y16, y16, lanes(grs, RW_N), MULT))
            row = lambda j: ln_wb[:, j].unsqueeze(1).broadcast_to([P, NT, RW_W])
            dve_step(nc.vector.tensor_tensor(Ytok[:, :, :], Ytok[:, :, :], row(0), MULT))
            dve_step(nc.vector.tensor_tensor(Ytok[:, :, :], Ytok[:, :, :], row(1), ADD))
            dve_step(nc.vector.tensor_tensor(Ytok[:, :, :], Ytok[:, :, :], z, ADD))
            nc.vector.tensor_tensor(Ytok[:, :, :], Ytok[:, :, :], gout, MULT).then_inc(s_ry, 1)
            for b in range(2):
                dve.wait_ge(s_ysp, b + 7)
                nc.vector.tensor_tensor(hT_lo[:, 4 + 2 * b:6 + 2 * b, :], aux[b][:, :].rearrange("p (h s) -> p h s", s=S),
                                        f32(hT_hi[:, 4 + 2 * b:6 + 2 * b, :]), SUB).then_inc(s_yT, 1)
            for c in range(4):
                dve_add_to_x(dve, "od_out", c)

        def dve_rwkv_group(dve, f):
            for d in range(2):
                dve.wait_ge(s_rF, 2 * f + d + 1)
                nc.vector.tensor_tensor(RA[:, d, :, 0, :], f_cols(kkT, f), Fx[:, d, :, 1, :], MULT)
                nc.vector.tensor_tensor(RA[:, d, :, 1, :], f_cols(rT, f), Fx[:, d, :, 0, :], MULT).then_inc(s_rRA, 1)
            for d in range(2):
                t1, last, first = FIRST_T[d], (P - 1, 0)[d], (0, P - 1)[d]
                dve_step(nc.vector.reciprocal(sc0[:, d:d + 1], Fx[:, d, 1 - t1, 1, first:first + 1]))
                m = nc.vector.tensor_tensor(scl[:, d:d + 1], sc0[:, d:d + 1], Fx[:, d, t1, 0, last:last + 1], MULT)
            dve_step(m)
            for d in range(2):
                for m_ in range(4):
                    n = 4 * d + m_
                    dve.wait_ge(s_rM, 8 * f + n + 1)
                    bk = bank[(4 + m_) if d == 0 else m_]
                    i0 = C["causal"].start + 256 * d
                    mask = const[:, i0:i0 + 256].unsqueeze(1).broadcast_to([P, 2, 256])
                    nc.vector.tensor_tensor(MAT[:, d, m_].rearrange("p (two k) s -> p two (k s)", two=2),
                                            bk[:, :].rearrange("p (two k) -> p two k", two=2), mask, MULT).then_inc(s_rMAT, 1)
            dve_inv(dve, 4 + f, rw_inv)
            dve.wait_ge(s_S, f + 5)
            for d in range(2):
                m = nc.vector.scalar_tensor_tensor(out=SD[:, d], in0=bank[2][:, d * P:(d + 1) * P], scalar=scl[:, d:d + 1],
                                                   in1=const[:, C["halves"]], op0=MULT, op1=MULT)
            m.then_inc(s_Ss, 1)
            dve.wait_ge(s_o, f + 5)
            nc.vector.tensor_copy(Ytok[:, :, f * P:(f + 1) * P],
                                  bank[0][:, 0:256].rearrange("p (t n) -> p t n", t=NT)).then_inc(s_os, 1)

        def pool_odd(pool):
            pool.wait_ge(s_kk, 1)
            pool.wait_ge(s_kd, 1)
            for d in range(2):
                m = nc.gpsimd.tensor_tensor(aT[:, d], aT[:, d], kkT, MULT)
            pool_step(m)
            for f in range(RW_F):
                for d in range(2):
                    pool.wait_ge(s_rF, 2 * f + d + 1)
                    nc.gpsimd.tensor_tensor(btl[:, d], f_cols(aT[:, d], f), Fx[:, d, :, 2, :], MULT)
                    nc.gpsimd.tensor_tensor(ktl[:, d], f_cols(kdT[:, d], f), Fx[:, d, :, 2, :], MULT).then_inc(s_rbk, 1)
                AT = [MAT[:, d, :, 0, :] for d in range(2)]
                for level in range(LEVELS):
                    for d in range(2):
                        if level == 0:
                            pool.wait_ge(s_rMAT, 8 * f + 4 * d + 4)
                        pool_inv_mask(pool, 4 + f, AT, rw_inv, level, d)

        def pe_odd(pe):
            pe_window(pe)
            pe_rwkv(pe)

        def act_odd(act):
            act_window(act)
            act_rwkv(act)

        def dve_odd(dve):
            dve_window(dve)
            dve_rwkv(dve)

        def norm_src(name):
            return memx if name.startswith("mem") else x

        HT_FREE = {"mem0": 0, "mem1": chunk_done("mem_v0", 0), "mix0": chunk_done("mem_v1", 0),
                   "xattn0": chunk_done("ev_out", 3), "ffn0": chunk_done("xa_q0", 0),
                   "mix1": chunk_done("ffn0", FF_TURNS * FF_CHUNKS - 1), "xattn1": chunk_done("od_out", 3),
                   "ffn1": chunk_done("xa_q1", 0)}

        def after(name):
            return starts[name][0] + dict((n, c) for n, c, _ in GEMMS)[name]

        X_READY = {"xattn0": after("ev_out"), "ffn0": after("xa_o0"), "mix1": after("ffn0"),
                   "xattn1": after("od_out"), "ffn1": after("xa_o1")}

        def run_norm(eng, norm, name):
            if name in X_READY:
                wait_chunks_taken(eng, X_READY[name])
            norm(eng, name, norm_src(name), HT_FREE[name])

        @block.tensor
        def _(pe):
            pe.wait_ge(s_load, 64)
            pe_bias(pe)
            pe_norm(pe, "mem0", before=[(s_bias_s, DSA_H)])
            pe_memory(pe, 0)
            pe_norm(pe, "mem1", before=[(s_mkT, 2)])
            pe_memory(pe, 1)
            pe_norm(pe, "mix0", before=[(s_mkT, 4)])
            pe_even(pe)
            for l in range(2):
                if l:
                    pe_norm(pe, "mix1", before=[(s_xoT, 2)])
                    pe_odd(pe)
                pe_norm(pe, f"xattn{l}")
                pe_cross(pe, l)
                pe_norm(pe, f"ffn{l}")
                pe_ffn(pe, l)

        @block.scalar
        def _(act):
            act_bias(act)
            act.wait_ge(s_load, 64)
            for l in range(2):
                run_norm(act, act_norm, f"mem{l}")
                act_memory(act, l)
            run_norm(act, act_norm, "mix0")
            act.wait_ge(s_bias_out, 16)
            act_even(act)
            for l in range(2):
                if l:
                    run_norm(act, act_norm, "mix1")
                    act_odd(act)
                run_norm(act, act_norm, f"xattn{l}")
                act_cross(act, l)
                run_norm(act, act_norm, f"ffn{l}")
                act_ffn(act, l)

        @block.vector
        def _(dve):
            dve.wait_ge(s_load, 64)
            nc.vector.tensor_tensor(gqk, par[:, Q["xa_qn"]], par[:, Q["xa_kn"]], MULT).then_inc(s_gqk, 1)
            for l in range(2):
                run_norm(dve, dve_norm, f"mem{l}")
                dve_memory(dve, l)
            run_norm(dve, dve_norm, "mix0")
            dve.wait_ge(s_bias_out, 16)
            dve_even(dve)
            for l in range(2):
                if l:
                    run_norm(dve, dve_norm, "mix1")
                    dve_odd(dve)
                run_norm(dve, dve_norm, f"xattn{l}")
                dve_cross(dve, l)
                run_norm(dve, dve_norm, f"ffn{l}")
                dve_ffn(dve, l)

        @block.gpsimd
        def _(pool):
            nc.gpsimd.memset(rel[N_BUCKETS:NB], NEG).then_inc(s_neg, 1)
            pool.wait_ge(s_load, 64)
            pool_even(pool)
            pool_odd(pool)


def constants():
    import math

    import numpy as np

    at, n = columns(CONST_COLS)
    c = np.zeros((P, n), np.float32)
    s, t = np.arange(P)[:, None], np.arange(P)[None, :]
    c[:, at["ident"]] = s == t
    level = np.zeros((P, 2, LEVELS, P), np.float32)
    for n_, size in enumerate(1 << np.arange(LEVELS)):
        pair = (s // (2 * size)) == (t // (2 * size))
        level[:, 0, n_] = pair & (s // size < t // size)
        level[:, 1, n_] = pair & (s // size > t // size)
    c[:, at["level"]] = level.reshape(P, -1)
    c[:, at["neg"]] = np.where(np.hstack([s <= t, s >= t]), 0.0, NEG)
    low, high = s < P // 2, s >= P // 2
    mid = [(s <= t) * 1.0 - low, (s < t) * 1.0 - low, (s >= t) * 1.0 - high, (s > t) * 1.0 - high]
    c[:, at["cum_mid"]] = np.hstack(mid)
    c[:, at["causal"]] = np.hstack([s < t, s <= t, s > t, s >= t])
    c[:, at["halves"]] = (s // RW_N) == (t // RW_N)
    c[:, at["ones"]] = 1.0
    c[:, at["half_cols"]] = np.hstack([low, high])

    table = np.zeros((N_BUCKETS + 1, DSA_G, 512), np.float32)
    half = N_BUCKETS // 2
    exact = half // 2
    for g, dil in enumerate(DILATIONS):
        rel = np.arange(512) - (S - 1)
        inside = (rel % dil == 0) & (np.abs(rel) <= N_SIDE * dil)
        dist = np.abs(rel)
        ratio = np.maximum(dist, exact).astype(np.float32) / np.float32(exact)
        scaled = np.log(ratio) / np.float32(math.log(MAX_DIST / exact))
        large = np.minimum(exact + (scaled * np.float32(half - exact)).astype(np.int32), half - 1)
        bucket = np.where(rel > 0, half, 0) + np.where(dist < exact, dist, large)
        for n_ in range(512):
            table[bucket[n_] if inside[n_] else N_BUCKETS, g, n_] = 1.0
    return c, table.reshape(N_BUCKETS + 1, -1)


def kernel(**inputs):
    import numpy as np
    import concourse.bacc as bacc
    from concourse.bass_utils import run_bass_kernel_spmd

    a = {name: np.asarray(value) for name, value in inputs.items()}

    sc = a["ev_w_in"][0][:, 4 * DN_W + 4 * DN_H:]
    sc_order = [(part, half) for half in range(2) for part in (1, 2, 0)]
    rw = a["od_w_in"][0][:, 3 * DSA_H * P:]
    matrices = {
        "ev_qkv": a["ev_w_in"][0][:, :3 * DN_W],
        "ev_gate": a["ev_w_in"][0][:, 3 * DN_W:4 * DN_W],
        "ev_sc": np.hstack([sc[:, p * 1024 + h * 512:p * 1024 + h * 512 + 512] for p, h in sc_order]),
        "ev_out": a["ev_w_out"][0],
        "od_q": a["od_w_in"][0][:, :DSA_H * P],
        "od_k": a["od_w_in"][0][:, DSA_H * P:2 * DSA_H * P],
        "od_v": a["od_w_in"][0][:, 2 * DSA_H * P:3 * DSA_H * P],
        "od_rw": np.pad(rw, ((0, 0), (0, 2048 - rw.shape[1]))),
        "od_out": a["od_w_out"][0],
    }
    for l in range(2):
        matrices[f"mem_k{l}"], matrices[f"mem_v{l}"] = a["xa_wk"][l], a["xa_wv"][l]
        matrices[f"xa_q{l}"], matrices[f"xa_o{l}"] = a["xa_wq"][l], a["xa_wo"][l]
    starts, _, n_units = gemm_starts()
    stream = np.zeros((n_units, P, UNIT), np.float32)

    def row_units(w):
        k, n = w.shape
        return w.reshape(k // 256, 2, P, n // 512, 512).transpose(3, 0, 2, 1, 4).reshape(-1, P, UNIT)

    def column_units(w):
        k, n = w.shape
        return w.reshape(k // 1024, 8, P, n // P, P).transpose(3, 0, 2, 1, 4).reshape(-1, P, UNIT)

    for name, _, _ in GEMMS:
        u = starts[name][1]
        if name.startswith("ffn"):
            l, width = int(name[-1]), F_FF // FF_TURNS
            parts = []
            for i in range(FF_TURNS):
                parts.append(column_units(a["ffn_w1"][l][:, i * width:(i + 1) * width]))
                parts.append(row_units(a["ffn_w2"][l][i * width:(i + 1) * width]))
            got = np.concatenate(parts)
        elif name in ("ev_qkv", "ev_sc", "od_q", "od_rw", "xa_q0", "xa_q1"):
            got = column_units(matrices[name])
        else:
            got = row_units(matrices[name])
        stream[u:u + len(got)] = got
    stream = stream.reshape(n_units // 2, 2, P, UNIT).transpose(0, 2, 1, 3).reshape(n_units // 2, P, BLOCK)

    tiles = lambda v: np.ascontiguousarray(v.reshape(-1, P).T)
    rows = lambda v: np.broadcast_to(v.reshape(1, -1), (P, v.size))
    at, n = columns(PARAM_COLS)
    small = np.zeros((P, n), np.float32)
    for l in range(2):
        for name, source in (("mix", "norm_mix"), ("xattn", "norm_xattn"), ("mem", "norm_mem"), ("ffn", "norm_ffn")):
            small[:, at[f"g_{name}{l}"]] = tiles(a[source][l])
    small[:, at["xa_qn"]], small[:, at["xa_kn"]] = a["xa_qn"].T, a["xa_kn"].T
    small[:, at["dn_conv"]] = a["dn_conv"][0].reshape(24, P, 3).transpose(1, 0, 2).reshape(P, 72)
    small[:, at["sc_conv"]] = a["sc_conv"][0].reshape(8, P, 3).transpose(1, 0, 2).reshape(P, 24)
    small[:, at["dn_norm"]] = rows(a["dn_norm"][0])
    small[:, at["a_log"]], small[:, at["dt_bias"]] = rows(a["dn_a_log"][0]), rows(a["dn_dt_bias"][0])
    small[:, at["ab_w"]] = (a["ev_w_in"][0][:, 4 * DN_W:4 * DN_W + 4 * DN_H]
                            .reshape(KD, P, 4 * DN_H).transpose(1, 0, 2).reshape(P, 512))
    small[:, at["ca_qn"]], small[:, at["ca_kn"]] = a["ca_qn"].T, a["ca_kn"].T
    small[:, at["rw_mu"]] = tiles(a["rw_mu"][0])
    small[:, at["rw_a0"]] = tiles(a["rw_a0"][0])
    small[:, at["rw_kk"]], small[:, at["rw_ka"]] = tiles(a["rw_k_k"][0]), tiles(a["rw_k_a"][0])
    small[:, at["rw_rk"]] = tiles(a["rw_r_k"][0])
    at, n = columns(WIDE_COLS)
    wide = np.zeros((P, n), np.float32)
    wide[:, at["w2"]], wide[:, at["a2"]] = a["rw_w2"][0].reshape(P, RW_W), a["rw_a2"][0].reshape(P, RW_W)
    wide[:, at["g2"]] = a["rw_g2"][0]
    wide[:, at["w0"]] = rows(a["rw_w0"][0])
    wide[:, at["ln_w"]], wide[:, at["ln_b"]] = rows(a["rw_ln_w"][0]), rows(a["rw_ln_b"][0])

    masks, table = constants()
    sent = {
        "x": a["x"][0], "mem": a["mem"][0], "stream": stream, "small": small, "wide": wide,
        "masks": masks, "bias_table": table, "rel_bias": a["rel_bias"],
    }
    nc = bacc.Bacc("TRN2", target_bir_lowering=False, num_devices=1, dynamic_dma_scratch_size=1024)
    arrays = {f"in_{name}": np.ascontiguousarray(v) for name, v in sent.items()}
    aps = [nc.dram_tensor(name, v.shape, mybir.dt.from_np(v.dtype), kind="ExternalInput").ap()
           for name, v in arrays.items()]
    out = nc.dram_tensor("out", (S, D), F32, kind="ExternalOutput").ap()
    scratch = nc.dram_tensor("bias_rows", (DSA_H, P, 512), F32, kind="Internal").ap()
    build(nc, *aps, scratch, out)
    r = run_bass_kernel_spmd(nc, [arrays], core_ids=[0])
    return r.results[0]["out"].reshape(1, S, D)
```

```python
from contextlib import ExitStack

import concourse.bass as bass
from concourse import mybir

P = 128
D = 2048
S = 256
NT = S // P
KD = D // P
RAW = 4
SPLIT = 4
AHEAD = SPLIT
UNIT = 1024
BLOCK = 2 * UNIT
WORK = 19200
F_FF = 4 * D
RMS_EPS = 1e-6

ALU = mybir.AluOpType
ACT = mybir.ActivationFunctionType
F32 = mybir.dt.float32
F32R = mybir.dt.float32r
AX_X = mybir.AxisListType.X

MULT, ADD, SUB, MAX = ALU.mult, ALU.add, ALU.subtract, ALU.max

DN_H = 8
DN_W = DN_H * P
DSA_G = 3
DSA_HG = 4
DSA_H = DSA_G * DSA_HG
DILATIONS = (1, 4, 16)
N_SIDE = 64
N_BUCKETS = 32
MAX_DIST = 1024
NEG = -1e30
RW_H = 8
RW_N = 64
RW_W = RW_H * RW_N
RW_F = RW_W // P
KAPPA = 0.6065306597126334
GN_EPS = 64e-5
XA_H = 4
HEAD_SCALE = float(P) ** -0.5
LEVELS = 7

FF_TURNS = 4
FF_CHUNKS = 8
FF_UNITS = 64
GEMMS = [
    ("mem_k0", 1, 8), ("mem_v0", 1, 8), ("mem_k1", 1, 8), ("mem_v1", 1, 8),
    ("ev_qkv", 6, 8), ("ev_gate", 2, 8), ("ev_sc", 6, 8), ("ev_out", 4, 8),
    ("xa_q0", 1, 8), ("xa_o0", 4, 2), ("ffn0", FF_TURNS * FF_CHUNKS, 8),
    ("od_q", 3, 8), ("od_k", 3, 8), ("od_v", 3, 8), ("od_rw", 4, 8), ("od_out", 4, 4),
    ("xa_q1", 1, 8), ("xa_o1", 4, 2), ("ffn1", FF_TURNS * FF_CHUNKS, 8),
]
UNITS_OF = {name: units for name, _, units in GEMMS}


def gemm_starts():
    at, chunk, unit = {}, 0, 0
    for name, chunks, units in GEMMS:
        at[name] = (chunk, unit)
        chunk += chunks
        unit += chunks * units
    return at, chunk, unit


CONST_COLS = [
    ("ident", P), ("level", 2 * LEVELS * P),
    ("neg", 2 * P), ("cum_mid", 4 * P), ("causal", 4 * P), ("halves", P), ("ones", 1), ("half_cols", 2),
]
PARAM_COLS = [
    ("g_mix0", 16), ("g_mix1", 16), ("g_xattn0", 16), ("g_xattn1", 16),
    ("g_mem0", 16), ("g_mem1", 16), ("g_ffn0", 16), ("g_ffn1", 16),
    ("xa_qn", 2), ("xa_kn", 2), ("dn_conv", 72), ("sc_conv", 24), ("dn_norm", P),
    ("a_log", 16), ("dt_bias", 16), ("ab_w", 512),
    ("ca_qn", 1), ("ca_kn", 1), ("rw_mu", 15), ("rw_a0", 8), ("rw_kk", 4), ("rw_ka", 4), ("rw_rk", 4),
]
WIDE_COLS = [("w2", 512), ("a2", 512), ("g2", 512), ("w0", 1024), ("ln_w", 512), ("ln_b", 512)]


def columns(table):
    at, n = {}, 0
    for name, width in table:
        at[name] = slice(n, n + width)
        n += width
    return at, n


class Chain:

    def __init__(self, engine, sem):
        self.engine, self.sem, self.n = engine, sem, 0

    def __call__(self, instruction):
        self.n += 1
        instruction.then_inc(self.sem, 1)
        self.engine.wait_ge(self.sem, self.n)


def build(nc, x_in, mem_in, stream, small, wide, masks, bias_table, rel_bias, bias_rows, x_out):
    starts, n_chunks, n_units = gemm_starts()
    C, n_const = columns(CONST_COLS)
    Q, n_param = columns(PARAM_COLS)
    WD, n_wide = columns(WIDE_COLS)

    ctx = ExitStack()
    with ctx:
        def sem(name):
            return ctx.enter_context(nc.semaphore(name))

        at = [1152]

        def place(name, shape, dtype=F32, offset=None):
            n = 4
            for d in shape[1:]:
                n *= d
            if offset is None:
                offset = at[0]
                at[0] += (n + 31) // 32 * 32
            return nc.alloc_sbuf_tensor_at(name, shape, dtype, offset=offset)

        x = place("x", [P, NT, D])
        const = place("const", [P, n_const])
        par = place("par", [P, n_param])
        mem_kT = [place(f"mem_kT{l}", [P, XA_H, S]) for l in range(2)]
        mem_v = [place(f"mem_v{l}", [P, NT, XA_H * P]) for l in range(2)]
        st = place("st", [P, 768])
        raw = place("raw", [P, RAW, BLOCK])
        split_hi = place("split_hi", [P, SPLIT, UNIT], F32R)
        split_lo = place("split_lo", [P, SPLIT, UNIT], F32R)
        hT_at = at[0]
        hT_hi = place("hT_hi", [P, KD, S], F32R)
        hT_lo = place("hT_lo", [P, KD, S], F32R)
        hwork = place("hwork", [P, 2 * KD * S], offset=hT_at)
        rwork = place("rwork", [P, 2 * SPLIT * UNIT], offset=hT_at - 8 * SPLIT * UNIT)
        work_at = at[0]
        work = place("work", [P, WORK])
        u_hi = place("u_hi", [P, 16, S], F32R, offset=work_at)
        u_lo = place("u_lo", [P, 16, S], F32R, offset=work_at + 4 * 4096)
        ab_hi = place("ab_hi", [P, 512], F32R, offset=work_at + 4 * 16384)
        ab_lo = place("ab_lo", [P, 512], F32R, offset=work_at + 4 * 16896)
        bank = [ctx.enter_context(nc.psum_tensor(f"bank{i}", [P, 512], F32)) for i in range(8)]
        aux = bank[4:]

        def view(area, at, *shape):
            n = 1
            for d in shape:
                n *= d
            v = area[:, at:at + n]
            if len(shape) == 1:
                return v
            names = "abcd"[:len(shape)]
            return v.rearrange(f"p ({' '.join(names)}) -> p {' '.join(names)}",
                               **dict(zip(names[1:], shape[1:])))

        def W(at, *shape):
            return view(work, at, *shape)

        def H(at, *shape):
            return view(hwork, at, *shape)

        def R(at, *shape):
            return view(rwork, at, *shape)

        def four(ap):
            return ap[:, :].rearrange("p (m n) -> p m n", n=P)

        def const_of(name, i, width=P):
            return const[:, C[name].start + i * width:C[name].start + (i + 1) * width]

        ident = const[:, C["ident"]]
        ones_col = const[:, C["ones"]]

        s_load = sem("s_load")
        s_mem_in, s_x_in = sem("s_mem_in"), sem("s_x_in")
        s_raw = [sem(f"s_raw{i}") for i in range(RAW)]
        s_hi, s_lo = sem("s_hi"), sem("s_lo")
        s_used = sem("s_used")
        s_taken = [sem(f"s_taken{i}") for i in range(2)]
        s_dve, s_act, s_pool = sem("s_dve"), sem("s_act"), sem("s_pool")
        s_sq = sem("s_sq")
        s_ms = sem("s_ms")
        s_sd = sem("s_sd")
        s_rstd = sem("s_rstd")
        s_xn = sem("s_xn")
        s_tr = sem("s_tr")
        s_hTh, s_hTl = sem("s_hTh"), sem("s_hTl")
        s_mk_ms, s_mk_sd, s_mk = sem("s_mk_ms"), sem("s_mk_sd"), sem("s_mk")
        s_mk_tr, s_mkT = sem("s_mk_tr"), sem("s_mkT")
        s_xq, s_xss, s_xms, s_xsd = (sem(n) for n in ("s_xq", "s_xss", "s_xms", "s_xsd"))
        s_xlog, s_xnm, s_xexp, s_xp = sem("s_xlog"), sem("s_xnm"), sem("s_xexp"), sem("s_xp")
        s_xpt, s_xpt_a, s_xpt_d = sem("s_xpt"), sem("s_xpt_a"), sem("s_xpt_d")
        s_xo, s_xoh, s_xoT = sem("s_xo"), sem("s_xoh"), sem("s_xoT")
        s_uh, s_u = sem("s_uh"), sem("s_u")
        s_ysp, s_abw = sem("s_ysp"), sem("s_abw")
        s_gqk = sem("s_gqk")
        s_out = sem("s_out")
        iv_mt = [sem("iv_mt0"), sem("iv_mt1")]
        iv_p, iv_ps, iv_q, iv_t, iv_tt = (sem(n) for n in ("iv_p", "iv_ps", "iv_q", "iv_t", "iv_tt"))
        s_ab, s_abv, s_ax, s_sp, s_g = (sem(n) for n in ("s_ab", "s_abv", "s_ax", "s_sp", "s_g"))
        s_cv, s_silu = sem("s_cv"), sem("s_silu")
        s_dsq, s_kvt, s_kv_a, s_kv_d = sem("s_dsq"), sem("s_kvt"), sem("s_kv_a"), sem("s_kv_d")
        s_dss, s_cum, s_cumv, s_dms, s_dsd, s_dE, s_stats = (
            sem(n) for n in ("s_dss", "s_cum", "s_cumv", "s_dms", "s_dsd", "s_dE", "s_stats"))
        s_pre, s_diff, s_D, s_eg, s_AT, s_qtg, s_vb = (
            sem(n) for n in ("s_pre", "s_diff", "s_D", "s_eg", "s_AT", "s_qtg", "s_vb"))
        s_vn1, s_vn1s, s_S, s_Ss, s_kS, s_R, s_vn2, s_vn2s, s_o, s_os = (
            sem(n) for n in ("s_vn1", "s_vn1s", "s_S", "s_Ss", "s_kS", "s_R", "s_vn2", "s_vn2s", "s_o", "s_os"))
        s_oms, s_osd, s_y, s_yt, s_yT = (sem(n) for n in ("s_oms", "s_osd", "s_y", "s_yt", "s_yT"))
        s_bt_in, s_bias_m, s_bias_s, s_bias_out, s_bias_in = (
            sem(n) for n in ("s_bt_in", "s_bias_m", "s_bias_s", "s_bias_out", "s_bias_in"))
        s_neg = sem("s_neg")
        s_oss, s_oms0, s_osd0 = (sem(n) for n in ("s_oss", "s_oms0", "s_osd0"))
        s_ok, s_okt, s_okT_a, s_okT_d = (
            sem(n) for n in ("s_ok", "s_okt", "s_okT_a", "s_okT_d"))
        s_ol, s_onm, s_oexp, s_op, s_opt, s_optT, s_opv, s_oyc = (
            sem(n) for n in ("s_ol", "s_onm", "s_oexp", "s_op", "s_opt", "s_optT", "s_opv", "s_oyc"))
        s_wide, s_rw, s_rtanh, s_rwm, s_rlw0, s_lw, s_rgm, s_rgs, s_ram, s_ra, s_rvt, s_rv = (
            sem(n) for n in ("s_wide", "s_rw", "s_rtanh", "s_rwm", "s_rlw0", "s_lw", "s_rgm", "s_rgs", "s_ram", "s_ra", "s_rvt", "s_rv"))
        s_kk0, s_kksq, s_kkm, s_kkms, s_kksd, s_kk, s_kd, s_pr, s_prm, s_bon = (
            sem(n) for n in ("s_kk0", "s_kksq", "s_kkm", "s_kkms", "s_kksd", "s_kk", "s_kd", "s_pr", "s_prm", "s_bon"))
        s_rc, s_rF, s_rRA, s_rbk, s_rM, s_rMAT, s_rbt, s_rBK, s_rz1, s_rz1s = (
            sem(n) for n in ("s_rc", "s_rF", "s_rRA", "s_rbk", "s_rM", "s_rMAT", "s_rbt", "s_rBK", "s_rz1", "s_rz1s"))
        s_gms, s_gsd, s_ry, s_ryt = (sem(n) for n in ("s_gms", "s_gsd", "s_ry", "s_ryt"))
        block = ctx.enter_context(nc.Block())

        NORMS = ["mem0", "mem1", "mix0", "xattn0", "ffn0", "mix1", "xattn1", "ffn1"]
        NORM_NO = {name: i for i, name in enumerate(NORMS)}
        squares = W(8192, NT, D)
        diag = W(18944, NT, P)
        memx = W(12288, NT, D)

        dve_chain, act_chain, pool_chain = Chain(nc.vector, s_dve), Chain(nc.scalar, s_act), Chain(nc.gpsimd, s_pool)
        dve_step, act_step, pool_step = dve_chain, act_chain, pool_chain

        def wait_chunks_taken(eng, chunk):
            for parity in range(2):
                n = (chunk + 1 - parity) // 2
                if n:
                    eng.wait_ge(s_taken[parity], 2 * n)

        ss, msq, sdv, rstd = st[:, 0:2], st[:, 2:4], st[:, 4:6], st[:, 6:8]
        mk_st = [[st[:, at + 8 * i:at + 8 + 8 * i] for i in range(4)] for at in (8, 704)]
        xa_ms, xa_sd, xa_r, xa_rq = (st[:, 40 + 8 * i:48 + 8 * i] for i in range(4))
        xa_mx, xa_nm, xa_sum, xa_rs = (st[:, 72 + 8 * i:80 + 8 * i] for i in range(4))
        gqk = st[:, 104:106]

        def f32(ap):
            return ap.bitcast(F32)

        def write_hi(act, u, turn=0):
            b = u // 2
            if u % 2 == 0:
                act.wait_ge(s_raw[b % RAW], turn * (FF_UNITS // 2 // RAW * 16) + (b // RAW + 1) * 16)
            if u >= SPLIT:
                act.wait_ge(s_used, turn * FF_UNITS + (u - SPLIT + 1))
            nc.scalar.activation(split_hi[:, u % SPLIT], raw[:, b % RAW, (u % 2) * UNIT:(u % 2 + 1) * UNIT],
                                 ACT.Copy).then_inc(s_hi, 1)

        def write_lo(dve, u, turn=0):
            b = u // 2
            dve.wait_ge(s_hi, turn * FF_UNITS + (u + 1))
            nc.vector.tensor_tensor(split_lo[:, u % SPLIT], raw[:, b % RAW, (u % 2) * UNIT:(u % 2 + 1) * UNIT],
                                    f32(split_hi[:, u % SPLIT]), SUB).then_inc(s_lo, 1)

        next_hi, next_lo = [0], [0]

        def hi_upto(act, n):
            while next_hi[0] < min(n, n_units):
                write_hi(act, next_hi[0])
                next_hi[0] += 1

        def lo_upto(dve, n):
            while next_lo[0] < min(n, n_units):
                write_lo(dve, next_lo[0])
                next_lo[0] += 1

        class Gemm:

            def __init__(self, pe, name, turn=0, turns=(FF_CHUNKS, FF_UNITS)):
                self.pe, self.turn, self.turns = pe, turn, turns
                self.chunk0, self.unit0 = starts[name]
                self.per = UNITS_OF[name]

            def unit(self, n):
                u = self.unit0 + n
                self.pe.wait_ge(s_lo, self.turn * self.turns[1] + (u + 1))
                return split_hi[:, u % SPLIT], split_lo[:, u % SPLIT]

            def banks(self, c):
                g = self.chunk0 + c
                if g >= 2:
                    self.pe.wait_ge(s_taken[g % 2], self.turn * self.turns[0] + g // 2 * 2)
                return bank[2 * (g % 2):2 * (g % 2) + 2]

            def row_chunk(self, c, lhsT, k_tiles=KD, k_ready=None):
                acc = self.banks(c)
                for k in range(k_tiles):
                    if k_ready:
                        k_ready(k)
                    if k % 2 == 0:
                        w_hi, w_lo = self.unit(c * self.per + k // 2)
                    cols = slice((k % 2) * 512, (k % 2 + 1) * 512)
                    for t in range(NT):
                        x_hi, x_lo = lhsT(k, t)
                        out = acc[t][:, :]
                        nc.tensor.matmul(out, lhsT=x_hi, rhs=w_hi[:, cols], start=k == 0, stop=False)
                        nc.tensor.matmul(out, lhsT=x_hi, rhs=w_lo[:, cols], start=False, stop=False)
                        m = nc.tensor.matmul(out, lhsT=x_lo, rhs=w_hi[:, cols], start=False, stop=k == k_tiles - 1)
                    if k % 2:
                        m.then_inc(s_used, 1)

            def column_chunk(self, c, tiles=4, k_ready=None):
                acc = self.banks(c)
                for i in range(tiles):
                    for j in range(2):
                        n = c * self.per + 2 * i + j
                        w_hi, w_lo = self.unit(n)
                        used = 1
                        if (i, j) == (tiles - 1, 1) and tiles < 4:
                            used += 2 * (4 - tiles)
                            self.unit(n + used - 1)
                        for kk in range(8):
                            k = 8 * j + kk
                            if k_ready and i == 0:
                                k_ready(k)
                            cols = slice(kk * P, (kk + 1) * P)
                            out = acc[i // 2][:, (i % 2) * S:(i % 2 + 1) * S]
                            nc.tensor.matmul(out, lhsT=w_hi[:, cols], rhs=hT_hi[:, k, :], start=k == 0, stop=False)
                            nc.tensor.matmul(out, lhsT=w_hi[:, cols], rhs=hT_lo[:, k, :], start=False, stop=False)
                            m = nc.tensor.matmul(out, lhsT=w_lo[:, cols], rhs=hT_hi[:, k, :], start=False, stop=k == KD - 1)
                        m.then_inc(s_used, used)

        def chunk_done(name, c):
            return starts[name][1] + UNITS_OF[name] * (c + 1)

        def chunk_banks(name, c):
            parity = (starts[name][0] + c) % 2
            return bank[2 * parity:2 * parity + 2], s_taken[parity]

        @block.sync
        def _(sp):
            sp.dma_start(memx, mem_in.rearrange("(t p) d -> p t d", p=P)).then_inc(s_mem_in, 16)
            sp.dma_start(const[:, :], masks).then_inc(s_load, 16)
            sp.dma_start(par[:, :], small).then_inc(s_load, 16)

            def load(b, slot):
                sp.dma_start(raw[:, slot, :], stream[b]).then_inc(s_raw[slot], 16)

            for slot in range(RAW):
                load(slot, slot)
            sp.dma_start(x[:, :, :], x_in.rearrange("(t p) d -> p t d", p=P)).then_inc(s_x_in, 16)
            with sp.Fori(1, n_units // 2 // RAW) as turn:
                for slot in range(RAW):
                    sp.wait_ge(s_lo, turn * (2 * RAW) + 2 * (slot - RAW + 1))
                    load(turn * RAW + slot, slot)
            wait_chunks_taken(sp, n_chunks)
            sp.dma_start(x_out.rearrange("(t p) d -> p t d", p=P), x[:, :, :]).then_inc(s_out, 16)
            sp.wait_ge(s_out, 16)

        def pe_norm(pe, name, before=()):
            n = NORM_NO[name]
            src = norm_src(name)
            pe.wait_ge(s_xn, max(n, 1))
            for sem_, value in before:
                pe.wait_ge(sem_, value)
            for b in range(8):
                if n or b >= 4:
                    pe.wait_ge(s_hTl, 8 * n + b - 3)
                for i in range(2):
                    for t in range(NT):
                        k = 2 * b + i
                        m = nc.tensor.matmul(aux[b % 4][:, (2 * i + t) * P:(2 * i + t + 1) * P],
                                             lhsT=src[:, t, k * P:(k + 1) * P], rhs=diag[:, t, :], start=True, stop=True)
                m.then_inc(s_tr, 1)

        def gained(name, b):
            for i in range(2):
                k = 2 * b + i
                yield k, aux[b % 4][:, i * S:(i + 1) * S], par[:, Q[f"g_{name}"].start + k:Q[f"g_{name}"].start + k + 1]

        def act_norm(act, name, src, hT_free):
            n = NORM_NO[name]
            if name != "mem1":
                if n:
                    act.wait_ge(s_tr, 8 * n)
                nc.scalar.activation(squares[:, 0, :], src[:, 0, :], ACT.Square, accum_out=ss[:, 0:1]).then_inc(s_sq, 1)
                act.wait_ge(s_ms, max(n, 1))
                nc.scalar.activation(sdv, msq, ACT.Sqrt).then_inc(s_sd, 1)
            act.wait_ge(s_used, hT_free)
            for b in range(8):
                act.wait_ge(s_tr, 8 * n + b + 1)
                for k, v, gain in gained(name, b):
                    m = nc.scalar.activation(hT_hi[:, k, :], v, ACT.Copy, scale=gain)
                m.then_inc(s_hTh, 1)

        def dve_norm(dve, name, src, hT_free):
            n = NORM_NO[name]
            if name != "mem1":
                if n:
                    dve.wait_ge(s_tr, 8 * n)
                dve_step(nc.vector.tensor_tensor_reduce(out=squares[:, 1, :], in0=src[:, 1, :], in1=src[:, 1, :], scale=1.0,
                                                        scalar=0.0, op0=MULT, op1=ADD, accum_out=ss[:, 1:2]))
                dve.wait_ge(s_sq, max(n, 1))
                nc.vector.tensor_scalar(msq, ss, 1.0 / D, RMS_EPS, MULT, ADD).then_inc(s_ms, 1)
                dve.wait_ge(s_sd, max(n, 1))
                nc.vector.reciprocal(rstd, sdv).then_inc(s_rstd, 1)
                dve.wait_ge(s_rstd, max(n, 1))
                for t in range(NT):
                    m = nc.vector.tensor_scalar(diag[:, t, :], ident, rstd[:, t:t + 1], None, MULT)
                m.then_inc(s_xn, 1)
            for b in range(8):
                dve.wait_ge(s_hTh, 8 * n + b + 1)
                for k, v, gain in gained(name, b):
                    m = nc.vector.scalar_tensor_tensor(out=hT_lo[:, k, :], in0=v, scalar=gain, in1=f32(hT_hi[:, k, :]),
                                                       op0=MULT, op1=SUB)
                m.then_inc(s_hTl, 1)

        def pe_hT(pe, name, tiles=KD):
            n = NORM_NO[name]
            pe.wait_ge(s_hTl, 8 * n + (tiles + 1) // 2)

        def hT_ready(pe, name):
            return lambda k: pe_hT(pe, name, k + 1) if k % 2 == 0 else None

        mk_of = [W(4096 + 1024 * l, NT, XA_H * P) for l in range(2)]
        mk_sq = W(17920, NT, XA_H * P)

        def heads8(ap):
            return ap.rearrange("p t (h e) -> p (t h) e", e=P)

        def lanes(ap, n):
            return ap.unsqueeze(2).broadcast_to([P, ap.shape[1], n])

        def hT_tile(k, t):
            return hT_hi[:, k, t * P:(t + 1) * P], hT_lo[:, k, t * P:(t + 1) * P]

        def pe_memory(pe, l):
            Gemm(pe, f"mem_k{l}").row_chunk(0, hT_tile, k_ready=hT_ready(pe, f"mem{l}"))
            Gemm(pe, f"mem_v{l}").row_chunk(0, hT_tile)

        def pe_memory_keys(pe, l):
            mk = mk_of[l]
            pe.wait_ge(s_mk, l + 1)
            for h in range(XA_H):
                for t in range(NT):
                    m = nc.tensor.transpose(aux[2 * l + h // 2][:, ((h % 2) * NT + t) * P:((h % 2) * NT + t + 1) * P],
                                            mk[:, t, h * P:(h + 1) * P], ident)
                if h % 2:
                    m.then_inc(s_mk_tr, 1)

        def take_row_chunk(act, name, c, dst):
            banks, taken = chunk_banks(name, c)
            hi_upto(act, chunk_done(name, c) + AHEAD)
            act.wait_ge(s_used, chunk_done(name, c))
            for t in range(NT):
                nc.scalar.activation(dst(t), banks[t][:, :], ACT.Copy).then_inc(taken, 1)

        def act_memory(act, l):
            take_row_chunk(act, f"mem_k{l}", 0, lambda t: mk_of[l][:, t, :])
            take_row_chunk(act, f"mem_v{l}", 0, lambda t: mem_v[l][:, t, :])

        def act_memory_root(act, l):
            act.wait_ge(s_mk_ms, l + 1)
            _, mk_ms, mk_sd, _ = mk_st[l]
            nc.scalar.activation(mk_sd, mk_ms, ACT.Sqrt).then_inc(s_mk_sd, 1)

        def act_memory_keys(act, l):
            for b in range(2):
                act.wait_ge(s_mk_tr, 2 * l + b + 1)
                nc.scalar.activation(mem_kT[l][:, 2 * b:2 * b + 2, :], aux[2 * l + b][:, :].rearrange("p (h s) -> p h s", s=S),
                                     ACT.Copy).then_inc(s_mkT, 1)

        def dve_memory(dve, l):
            lo_upto(dve, chunk_done(f"mem_k{l}", 0) + AHEAD)
            lo_upto(dve, chunk_done(f"mem_v{l}", 0) + AHEAD)

        def dve_memory_squares(dve, l):
            mk = mk_of[l]
            mk_ss, mk_ms, _, _ = mk_st[l]
            parity = starts[f"mem_k{l}"][0] % 2
            dve.wait_ge(s_taken[parity], 2 * (starts[f"mem_k{l}"][0] // 2 + 1))
            dve_step(nc.vector.tensor_tensor(mk_sq, mk, mk, MULT))
            dve_step(nc.vector.reduce_sum(mk_ss, heads8(mk_sq), AX_X))
            nc.vector.tensor_scalar(mk_ms, mk_ss, 1.0 / P, RMS_EPS, MULT, ADD).then_inc(s_mk_ms, 1)

        def dve_memory_keys(dve, l):
            mk = mk_of[l]
            _, _, mk_sd, mk_r = mk_st[l]
            dve.wait_ge(s_mk_sd, l + 1)
            dve_step(nc.vector.reciprocal(mk_r, mk_sd))
            nc.vector.tensor_tensor(heads8(mk), heads8(mk), lanes(mk_r, P), MULT).then_inc(s_mk, 1)

        xq_sq, xqT = W(0, XA_H, S), W(1024, XA_H, S)
        xp = W(2048, NT, XA_H, S)
        xpT = W(4096, NT, XA_H, S)

        def pe_cross(pe, l):
            Gemm(pe, f"xa_q{l}").column_chunk(0, k_ready=hT_ready(pe, f"xattn{l}"))
            pe.wait_ge(s_xq, l + 1)
            for t in range(NT):
                for h in range(XA_H):
                    m = nc.tensor.matmul(aux[0][:, t * XA_H + h:t * XA_H + h + 1],
                                         lhsT=xq_sq[:, h, t * P:(t + 1) * P], rhs=ones_col, start=True, stop=True)
            m.then_inc(s_xss, 1)
            for b in list(range(1, 4)) + [0]:
                t, hp = b // 2, b % 2
                if b == 0:
                    pe.wait_ge(s_xms, l + 1)
                for i in range(2):
                    h = 2 * hp + i
                    m = nc.tensor.matmul(aux[b][:, i * S:(i + 1) * S], lhsT=xqT[:, h, t * P:(t + 1) * P],
                                         rhs=mem_kT[l][:, h, :], start=True, stop=True)
                m.then_inc(s_xlog, 1)
            for n, b in enumerate(XB):
                t, hp = b // 2, b % 2
                pe.wait_ge(s_xp, 4 * l + n + 1)
                for i in range(2):
                    for mt in range(NT):
                        m = nc.tensor.transpose(aux[b][:, (2 * i + mt) * P:(2 * i + mt + 1) * P],
                                                xp[:, t, 2 * hp + i, mt * P:(mt + 1) * P], ident)
                m.then_inc(s_xpt, 1)
            pe.wait_ge(s_xpt_a, 2 * l + 2)
            pe.wait_ge(s_xpt_d, 2 * l + 2)
            for h in range(XA_H):
                for mt in range(NT):
                    m = nc.tensor.matmul(aux[h // 2][:, (h % 2) * S:(h % 2 + 1) * S],
                                         lhsT=mem_v[l][:, mt, h * P:(h + 1) * P], rhs=xpT[:, mt, h, :],
                                         start=mt == 0, stop=mt == NT - 1)
                if h % 2:
                    m.then_inc(s_xo, 1)
            pe.wait_ge(s_xoT, 2 * l + 2)
            for c in range(4):
                Gemm(pe, f"xa_o{l}").row_chunk(c, hT_tile, k_tiles=XA_H)

        XB = [1, 2, 3, 0]

        def pt_out(b):
            t, hp = b // 2, b % 2
            dst = xpT[:, :, 2 * hp:2 * hp + 2, t * P:(t + 1) * P].rearrange("p m i s -> p i m s")
            return dst, aux[b][:, :].rearrange("p (i m s) -> p i m s", i=2, s=P)

        def act_cross(act, l):
            name = f"xa_q{l}"
            banks, taken = chunk_banks(name, 0)
            hi_upto(act, chunk_done(name, 0) + AHEAD)
            act.wait_ge(s_used, chunk_done(name, 0))
            act.wait_ge(s_gqk, 1)
            for b in range(2):
                v = banks[b][:, :].rearrange("p (h s) -> p h s", s=S)
                nc.scalar.activation(xq_sq[:, 2 * b:2 * b + 2, :], v, ACT.Square)
                m = nc.scalar.activation(xqT[:, 2 * b:2 * b + 2, :], v, ACT.Copy, scale=gqk[:, l:l + 1])
                m.then_inc(taken, 1)
            act.wait_ge(taken, 2 * (starts[name][0] // 2 + 1))
            act.sem_inc(s_xq, 1)
            act.wait_ge(s_xms, l + 1)
            nc.scalar.activation(xa_sd, xa_ms, ACT.Sqrt).then_inc(s_xsd, 1)
            for n, b in enumerate(XB):
                t, hp = b // 2, b % 2
                act.wait_ge(s_xnm, 4 * l + n + 1)
                for i in range(2):
                    j = t * XA_H + 2 * hp + i
                    nc.scalar.activation(xp[:, t, 2 * hp + i, :], aux[b][:, i * S:(i + 1) * S], ACT.Exp,
                                         bias=xa_nm[:, j:j + 1], scale=xa_rq[:, j:j + 1],
                                         accum_out=xa_sum[:, j:j + 1]).then_inc(s_xexp, 1)
            for n, b in enumerate(XB):
                if b >= 2:
                    continue
                act.wait_ge(s_xpt, 4 * l + n + 1)
                dst, src = pt_out(b)
                for i in range(2):
                    m = nc.scalar.activation(dst[:, i], src[:, i], ACT.Copy)
                m.then_inc(s_xpt_a, 1)
            for b in range(2):
                act.wait_ge(s_xo, 2 * l + b + 1)
                nc.scalar.activation(hT_hi[:, 2 * b:2 * b + 2, :], aux[b][:, :].rearrange("p (h s) -> p h s", s=S),
                                     ACT.Copy).then_inc(s_xoh, 1)
            for c in range(4):
                hi_upto(act, chunk_done(f"xa_o{l}", c) + AHEAD)

        def dve_cross(dve, l):
            lo_upto(dve, chunk_done(f"xa_q{l}", 0) + AHEAD)
            dve.wait_ge(s_xss, l + 1)
            nc.vector.tensor_scalar(xa_ms, aux[0][:, 0:8], 1.0 / P, RMS_EPS, MULT, ADD).then_inc(s_xms, 1)
            dve.wait_ge(s_xsd, l + 1)
            dve_step(nc.vector.reciprocal(xa_r, xa_sd))
            dve_step(nc.vector.tensor_scalar(xa_rq, xa_r, HEAD_SCALE, None, MULT))
            for n, b in enumerate(XB):
                t, hp = b // 2, b % 2
                j = slice(t * XA_H + 2 * hp, t * XA_H + 2 * hp + 2)
                dve.wait_ge(s_xlog, 4 * l + n + 1)
                dve_step(nc.vector.reduce_max(xa_mx[:, j], aux[b][:, :].rearrange("p (i m) -> p i m", i=2), AX_X))
                nc.vector.scalar_tensor_tensor(out=xa_nm[:, j], in0=xa_mx[:, j], scalar=-1.0, in1=xa_rq[:, j],
                                               op0=MULT, op1=MULT).then_inc(s_xnm, 1)
            for n, b in enumerate(XB):
                t, hp = b // 2, b % 2
                j = slice(t * XA_H + 2 * hp, t * XA_H + 2 * hp + 2)
                dve.wait_ge(s_xexp, 8 * l + 2 * n + 2)
                dve_step(nc.vector.reciprocal(xa_rs[:, j], xa_sum[:, j]))
                pv = xp[:, t, 2 * hp:2 * hp + 2, :]
                nc.vector.tensor_tensor(pv, pv, lanes(xa_rs[:, j], S), MULT).then_inc(s_xp, 1)
            for n, b in enumerate(XB):
                if b < 2:
                    continue
                dve.wait_ge(s_xpt, 4 * l + n + 1)
                dst, src = pt_out(b)
                nc.vector.tensor_copy(dst, src).then_inc(s_xpt_d, 1)
            for b in range(2):
                dve.wait_ge(s_xoh, 2 * l + b + 1)
                nc.vector.tensor_tensor(hT_lo[:, 2 * b:2 * b + 2, :], aux[b][:, :].rearrange("p (h s) -> p h s", s=S),
                                        f32(hT_hi[:, 2 * b:2 * b + 2, :]), SUB).then_inc(s_xoT, 1)
            for c in range(4):
                dve_add_to_x(dve, f"xa_o{l}", c)

        def dve_add_to_x(dve, name, c):
            banks, taken = chunk_banks(name, c)
            lo_upto(dve, chunk_done(name, c) + AHEAD)
            dve.wait_ge(s_used, chunk_done(name, c))
            for t in range(NT):
                cols = x[:, t, c * 512:(c + 1) * 512]
                nc.vector.tensor_tensor(cols, cols, banks[t][:, :], ADD).then_inc(taken, 1)

        relu = W(16384, 2, UNIT)
        usq = W(12288, 4, UNIT)

        def u_tile(k, t):
            return u_hi[:, k, t * P:(t + 1) * P], u_lo[:, k, t * P:(t + 1) * P]

        def pe_ffn(pe, l):
            pe_hT(pe, f"ffn{l}")
            with pe.Fori(0, FF_TURNS) as turn:
                mlp = Gemm(pe, f"ffn{l}", turn)
                for c in range(4):
                    mlp.column_chunk(c)

                def u_ready(k):
                    if k % 4 == 0:
                        pe.wait_ge(s_u, turn * 4 + (4 * FF_TURNS * l + k // 4 + 1))

                for c in range(4, 8):
                    mlp.row_chunk(c, u_tile, k_ready=u_ready if c == 4 else None)

        def split_in_turn(write, eng, l, c, turn, last):
            u0 = starts[f"ffn{l}"][1] + AHEAD + 8 * c
            for u in range(u0, u0 + 8):
                if not last or u + (FF_TURNS - 1) * FF_UNITS < n_units:
                    write(eng, u, turn)

        def act_ffn(act, l):
            name = f"ffn{l}"
            hi_upto(act, starts[name][1] + AHEAD)

            def one_turn(turn, last):
                for c in range(FF_CHUNKS):
                    split_in_turn(write_hi, act, l, c, turn, last)
                    if c >= 4:
                        continue
                    banks, taken = chunk_banks(name, c)
                    g = starts[name][0] + c
                    act.wait_ge(s_used, turn * FF_UNITS + chunk_done(name, c))
                    for b in range(2):
                        nc.scalar.activation(relu[:, c % 2, b * 512:(b + 1) * 512], banks[b][:, :], ACT.Relu).then_inc(taken, 1)
                    act.wait_ge(taken, turn * FF_CHUNKS + (g // 2 + 1) * 2)
                    nc.scalar.activation(usq[:, c], relu[:, c % 2], ACT.Square)
                    nc.scalar.activation(u_hi[:, 4 * c:4 * c + 4, :].rearrange("p k s -> p (k s)"), relu[:, c % 2],
                                         ACT.Square).then_inc(s_uh, 1)

            run_turns(act, l, one_turn)
            next_hi[0] += FF_TURNS * FF_UNITS

        def run_turns(eng, l, one_turn):
            with eng.Fori(0, FF_TURNS - l) as turn:
                one_turn(turn, False)
            if l:
                one_turn(FF_TURNS - 1, True)

        def dve_ffn(dve, l):
            name = f"ffn{l}"
            lo_upto(dve, starts[name][1] + AHEAD)

            def one_turn(turn, last):
                for c in range(FF_CHUNKS):
                    split_in_turn(write_lo, dve, l, c, turn, last)
                    if c < 4:
                        dve.wait_ge(s_uh, turn * 4 + (4 * FF_TURNS * l + c + 1))
                        nc.vector.tensor_tensor(u_lo[:, 4 * c:4 * c + 4, :].rearrange("p k s -> p (k s)"), usq[:, c],
                                                f32(u_hi[:, 4 * c:4 * c + 4, :].rearrange("p k s -> p (k s)")), SUB).then_inc(s_u, 1)
                        continue
                    banks, taken = chunk_banks(name, c)
                    dve.wait_ge(s_used, turn * FF_UNITS + chunk_done(name, c))
                    for t in range(NT):
                        cols = x[:, t, (c - 4) * 512:(c - 3) * 512]
                        nc.vector.tensor_tensor(cols, cols, banks[t][:, :], ADD).then_inc(taken, 1)

            run_turns(dve, l, one_turn)
            next_lo[0] += FF_TURNS * FF_UNITS
        SMALL = 5

        def side_of(ap, level, right):
            size = 1 << level
            if len(ap.shape) == 3:
                return ap.rearrange("p m (n two s) -> p m n two s", two=2, s=size)[:, :, :, int(right)]
            return ap.rearrange("p (n two s) -> p n two s", two=2, s=size)[:, :, int(right)]

        def level_mask(d, level):
            i = C["level"].start + (d * LEVELS + level) * P
            return const[:, i:i + P].unsqueeze(1).broadcast_to([P, 4, P])

        def nth(group, level, d, first=0, count=LEVELS):
            return (group * count + level - first) * 2 + d + 1

        def iv_p_of(group, level, d):
            return nth(group, level, d, 1, LEVELS - 1)

        def pool_inv_mask(pool, group, AT, views, level, d):
            MT = views[3]
            n = group * LEVELS + level
            if n >= len(MT):
                before, its_level = divmod(n - len(MT), LEVELS)
                pool.wait_ge(iv_p if its_level else iv_t,
                             iv_p_of(before, its_level, d) if its_level else nth(before, 0, d))
            nc.gpsimd.tensor_tensor(MT[n % len(MT)][:, d], AT[d], level_mask(d, level), MULT).then_inc(iv_mt[d], 1)

        def pe_inv_level(pe, group, views, level, between):
            T, Tt, Pm, MT = views
            for d in range(2):
                pe.wait_ge(iv_mt[d], group * LEVELS + level + 1)
                pe.wait_ge(iv_t, nth(group, level - 1, d))
                for m in range(4):
                    i = nc.tensor.matmul(aux[d][:, m * P:(m + 1) * P], lhsT=MT[(group * LEVELS + level) % len(MT)][:, d, m],
                                         rhs=T[:, d, m], start=True, stop=True)
                i.then_inc(iv_p, 1)
            between(2 * level - 2)
            for d in range(2):
                pe.wait_ge(iv_ps, iv_p_of(group, level, d))
                if level <= SMALL:
                    pe.wait_ge(iv_tt, nth(group, level - 1, d, 0, SMALL))
                for m in range(4):
                    for j, (lhsT, rhs, needed) in enumerate((
                            (Tt[:, d, m], side_of(Pm[:, d, m], level, d == 1), level < LEVELS - 1),
                            (Pm[:, d, m], side_of(Tt[:, d, m], level, d == 0), level >= SMALL))):
                        if not needed:
                            continue
                        at = (4 * j + m) * 64
                        out = aux[2 + d][:, at:at + 64].rearrange("p (n s) -> p n s", s=1 << level)
                        i = nc.tensor.matmul(out, lhsT=lhsT, rhs=rhs, start=True, stop=True)
                i.then_inc(iv_q, 1)
            between(2 * level - 1)

        def pe_inv(pe, group, views, between):
            for level in range(1, LEVELS):
                pe_inv_level(pe, group, views, level, between)

        def act_inv(act, group, views, between):
            Pm = views[2]
            for level in range(1, LEVELS):
                for d in range(2):
                    act.wait_ge(iv_p, iv_p_of(group, level, d))
                    if iv_p_of(group, level, d) > 2:
                        act.wait_ge(iv_q, iv_p_of(group, level, d) - 2)
                    nc.scalar.activation(Pm[:, d], four(aux[d]), ACT.Copy).then_inc(iv_ps, 1)
                between(level)

        def dve_inv(dve, group, views, between):
            T, Tt, Pm, MT = views
            flat = lambda v: v.rearrange("p m s -> p (m s)")
            for level in range(LEVELS):
                for d in range(2):
                    if level == 0:
                        dve.wait_ge(iv_mt[d], group * LEVELS + 1)
                        eye = ident.unsqueeze(1).broadcast_to([P, 4, P])
                        nc.vector.tensor_tensor(Tt[:, d], eye, MT[group * LEVELS % len(MT)][:, d], SUB).then_inc(iv_tt, 1)
                        dve.wait_ge(iv_tt, nth(group, 0, d, 0, SMALL))
                        nc.vector.transpose(flat(T[:, d]), flat(Tt[:, d])).then_inc(iv_t, 1)
                        continue
                    dve.wait_ge(iv_q, iv_p_of(group, level, d))
                    for j, (dst, right, needed) in enumerate(((T, d == 1, level < LEVELS - 1), (Tt, d == 0, level >= SMALL))):
                        if not needed:
                            continue
                        v = side_of(dst[:, d], level, right)
                        got = aux[2 + d][:, j * 256:(j + 1) * 256].rearrange("p (m n s) -> p m n s", m=4, s=1 << level)
                        i = nc.vector.tensor_tensor(v, v, got, SUB)
                    i.then_inc(iv_t, 1)
                    if level < SMALL:
                        dve.wait_ge(iv_t, nth(group, level, d))
                        nc.vector.transpose(flat(Tt[:, d]), flat(T[:, d])).then_inc(iv_tt, 1)
                between(level)


        dn_qT, dn_kT = W(0, DN_H, S), W(2048, DN_H, S)
        dn_k, dn_v = W(4096, NT, DN_W), W(6144, NT, DN_W)
        gate = W(8192, NT, DN_W)
        yscT = W(10240, 8, S)
        G = 12288
        stage = [W(G + 1032 * i, 4, S + 2) for i in range(2)]
        conv = [W(G + 2064 + 1024 * i, 4, S) for i in range(2)]
        cgate = W(G + 4112, 4, S)
        abT = W(17408, S)[0:32]
        dn_vT = W(6144, DN_H, S)
        q_sq, k_sq = H(0, DN_H, S), H(2048, NT, DN_H, P)
        dn_AT = [R(2048, 2, 4, P), W(G, 2, 4, P)]
        dn_Tt = [R(1024, 2, 4, P), W(G + 2048, 2, 4, P)]
        QKT = [R(0, 2, 4, P), H(0, 2, 4, P)]
        Dm, DB = R(3072, 2, 4, P), R(4096, 2, 4, P)
        qTg = [H(1024, 2, 2, P), H(1536, 2, 2, P)]
        eg, vb1, vb2, kd1, vn1, vn2, S1 = (H(2048 + 512 * i, 2, 2, P) for i in range(7))
        dn_inv = [(W(G + 1024, 2, 4, P), Tt, W(G + 3072, 2, 4, P), [W(G + 4096, 2, 4, P), W(G + 5120, 2, 4, P), H(6144, 2, 4, P)])
                  for Tt in dn_Tt]
        o_tok = W(6144, NT, DN_H, P)
        o_sq = H(5632, NT, 2, P)
        y_tok = W(G + 2048, NT, DN_H, P)

        def stat(at, n=32):
            return st[:, 128 + at:128 + at + n].rearrange("p (t n) -> p t n", t=NT)

        abv, beta, xb, ax, soft, decay_g = stat(0, 64), stat(64), stat(96), stat(128), stat(160), stat(192)
        ea = st[:, 128 + 224:128 + 240]
        cum, ecum = stat(240, 64), stat(304, 64)
        dn_ms, dn_sd, dn_rn = stat(368), stat(400), stat(432)
        rq = stat(464, 16)
        brk, nbe, kds = stat(480), stat(512), stat(544)
        o_ss, o_ms, o_sd, o_r = (st[:, 128 + 576 + 16 * i:128 + 592 + 16 * i] for i in range(4))
        FIRST = (0, 1)
        N_SC = 6

        def conv_w(name, tile, tap):
            i = Q[name].start + 3 * tile + tap
            return par[:, i:i + 1]

        def per_dir(v, t, d, hp):
            return v[:, t, 8 * d + 2 * hp:8 * d + 2 * hp + 2]

        def pe_even(pe):
            pe.wait_ge(s_abw, 2)
            for k in range(KD):
                hT_ready(pe, "mix0")(k)
                cols = slice(32 * k, 32 * k + 32)
                out = aux[0][0:32, 0:S]
                nc.tensor.matmul(out, lhsT=ab_hi[:, cols], rhs=hT_hi[:, k, :], start=k == 0, stop=False)
                nc.tensor.matmul(out, lhsT=ab_hi[:, cols], rhs=hT_lo[:, k, :], start=False, stop=False)
                m = nc.tensor.matmul(out, lhsT=ab_lo[:, cols], rhs=hT_hi[:, k, :], start=False, stop=k == KD - 1)
            m.then_inc(s_ab, 1)
            pe.wait_ge(s_abv, 1)
            for t in range(NT):
                m = nc.tensor.transpose(aux[1][:, 32 * t:32 * t + 32], abT[:, t * P:(t + 1) * P], ident[0:32, 0:32])
            m.then_inc(s_ab, 1)
            with pe.Fori(0, 3) as turn:
                for c in range(2):
                    Gemm(pe, "ev_qkv", turn, (2, 16)).column_chunk(c)
            for c in range(2):
                Gemm(pe, "ev_gate").row_chunk(c, hT_tile)
            for l in range(2):
                pe_memory_keys(pe, l)
            for c in range(N_SC):
                Gemm(pe, "ev_sc").column_chunk(c)
            pe.wait_ge(s_silu, 6)
            wait_chunks_taken(pe, after("ev_sc"))
            pe.wait_ge(s_abv, 2)
            pe.wait_ge(s_mkT, 4)
            for b in range(8):
                for t in range(NT):
                    for i in range(2):
                        src = (dn_kT, dn_vT)[b // 4][:, 2 * (b % 4) + i, t * P:(t + 1) * P]
                        m = nc.tensor.transpose(bank[b][:, (2 * t + i) * P:(2 * t + i + 1) * P], src, ident)
                m.then_inc(s_kvt, 1)
            pe.wait_ge(s_g, 1)
            pe.wait_ge(s_kv_a, 2)
            for t in range(NT):
                for kind, masks_ in enumerate(((1, 3), (2, 0))):
                    for d in range(2):
                        at = t * 32 + kind * 16 + 8 * d
                        m = nc.tensor.matmul(bank[1][:, at:at + 8], lhsT=const_of("causal", masks_[d]),
                                             rhs=decay_g[:, t, 8 * d:8 * d + 8], start=True, stop=True)
            m.then_inc(s_cum, 1)
            pe.wait_ge(s_dsq, 1)
            for t in range(NT):
                for h in range(DN_H):
                    m = nc.tensor.matmul(bank[0][:, 8 * t + h:8 * t + h + 1], lhsT=q_sq[:, h, t * P:(t + 1) * P],
                                         rhs=ones_col, start=True, stop=True)
            m.then_inc(s_dss, 1)
            pe.wait_ge(s_stats, 1)
            pe.wait_ge(s_kv_a, 4)
            pe.wait_ge(s_kv_d, 4)
            pe_delta_pre(pe, 0, 0)
            pe_delta_pre(pe, 0, 1)
            pe.wait_ge(s_eg, 2)
            for hp in range(DN_GROUPS):
                def between(slot):
                    if hp and slot < 5:
                        pe_delta_tail(pe, hp - 1, slot)
                    if hp + 1 < DN_GROUPS and slot in PRE_SLOT:
                        pe_delta_pre(pe, hp + 1, PRE_SLOT.index(slot))

                pe_inv(pe, hp, dn_inv[hp % 2], between)
            for step in range(5):
                pe_delta_tail(pe, DN_GROUPS - 1, step)
            for b in range(4):
                pe.wait_ge(s_y, b // 2 + 1)
                for i in range(2):
                    for t in range(NT):
                        m = nc.tensor.transpose(aux[b][:, (2 * i + t) * P:(2 * i + t + 1) * P],
                                                y_tok[:, t, 2 * b + i, :], ident)
                m.then_inc(s_yt, 1)
            for c in range(4):
                Gemm(pe, "ev_out").row_chunk(c, hT_tile, k_ready=lambda k: pe.wait_ge(s_yT, min(k // 2 + 2, 5)) if c == 0 else None)

        DN_GROUPS = 4
        PRE_SLOT = (5, 9)

        def pre_banks(hp, d):
            return bank[4:8] if hp == 0 and d == 1 else bank[0:4]

        def pe_delta_pre(pe, hp, d):
            b = pre_banks(hp, d)
            if hp:
                if d == 0 and hp >= 2:
                    pe.wait_ge(s_os, hp - 1)
                pe.wait_ge(s_AT, 2 * hp + d)
                pe.wait_ge(s_eg, 2 * hp + d)
            for i in range(2):
                for t in range(NT):
                    h, cols = 2 * hp + i, slice((2 * i + t) * P, (2 * i + t + 1) * P)
                    tile = slice(t * P, (t + 1) * P)
                    g_col = decay_g[:, t, 8 * d + h:8 * d + h + 1].broadcast_to([P, P])
                    b_col = brk[:, t, 8 * d + h:8 * d + h + 1].broadcast_to([P, P])
                    for bk, lhsT, rhs in ((b[0], g_col, const_of("causal", 2 * d + 1)), (b[1], b_col, ident),
                                          (b[2], dn_kT[:, h, tile], dn_kT[:, h, tile]),
                                          (b[3], dn_kT[:, h, tile], dn_qT[:, h, tile])):
                        m = nc.tensor.matmul(bk[:, cols], lhsT=lhsT, rhs=rhs, start=True, stop=True)
            m.then_inc(s_pre, 1)

        def pe_delta_tail(pe, hp, step):
            Tt = dn_Tt[hp % 2]
            at = lambda d, i: slice((2 * d + i) * P, (2 * d + i + 1) * P)
            both = [(d, i) for d in range(2) for i in range(2)]
            if step == 0:
                nxt = min(hp + 1, DN_GROUPS - 1)
                pe.wait_ge(s_AT, 2 * nxt + 2)
                pe.wait_ge(s_eg, 2 * nxt + 2)
                pe.wait_ge(s_vb, hp + 1)
                pe.wait_ge(iv_t, nth(hp, LEVELS - 1, 1))
                for d, i in both:
                    m = nc.tensor.matmul(bank[0][:, at(d, i)], lhsT=Tt[:, d, 2 * i + FIRST[d]], rhs=vb1[:, d, i],
                                         start=True, stop=True)
                m.then_inc(s_vn1, 1)
            elif step == 1:
                pe.wait_ge(s_vn1s, hp + 1)
                for d, i in both:
                    m = nc.tensor.matmul(bank[1][:, at(d, i)], lhsT=kd1[:, d, i], rhs=vn1[:, d, i], start=True, stop=True)
                m.then_inc(s_S, 1)
            elif step == 2:
                pe.wait_ge(s_Ss, hp + 1)
                for d, i in both:
                    t2 = 1 - FIRST[d]
                    m = nc.tensor.matmul(bank[2][:, at(d, i)], lhsT=dn_kT[:, 2 * hp + i, t2 * P:(t2 + 1) * P],
                                         rhs=S1[:, d, i], start=True, stop=True)
                m.then_inc(s_kS, 1)
            elif step == 3:
                pe.wait_ge(s_R, hp + 1)
                for d, i in both:
                    m = nc.tensor.matmul(bank[3][:, at(d, i)], lhsT=Tt[:, d, 2 * i + 1 - FIRST[d]], rhs=vb2[:, d, i],
                                         start=True, stop=True)
                m.then_inc(s_vn2, 1)
            else:
                pe.wait_ge(s_vn2s, hp + 1)
                pe.wait_ge(s_qtg, 2 * hp + 2)
                for t in range(NT):
                    d1, d2 = (0, 1) if t == 0 else (1, 0)
                    for i in range(2):
                        out = bank[0][:, (2 * t + i) * P:(2 * t + i + 1) * P]
                        qkt = QKT[hp % 2]
                        nc.tensor.matmul(out, lhsT=qkt[:, d1, 2 * i + t], rhs=vn1[:, d1, i], start=True, stop=False)
                        nc.tensor.matmul(out, lhsT=qkt[:, d2, 2 * i + t], rhs=vn2[:, d2, i], start=False, stop=False)
                        m = nc.tensor.matmul(out, lhsT=qTg[hp % 2][:, d2, i], rhs=S1[:, d2, i], start=False, stop=True)
                m.then_inc(s_o, 1)

        def act_even(act):
            nc.scalar.activation(ab_hi[:, :], par[:, Q["ab_w"]], ACT.Copy).then_inc(s_abw, 1)
            act.wait_ge(s_abv, 2)
            nc.scalar.activation(beta, abv[:, :, 0:16], ACT.Sigmoid)
            act.wait_ge(s_ax, 1)
            act_step(nc.scalar.activation(soft, ax, ACT.Exp, scale=-1.0))
            nc.scalar.activation(ea, par[:, Q["a_log"]], ACT.Exp)
            nc.scalar.activation(soft, soft, ACT.Ln, bias=1.0).then_inc(s_sp, 1)

            def silu(c):
                act.wait_ge(s_cv, c + 1)
                dst = (dn_qT, dn_kT, dn_vT)[c // 2][:, 4 * (c % 2):4 * (c % 2) + 4, :]
                nc.scalar.activation(dst, conv[c % 2], ACT.Silu).then_inc(s_silu, 1)

            for c in range(6):
                banks, taken = chunk_banks("ev_qkv", c)
                hi_upto(act, chunk_done("ev_qkv", c) + AHEAD)
                act.wait_ge(s_used, chunk_done("ev_qkv", c))
                if c >= 2:
                    act.wait_ge(s_cv, c - 1)
                for b in range(2):
                    nc.scalar.activation(stage[c % 2][:, 2 * b:2 * b + 2, 1:S + 1],
                                         banks[b][:, :].rearrange("p (h s) -> p h s", s=S), ACT.Copy).then_inc(taken, 1)
                if c:
                    silu(c - 1)
            silu(5)
            for c in range(2):
                banks, taken = chunk_banks("ev_gate", c)
                hi_upto(act, chunk_done("ev_gate", c) + AHEAD)
                act.wait_ge(s_used, chunk_done("ev_gate", c))
                for t in range(NT):
                    nc.scalar.activation(gate[:, t, c * 512:(c + 1) * 512], banks[t][:, :], ACT.Silu).then_inc(taken, 1)
                if c == 0:
                    for l in range(2):
                        act_memory_root(act, l)
            for half in range(2):
                c = 3 * half
                banks, taken = chunk_banks("ev_sc", c)
                hi_upto(act, chunk_done("ev_sc", c) + AHEAD)
                act.wait_ge(s_used, chunk_done("ev_sc", c))
                if half:
                    wait_chunks_taken(act, starts["ev_sc"][0] + 2)
                if not half:
                    for l in range(2):
                        act_memory_keys(act, l)
                for b in range(2):
                    nc.scalar.activation(cgate[:, 2 * b:2 * b + 2, :], banks[b][:, :].rearrange("p (h s) -> p h s", s=S),
                                         ACT.Copy).then_inc(taken, 1)
                for i in (c + 1, c + 2):
                    hi_upto(act, min(chunk_done("ev_sc", i) + AHEAD, starts["ev_out"][1]))
            act.wait_ge(s_used, chunk_done("ev_sc", 5))
            nc.scalar.activation(q_sq, dn_qT, ACT.Square).then_inc(s_dsq, 1)
            for b in range(4):
                act.wait_ge(s_kvt, b + 1)
                dst = dn_k.rearrange("p t (h e) -> p t h e", e=P)[:, :, 2 * b:2 * b + 2, :]
                nc.scalar.activation(dst, bank[b][:, :].rearrange("p (t h e) -> p t h e", t=NT, e=P),
                                     ACT.Copy).then_inc(s_kv_a, 1)
            act.wait_ge(s_cumv, 1)
            nc.scalar.activation(ecum, cum, ACT.Exp).then_inc(s_dE, 1)
            act.wait_ge(s_dms, 1)
            nc.scalar.activation(dn_sd, dn_ms, ACT.Sqrt).then_inc(s_dsd, 1)
            act_delta_pre(act, 0, 0)
            act_delta_pre(act, 0, 1)
            for hp in range(DN_GROUPS):
                def between(level):
                    if hp and level <= 2:
                        act_delta_tail(act, hp - 1, range(2) if level == 1 else (2,))
                    if hp + 1 < DN_GROUPS and level in (4, 5):
                        act_delta_pre(act, hp + 1, (4, 5).index(level))
                    if hp + 1 == DN_GROUPS and level == 4:
                        act.wait_ge(s_o, DN_GROUPS - 1)
                        hi_upto(act, starts["ev_out"][1] + AHEAD)

                act_inv(act, hp, dn_inv[hp % 2], between)
            act_delta_tail(act, DN_GROUPS - 1, range(3))
            act.wait_ge(s_oms, 1)
            nc.scalar.activation(o_sd, o_ms, ACT.Sqrt).then_inc(s_osd, 1)
            act.wait_ge(s_o, 4)
            nc.scalar.activation(hT_hi[:, 8:16, :], yscT, ACT.Copy).then_inc(s_ysp, 1)
            for b in range(4):
                act.wait_ge(s_yt, b + 1)
                nc.scalar.activation(hT_hi[:, 2 * b:2 * b + 2, :], aux[b][:, :].rearrange("p (h s) -> p h s", s=S),
                                     ACT.Copy).then_inc(s_ysp, 1)
            for c in range(4):
                hi_upto(act, chunk_done("ev_out", c) + AHEAD)

        def act_delta_pre(act, hp, d):
            act.wait_ge(s_diff, 2 * hp + d + 1)
            nc.scalar.activation(Dm[:, d], Dm[:, d], ACT.Exp).then_inc(s_D, 1)
            if hp:
                act.wait_ge(s_qtg, 2 * hp)
            src = pre_banks(hp, d)[0][:, :].rearrange("p (i t s) -> p i t s", t=NT, s=P)[:, :, 1 - FIRST[d], :]
            nc.scalar.activation(eg[:, d], src, ACT.Exp).then_inc(s_eg, 1)

        def act_delta_tail(act, hp, steps):
            for step in steps:
                ready, src, dst, done = ((s_vn1, 0, vn1, s_vn1s), (s_S, 1, S1, s_Ss), (s_vn2, 3, vn2, s_vn2s))[step]
                act.wait_ge(ready, hp + 1)
                nc.scalar.activation(dst.rearrange("p d i e -> p (d i) e"), four(bank[src]), ACT.Copy).then_inc(done, 1)

        def dve_conv(dve, src, dst, name, tile0, done):
            for i in range(4):
                m = nc.vector.tensor_scalar(dst[:, i], src[:, i, 1:S + 1], conv_w(name, tile0 + i, 1), None, MULT)
            dve_step(m)
            for tap, at in ((0, 0), (2, 2)):
                for i in range(4):
                    m = nc.vector.scalar_tensor_tensor(out=dst[:, i], in0=src[:, i, at:at + S],
                                                       scalar=conv_w(name, tile0 + i, tap), in1=dst[:, i],
                                                       op0=MULT, op1=ADD)
                if tap == 0:
                    dve_step(m)
            if done is None:
                dve_step(m)
            else:
                m.then_inc(done, 1)

        def dve_even(dve):
            for s_ in stage:
                nc.vector.memset(s_[:, :, 0:1], 0.0)
                m = nc.vector.memset(s_[:, :, S + 1:S + 2], 0.0)
            dve_step(m)
            dve.wait_ge(s_abw, 1)
            nc.vector.tensor_tensor(ab_lo[:, :], par[:, Q["ab_w"]], f32(ab_hi[:, :]), SUB).then_inc(s_abw, 1)
            dve.wait_ge(s_ab, 1)
            nc.vector.tensor_copy(abT, aux[0][0:32, 0:S]).then_inc(s_abv, 1)
            dve.wait_ge(s_ab, 2)
            nc.vector.tensor_copy(abv, aux[1][:, 0:64].rearrange("p (t n) -> p t n", t=NT)).then_inc(s_abv, 1)
            dve.wait_ge(s_abv, 2)
            dt = par[:, Q["dt_bias"]].unsqueeze(1).broadcast_to([P, NT, 16])
            dve_step(nc.vector.tensor_tensor(xb, abv[:, :, 16:32], dt, ADD))
            nc.vector.scalar_tensor_tensor(out=ax, in0=xb, scalar=-1.0, in1=xb, op0=MULT, op1=MAX).then_inc(s_ax, 1)
            dve.wait_ge(s_sp, 1)
            dve_step(nc.vector.scalar_tensor_tensor(out=xb, in0=xb, scalar=0.0, in1=soft, op0=MAX, op1=ADD))
            nc.vector.scalar_tensor_tensor(out=decay_g, in0=xb, scalar=-1.0, in1=ea.unsqueeze(1).broadcast_to([P, NT, 16]),
                                           op0=MULT, op1=MULT).then_inc(s_g, 1)
            for c in range(6):
                _, taken = chunk_banks("ev_qkv", c)
                lo_upto(dve, chunk_done("ev_qkv", c) + AHEAD)
                dve.wait_ge(taken, 2 * ((starts["ev_qkv"][0] + c) // 2 + 1))
                if c >= 2:
                    dve.wait_ge(s_silu, c - 1)
                dve_conv(dve, stage[c % 2], conv[c % 2], "dn_conv", 4 * c, s_cv)
            for c in range(2):
                lo_upto(dve, chunk_done("ev_gate", c) + AHEAD)
                for l in range(2):
                    (dve_memory_squares, dve_memory_keys)[c](dve, l)
            wait_chunks_taken(dve, after("ev_gate"))
            gain = par[:, Q["dn_norm"]].unsqueeze(1).broadcast_to([P, NT * DN_H, P])
            gv = gate.rearrange("p t (h e) -> p (t h) e", e=P)
            nc.vector.tensor_tensor(gv, gv, gain, MULT)
            dve.wait_ge(s_silu, 6)
            for half in range(2):
                c = 3 * half + 1
                banks, taken = chunk_banks("ev_sc", c)
                lo_upto(dve, chunk_done("ev_sc", c - 1) + AHEAD)
                lo_upto(dve, chunk_done("ev_sc", c) + AHEAD)
                wait_chunks_taken(dve, starts["ev_sc"][0] + c)
                dve.wait_ge(s_used, chunk_done("ev_sc", c))
                for b in range(2):
                    nc.vector.tensor_tensor(stage[0][:, 2 * b:2 * b + 2, 1:S + 1], cgate[:, 2 * b:2 * b + 2, :],
                                            banks[b][:, :].rearrange("p (h s) -> p h s", s=S), MULT).then_inc(taken, 1)
                dve.wait_ge(taken, 2 * ((starts["ev_sc"][0] + c) // 2 + 1))
                dve_conv(dve, stage[0], conv[0], "sc_conv", 4 * half, None)
                banks, taken = chunk_banks("ev_sc", c + 1)
                lo_upto(dve, min(chunk_done("ev_sc", c + 1) + AHEAD, starts["ev_out"][1]))
                dve.wait_ge(s_used, chunk_done("ev_sc", c + 1))
                for b in range(2):
                    nc.vector.tensor_tensor(yscT[:, 4 * half + 2 * b:4 * half + 2 * b + 2, :],
                                            conv[0][:, 2 * b:2 * b + 2, :],
                                            banks[b][:, :].rearrange("p (h s) -> p h s", s=S), MULT).then_inc(taken, 1)
            dve.wait_ge(s_kvt, 8)
            for b in range(4):
                dst = dn_v.rearrange("p t (h e) -> p t h e", e=P)[:, :, 2 * b:2 * b + 2, :]
                nc.vector.tensor_copy(dst, bank[4 + b][:, :].rearrange("p (t h e) -> p t h e", t=NT, e=P)).then_inc(s_kv_d, 1)
            dve.wait_ge(s_cum, 1)
            nc.vector.tensor_copy(cum, bank[1][:, 0:64].rearrange("p (t n) -> p t n", t=NT)).then_inc(s_cumv, 1)
            dve.wait_ge(s_kv_a, 4)
            kv = dn_k.rearrange("p t (h e) -> p t h e", e=P)
            dve_step(nc.vector.tensor_tensor(k_sq, kv, kv, MULT))
            dve_step(nc.vector.reduce_sum(dn_ms[:, :, 8:16], k_sq, AX_X))
            nc.vector.tensor_scalar(dn_ms[:, :, 8:16], dn_ms[:, :, 8:16], 1e-6, None, ADD)
            dve.wait_ge(s_dss, 1)
            nc.vector.tensor_scalar(dn_ms[:, :, 0:8], bank[0][:, 0:16].rearrange("p (t n) -> p t n", t=NT), 1e-6, None, ADD).then_inc(s_dms, 1)
            dve.wait_ge(s_dsd, 1)
            dve_step(nc.vector.reciprocal(dn_rn, dn_sd))
            nc.vector.tensor_scalar(rq, dn_rn[:, :, 0:8], HEAD_SCALE, None, MULT)
            rk2 = dn_rn[:, :, 8:16].unsqueeze(2).broadcast_to([P, NT, 2, 8])
            two = lambda v: v.rearrange("p t (d h) -> p t d h", d=2)
            dve_step(nc.vector.tensor_tensor(two(brk), two(beta), rk2, MULT))
            dve.wait_ge(s_dE, 1)
            nc.vector.scalar_tensor_tensor(out=nbe, in0=brk, scalar=-1.0, in1=ecum[:, :, 0:16], op0=MULT, op1=MULT)
            nc.vector.tensor_tensor(two(kds), two(ecum[:, :, 16:32]), rk2, MULT).then_inc(s_stats, 1)
            dve.wait_ge(s_stats, 1)
            for d in range(2):
                dve_delta_diff(dve, 0, d)
                dve_delta_masks(dve, 0, d)
            for hp in range(DN_GROUPS):
                def between(level):
                    if hp and level == 1:
                        dve_delta_R(dve, hp - 1)
                    if hp and level == 2:
                        dve_delta_out(dve, hp - 1)
                    if hp + 1 < DN_GROUPS and level in (3, 5):
                        dve_delta_diff(dve, hp + 1, (3, 5).index(level))
                    if hp + 1 < DN_GROUPS and level in (4, 5):
                        dve_delta_masks(dve, hp + 1, (4, 5).index(level))
                    if hp + 1 == DN_GROUPS and level == 4:
                        lo_upto(dve, starts["ev_out"][1] + AHEAD)

                dve_inv(dve, hp, dn_inv[hp % 2], between)
            dve_delta_R(dve, DN_GROUPS - 1)
            dve_delta_out(dve, DN_GROUPS - 1)
            nc.vector.tensor_scalar(o_ms, o_ss, 1.0 / P, RMS_EPS, MULT, ADD).then_inc(s_oms, 1)
            dve.wait_ge(s_osd, 1)
            dve_step(nc.vector.reciprocal(o_r, o_sd))
            for b in range(2):
                own = slice(4 * b, 4 * b + 4)
                for t in range(NT):
                    m = nc.vector.tensor_tensor(y_tok[:, t, own, :], o_tok[:, t, own, :],
                                                lanes(o_r[:, 8 * t + 4 * b:8 * t + 4 * b + 4], P), MULT)
                dve_step(m)
                g4 = gate.rearrange("p t (h e) -> p t h e", e=P)[:, :, own, :]
                nc.vector.tensor_tensor(y_tok[:, :, own, :], y_tok[:, :, own, :], g4, MULT).then_inc(s_y, 1)
            dve.wait_ge(s_ysp, 1)
            nc.vector.tensor_tensor(hT_lo[:, 8:16, :], yscT, f32(hT_hi[:, 8:16, :]), SUB).then_inc(s_yT, 1)
            for b in range(4):
                dve.wait_ge(s_ysp, b + 2)
                nc.vector.tensor_tensor(hT_lo[:, 2 * b:2 * b + 2, :], aux[b][:, :].rearrange("p (h s) -> p h s", s=S),
                                        f32(hT_hi[:, 2 * b:2 * b + 2, :]), SUB).then_inc(s_yT, 1)
            for c in range(4):
                dve_add_to_x(dve, "ev_out", c)

        def each_of(hp, d):
            return [(2 * i + t, t, 8 * d + 2 * hp + i, 8 + 2 * hp + i) for i in range(2) for t in range(NT)]

        def dve_delta_diff(dve, hp, d):
            b = pre_banks(hp, d)
            dve.wait_ge(s_pre, 2 * hp + d + 1)
            for m, t, j, _ in each_of(hp, d):
                i_ = nc.vector.scalar_tensor_tensor(out=Dm[:, d, m], in0=b[0][:, m * P:(m + 1) * P],
                                                    scalar=cum[:, t, j:j + 1], in1=const_of("neg", d), op0=SUB, op1=ADD)
            i_.then_inc(s_diff, 1)

        def dve_delta_masks(dve, hp, d):
            b = pre_banks(hp, d)
            dve.wait_ge(s_D, 2 * hp + d + 1)
            dve_step(nc.vector.tensor_tensor(DB[:, d], Dm[:, d], four(b[1]), MULT))
            for m, t, _, kh in each_of(hp, d):
                nc.vector.scalar_tensor_tensor(out=QKT[hp % 2][:, d, m], in0=b[3][:, m * P:(m + 1) * P],
                                               scalar=dn_rn[:, t, kh:kh + 1], in1=Dm[:, d, m], op0=MULT, op1=MULT)
            for m, t, _, kh in each_of(hp, d):
                i_ = nc.vector.scalar_tensor_tensor(out=dn_AT[hp % 2][:, d, m], in0=b[2][:, m * P:(m + 1) * P],
                                                    scalar=dn_rn[:, t, kh:kh + 1], in1=DB[:, d, m], op0=MULT, op1=MULT)
            i_.then_inc(s_AT, 1)

        def dve_delta_R(dve, hp):
            dve.wait_ge(s_kS, hp + 1)
            dve.wait_ge(s_vb, hp + 1)
            for d in range(2):
                for i in range(2):
                    j = 8 * d + 2 * hp + i
                    m = nc.vector.scalar_tensor_tensor(out=vb2[:, d, i], in0=bank[2][:, (2 * d + i) * P:(2 * d + i + 1) * P],
                                                       scalar=nbe[:, 1 - FIRST[d], j:j + 1], in1=vb2[:, d, i],
                                                       op0=MULT, op1=ADD)
            m.then_inc(s_R, 1)

        def dve_delta_out(dve, hp):
            dve.wait_ge(s_o, hp + 1)
            for t in range(NT):
                m = nc.vector.tensor_tensor(o_tok[:, t, 2 * hp:2 * hp + 2, :],
                                            bank[0][:, t * 256:(t + 1) * 256].rearrange("p (i e) -> p i e", e=P),
                                            lanes(rq[:, t, 2 * hp:2 * hp + 2], P), MULT)
            m.then_inc(s_os, 1)
            dve.wait_ge(s_os, hp + 1)
            own = slice(2 * hp, 2 * hp + 2)
            dve_step(nc.vector.tensor_tensor(o_sq, o_tok[:, :, own, :], o_tok[:, :, own, :], MULT))
            dve_step(nc.vector.reduce_sum(o_ss.rearrange("p (t h) -> p t h", t=NT)[:, :, own], o_sq, AX_X))

        def pool_delta_values(pool, hp):
            if hp:
                pool.wait_ge(s_o, hp)
            for d in range(2):
                t1, t2 = FIRST[d], 1 - FIRST[d]
                for dst, src, t, w in ((vb1, dn_v, t1, beta), (vb2, dn_v, t2, beta), (kd1, dn_k, t1, kds)):
                    v = src[:, t, 2 * hp * P:(2 * hp + 2) * P].rearrange("p (i e) -> p i e", e=P)
                    m = nc.gpsimd.tensor_tensor(dst[:, d], v, lanes(per_dir(w, t, d, hp), P), MULT)
            m.then_inc(s_vb, 1)

        def pool_delta_pre(pool, hp, d):
            t2 = 1 - FIRST[d]
            pool.wait_ge(s_AT, 2 * hp + d + 1)
            AT = dn_AT[hp % 2]
            for level in range(2):
                pool_inv_mask(pool, hp, [AT[:, 0], AT[:, 1]], dn_inv[hp % 2], level, d)
            pool.wait_ge(s_eg, 2 * hp + d + 1)
            nc.gpsimd.tensor_tensor(qTg[hp % 2][:, d], dn_qT[:, 2 * hp:2 * hp + 2, t2 * P:(t2 + 1) * P], eg[:, d],
                                    MULT).then_inc(s_qtg, 1)

        def pool_even(pool):
            pool.wait_ge(s_stats, 1)
            for d in range(2):
                pool_delta_pre(pool, 0, d)
            for hp in range(DN_GROUPS):
                AT = dn_AT[hp % 2]
                for level in range(2, LEVELS):
                    for d in range(2):
                        pool_inv_mask(pool, hp, [AT[:, 0], AT[:, 1]], dn_inv[hp % 2], level, d)
                    if level == 4:
                        pool_delta_values(pool, hp)
                if hp + 1 < DN_GROUPS:
                    for d in range(2):
                        pool_delta_pre(pool, hp + 1, d)


        NB = N_BUCKETS + 1
        btab = W(16384, DSA_G, 512)[0:NB]
        rel = st[0:NB, 112:112 + DSA_H]
        brow = W(2048, DSA_G, 512)[0:DSA_HG]

        def pe_bias(pe):
            pe.wait_ge(s_bt_in, 32)
            pe.wait_ge(s_neg, 1)
            for g in range(DSA_G):
                nc.tensor.matmul(aux[g][0:DSA_HG, :], lhsT=rel[:, g * DSA_HG:(g + 1) * DSA_HG],
                                 rhs=btab[:, g, :], start=True, stop=True).then_inc(s_bias_m, 1)

        def act_bias(act):
            act.dma_start(rel[0:N_BUCKETS], rel_bias).then_inc(s_bt_in, 16)
            act.dma_start(btab, bias_table.rearrange("b (g n) -> b g n", g=DSA_G)).then_inc(s_bt_in, 16)
            for g in range(DSA_G):
                act.wait_ge(s_bias_m, g + 1)
                nc.scalar.activation(brow[:, g, :], aux[g][0:DSA_HG, :], ACT.Copy).then_inc(s_bias_s, 1)

        def act_bias_out(act, l):
            if l == 0:
                act.wait_ge(s_bias_s, DSA_G)
                for g in range(DSA_G):
                    act.dma_start(bias_rows[g * DSA_HG:(g + 1) * DSA_HG],
                                  brow[:, g, :].unsqueeze(1).broadcast_to([DSA_HG, P, 512])).then_inc(s_bias_out, 16)

        oq, ok, ov = W(0, DSA_H, S), W(3072, NT, DSA_H * P), W(6144, NT, DSA_H * P)
        oq_sq = W(15120, 2, 4, S)
        ok_sq = W(17168, NT, 512)
        okT = W(13056, DSA_H, S)
        osc = W(16128, 2, DSA_G, S)
        bias, oPT = H(0, NT, DSA_H, S), H(6144, 2, 6, P)
        ycT = mem_kT[0][:, :, :]
        ost = lambda i: st[:, 128 + 24 * i:152 + 24 * i]
        oms, osd, orq0, orq, kss, kms, ksd, krs = (ost(i) for i in range(8))
        omx, onm, osum, ors = (st[:, 320 + 2 * i:322 + 2 * i] for i in range(4))
        gca = st[:, 328:329]
        ITEMS = [(hg, t) for hg in range(DSA_HG) for t in range(NT)]

        def taken_of(eng, name, c):
            g = starts[name][0] + c
            eng.wait_ge(s_taken[g % 2], 2 * (g // 2 + 1))

        def pe_window(pe):
            pe_hT(pe, "mix1")
            q, k, v = (Gemm(pe, n) for n in ("od_q", "od_k", "od_v"))

            def ssq(c):
                taken_of(pe, "od_q", c)
                for t in range(NT):
                    for i in range(4):
                        at = t * DSA_H + 4 * c + i
                        m = nc.tensor.matmul(aux[0][:, at:at + 1], lhsT=oq_sq[:, c % 2, i, t * P:(t + 1) * P],
                                             rhs=ones_col, start=True, stop=True)
                m.then_inc(s_oss, 1)

            q.column_chunk(0)
            q.column_chunk(1)
            ssq(0)
            q.column_chunk(2)
            ssq(1)
            k.row_chunk(0, hT_tile)
            ssq(2)
            k.row_chunk(1, hT_tile)
            k.row_chunk(2, hT_tile)
            for c in range(3):
                v.row_chunk(c, hT_tile)
            rw = Gemm(pe, "od_rw")
            for c in range(4):
                rw.column_chunk(c, tiles=3 if c == 3 else 4)
            pe.wait_ge(s_ok, 1)
            pe.wait_ge(s_oms0, 1)
            for b in range(6):
                if b >= 4:
                    pe.wait_ge((s_okT_a, s_okT_d)[b % 2], (b - 4) // 2 + 1)
                for i in range(2):
                    for t in range(NT):
                        h = 2 * b + i
                        m = nc.tensor.transpose(aux[b % 4][:, (2 * i + t) * P:(2 * i + t + 1) * P],
                                                ok[:, t, h * P:(h + 1) * P], ident)
                m.then_inc(s_okt, 1)
            pe.wait_ge(s_okT_a, 3)
            pe.wait_ge(s_okT_d, 3)
            wait_chunks_taken(pe, after("od_rw"))

            def scores(n):
                hg, t = ITEMS[n]
                p = n % 2
                if n >= 2:
                    pe.wait_ge(s_optT, n - 1)
                for g in range(DSA_G):
                    h = g * DSA_HG + hg
                    m = nc.tensor.matmul(aux[2 * p + g // 2][:, (g % 2) * S:(g % 2 + 1) * S],
                                         lhsT=oq[:, h, t * P:(t + 1) * P], rhs=okT[:, h, :], start=True, stop=True)
                m.then_inc(s_ol, 1)

            scores(0)
            for n, (hg, t) in enumerate(ITEMS):
                p = n % 2
                if n + 1 < len(ITEMS):
                    scores(n + 1)
                if n == 0:
                    pe.wait_ge(s_kksq, 1)
                    for b in range(2):
                        for i in range(2):
                            m = nc.tensor.matmul(bank[2 + b][:, i * S:(i + 1) * S], lhsT=const[:, C["halves"]],
                                                 rhs=ksqT[:, 2 * b + i, :], start=True, stop=True)
                        m.then_inc(s_kkm, 1)
                pe.wait_ge(s_op, n + 1)
                for g in range(DSA_G):
                    for mt in range(NT):
                        j = 2 * g + mt
                        m = nc.tensor.transpose(aux[2 * p + j // 4][:, (j % 4) * P:(j % 4 + 1) * P],
                                                osc[:, p, g, mt * P:(mt + 1) * P], ident)
                m.then_inc(s_opt, 1)
                pe.wait_ge(s_optT, n + 1)
                if n >= 2:
                    pe.wait_ge(s_oyc, n - 1)
                for g in range(DSA_G):
                    for mt in range(NT):
                        h = g * DSA_HG + hg
                        m = nc.tensor.matmul(bank[p][:, 0:P], lhsT=ov[:, mt, h * P:(h + 1) * P],
                                             rhs=oPT[:, p, 2 * g + mt, :], start=g + mt == 0, stop=g + mt == 3)
                m.then_inc(s_opv, 1)

        def act_window(act):
            act.wait_ge(s_gqk, 2)
            for c in range(3):
                banks, taken = chunk_banks("od_q", c)
                hi_upto(act, chunk_done("od_q", c) + AHEAD)
                act.wait_ge(s_used, chunk_done("od_q", c))
                if c == 2:
                    act.wait_ge(s_oss, 1)
                for b in range(2):
                    v = banks[b][:, :].rearrange("p (h s) -> p h s", s=S)
                    nc.scalar.activation(oq_sq[:, c % 2, 2 * b:2 * b + 2, :], v, ACT.Square)
                    nc.scalar.activation(oq[:, 4 * c + 2 * b:4 * c + 2 * b + 2, :], v, ACT.Copy, scale=gca).then_inc(taken, 1)
            for name, dst in (("od_k", ok), ("od_v", ov)):
                for c in range(3):
                    take_row_chunk(act, name, c, lambda t: dst[:, t, c * 512:(c + 1) * 512])
                    if name == "od_v" and c == 0:
                        act.wait_ge(s_oms0, 2)
                        nc.scalar.activation(osd, oms, ACT.Sqrt)
                        nc.scalar.activation(ksd, kms, ACT.Sqrt).then_inc(s_osd0, 1)
            act.dma_start(ln_wb.rearrange("p a n -> p (a n)"), wide[:, 2560:3584]).then_inc(s_wide, 16)
            act.wait_ge(s_rw, 1)
            for c in range(4):
                banks, taken = chunk_banks("od_rw", c)
                hi_upto(act, min(chunk_done("od_rw", c) + AHEAD, starts["od_out"][1]))
                act.wait_ge(s_used, chunk_done("od_rw", c))
                if c >= 2:
                    act.wait_ge(s_rw, c)
                for b in range(2):
                    n = 1 if (c, b) == (3, 1) else 2
                    nc.scalar.activation(rstage[c % 2][:, 2 * b:2 * b + n, 1:S + 1],
                                         banks[b][:, 0:n * S].rearrange("p (h s) -> p h s", s=S), ACT.Copy).then_inc(taken, 1)
            for t in range(NT):
                src = bass.AP(bias_rows.tensor, S - 1 - P * t, [[511, P], [P * 512, DSA_H], [1, S]])
                act.dma_start(bias[:, t], src).then_inc(s_bias_in, 16)
            act.wait_ge(s_rw, 5)
            nc.scalar.activation(wagT[:, 0, :], wagT[:, 0, :], ACT.Tanh)
            nc.scalar.activation(wagT[:, 2, :], wagT[:, 2, :], ACT.Sigmoid).then_inc(s_rtanh, 1)
            for b in range(0, 6, 2):
                act.wait_ge(s_okt, b + 1)
                nc.scalar.activation(okT[:, 2 * b:2 * b + 2, :], aux[b % 4][:, :].rearrange("p (h s) -> p h s", s=S),
                                     ACT.Copy).then_inc(s_okT_a, 1)
            act.wait_ge(s_kk0, 1)
            nc.scalar.activation(ksqT, kk0T, ACT.Square).then_inc(s_kksq, 1)
            def exps(n):
                p = n % 2
                act.wait_ge(s_onm, n + 1)
                v = osc[:, p].rearrange("p g m -> p (g m)")
                nc.scalar.activation(v, v, ACT.Exp, bias=onm[:, p:p + 1], accum_out=osum[:, p:p + 1]).then_inc(s_oexp, 1)

            exps(0)
            for n, (hg, t) in enumerate(ITEMS):
                p = n % 2
                if n == 3:
                    act.wait_ge(s_kkms, 1)
                    nc.scalar.activation(kmsT, kmsT, ACT.Sqrt).then_inc(s_kksd, 1)
                act.wait_ge(s_opt, n + 1)
                nc.scalar.activation(oPT[:, p, 0:4, :], four(aux[2 * p]), ACT.Copy)
                nc.scalar.activation(oPT[:, p, 4:6, :], aux[2 * p + 1][:, 0:256].rearrange("p (m s) -> p m s", s=P),
                                     ACT.Copy).then_inc(s_optT, 1)
                if n + 1 < len(ITEMS):
                    exps(n + 1)
                act.wait_ge(s_opv, n + 1)
                nc.scalar.activation(ycT[:, hg, t * P:(t + 1) * P], bank[p][:, 0:P], ACT.Copy).then_inc(s_oyc, 1)

        def dve_window(dve):
            nc.vector.tensor_tensor(gca, par[:, Q["ca_qn"]], par[:, Q["ca_kn"]], MULT).then_inc(s_gqk, 1)
            nc.vector.tensor_scalar(mid_w, par[:, Q["rw_mu"]], -1.0, 1.0, MULT, ADD)
            nc.vector.tensor_scalar(side_w, par[:, Q["rw_mu"]], 0.5, None, MULT)
            nc.vector.tensor_scalar(one_ka, par[:, Q["rw_ka"]], -1.0, 1.0, MULT, ADD)
            for s_ in rstage:
                nc.vector.memset(s_[:, :, 0:1], 0.0)
                m = nc.vector.memset(s_[:, :, S + 1:S + 2], 0.0)
            m.then_inc(s_rw, 1)
            for c in range(3):
                lo_upto(dve, chunk_done("od_q", c) + AHEAD)
            for c in range(3):
                lo_upto(dve, chunk_done("od_k", c) + AHEAD)
                taken_of(dve, "od_k", c)
                dve_step(nc.vector.tensor_tensor(ok_sq, ok[:, :, c * 512:(c + 1) * 512], ok[:, :, c * 512:(c + 1) * 512], MULT))
                for t in range(NT):
                    m = nc.vector.reduce_sum(kss[:, t * DSA_H + 4 * c:t * DSA_H + 4 * c + 4],
                                             ok_sq[:, t, :].rearrange("p (h e) -> p h e", e=P), AX_X)
                dve_step(m)
            dve.wait_ge(s_oss, 3)
            nc.vector.tensor_scalar(oms, aux[0][:, 0:24], 1.0 / P, RMS_EPS, MULT, ADD).then_inc(s_oms0, 1)
            nc.vector.tensor_scalar(kms, kss, 1.0 / P, RMS_EPS, MULT, ADD).then_inc(s_oms0, 1)
            lo_upto(dve, chunk_done("od_v", 0) + AHEAD)
            dve.wait_ge(s_osd0, 1)
            dve_step(nc.vector.reciprocal(orq0, osd))
            dve_step(nc.vector.tensor_scalar(orq, orq0, HEAD_SCALE, None, MULT))
            dve_step(nc.vector.reciprocal(krs, ksd))
            kv = ok.rearrange("p t (h e) -> p (t h) e", e=P)
            nc.vector.tensor_tensor(kv, kv, lanes(krs, P), MULT).then_inc(s_ok, 1)
            for c in range(1, 3):
                lo_upto(dve, chunk_done("od_v", c) + AHEAD)
            dve.wait_ge(s_rw, 1)
            for c, dst in enumerate((rT, krT, vrT, wagT)):
                lo_upto(dve, min(chunk_done("od_rw", c) + AHEAD, starts["od_out"][1]))
                taken_of(dve, "od_rw", c)
                dve_shift(dve, rstage[c % 2], dst, 4 * c, 3 if c == 3 else 4)
            for f in range(RW_F):
                j = Q["rw_kk"].start + f
                m = nc.vector.tensor_scalar(kk0T[:, f, :], krT[:, f, :], par[:, j:j + 1], None, MULT)
            m.then_inc(s_kk0, 1)
            dve.wait_ge(s_rw, 5)
            for b in range(1, 6, 2):
                dve.wait_ge(s_okt, b + 1)
                nc.vector.tensor_copy(okT[:, 2 * b:2 * b + 2, :], aux[b % 4][:, :].rearrange("p (h s) -> p h s", s=S)).then_inc(s_okT_d, 1)
            dve.wait_ge(s_bias_in, 32)

            def scores(n):
                hg, t = ITEMS[n]
                p = n % 2
                dve.wait_ge(s_ol, n + 1)
                if n >= 2:
                    dve.wait_ge(s_opt, n - 1)
                for g in range(DSA_G):
                    h = g * DSA_HG + hg
                    m = nc.vector.scalar_tensor_tensor(out=osc[:, p, g, :], in0=aux[2 * p + g // 2][:, (g % 2) * S:(g % 2 + 1) * S],
                                                       scalar=orq[:, t * DSA_H + h:t * DSA_H + h + 1], in1=bias[:, t, h, :],
                                                       op0=MULT, op1=ADD)
                dve_step(m)
                dve_step(nc.vector.reduce_max(omx[:, p:p + 1], osc[:, p].rearrange("p g m -> p (g m)"), AX_X))
                nc.vector.tensor_scalar(onm[:, p:p + 1], omx[:, p:p + 1], -1.0, None, MULT).then_inc(s_onm, 1)

            scores(0)
            for n, (hg, t) in enumerate(ITEMS):
                p = n % 2
                if n == 2:
                    for b in range(2):
                        dve.wait_ge(s_kkm, b + 1)
                        m = nc.vector.tensor_scalar(kmsT[:, 2 * b:2 * b + 2, :], bank[2 + b][:, :].rearrange("p (h s) -> p h s", s=S),
                                                    1e-6, None, ADD)
                    m.then_inc(s_kkms, 1)
                if n >= len(ITEMS) - RW_F:
                    f = n - (len(ITEMS) - RW_F)
                    dve.wait_ge(s_kksd, 1)
                    nc.vector.reciprocal(krsT[:, f, :], kmsT[:, f, :])
                dve.wait_ge(s_oexp, n + 1)
                dve_step(nc.vector.reciprocal(ors[:, p:p + 1], osum[:, p:p + 1]))
                v = osc[:, p].rearrange("p g m -> p (g m)")
                nc.vector.tensor_scalar(v, v, ors[:, p:p + 1], None, MULT).then_inc(s_op, 1)
                if n + 1 < len(ITEMS):
                    scores(n + 1)

        rT, krT, vrT, wagT = W(9216, RW_F, S), W(10240, RW_F, S), W(11264, RW_F, S), W(12288, 3, S)
        rstage = [W(13056 + 1032 * i, 4, S + 2) for i in range(2)]
        ln_wb = W(17664, 2, RW_W)
        kk0T, ksqT, kmsT, krsT = (R(1024 * i, RW_F, S) for i in range(4))
        kkT, rv, lw, gout = W(0, RW_F, S), W(1024, NT, RW_W), W(2048, NT, 2, RW_W), W(4096, NT, RW_W)
        kdT, aT = W(5120, 2, RW_F, S), W(7168, 2, RW_F, S)
        wide_w = W(13056, 2560)
        w2, a2, g2, w0 = (wide_w[:, WD[n]] for n in ("w2", "a2", "g2", "w0"))
        rpr = W(16640, RW_F, S)
        MAT = [V(0, 2, 4, 4, P) for V in (R, H)]
        RA = [V(4096, 2, NT, 2, P) for V in (R, H)]
        btl, ktl = ([V(at, 2, NT, P) for V in (R, H)] for at in (5120, 5632))
        rw_Tt = [R(6144, 2, 4, P), W(11264, 2, 4, P)]
        Fx, BK = H(6144, 2, NT, 3, P), H(7680, 2, 2, P)
        rw_inv = [(W(10240, 2, 4, P), Tt, W(12288, 2, 4, P), [W(13312 + 1024 * i, 2, 4, P) for i in range(3)])
                  for Tt in rw_Tt]
        Z1, U1, Z2, U2 = (W(16384 + 256 * i, 2, 2, RW_N) for i in range(4))
        SD = W(17408, 2, P)
        Ytok = mem_v[0]
        mid_w, side_w = st[:, 336:351], st[:, 352:367]
        one_ka = st[:, 368:372]
        bon = st[:, 376:392].rearrange("p (t h) -> p t h", t=NT)
        sc0, scl = st[:, 392:394], [st[:, 394:396], st[:, 396:398]]
        gsum, gmean, gvar, gms, gsd, grs = (st[:, 400 + 16 * i:416 + 16 * i] for i in range(6))

        def f_cols(v, f):
            return v[:, f, :].rearrange("p (t s) -> p t s", s=P)

        def pe_rwkv(pe):
            pe.wait_ge(s_oyc, len(ITEMS))
            pe.wait_ge(s_wide, 32)
            pe.wait_ge(s_kkms, 1)
            pe.wait_ge(s_rtanh, 1)
            for d in range(2):
                for t in range(NT):
                    nc.tensor.matmul(bank[2 * d + t][:, :], lhsT=wagT[64 * d:64 * d + 64, 0, t * P:(t + 1) * P],
                                     rhs=w2[64 * d:64 * d + 64, :], start=True, stop=True).then_inc(s_rwm, 1)
            for t in range(NT):
                nc.tensor.matmul(bank[4 + t][:, :], lhsT=wagT[:, 2, t * P:(t + 1) * P], rhs=g2,
                                 start=True, stop=True).then_inc(s_rgm, 1)
            for b in range(2):
                for t in range(NT):
                    for i in range(2):
                        m = nc.tensor.transpose(bank[6 + b][:, (2 * t + i) * P:(2 * t + i + 1) * P],
                                                vrT[:, 2 * b + i, t * P:(t + 1) * P], ident)
                m.then_inc(s_rvt, 1)
            for d in range(2):
                for fp in range(2):
                    pe.wait_ge(s_rlw0, 2 * d + fp + 1)
                    for i in range(2):
                        f = 2 * fp + i
                        m = nc.tensor.matmul(bank[2 * d + fp][:, i * S:(i + 1) * S],
                                             lhsT=a2[64 * d:64 * d + 64, f * P:(f + 1) * P],
                                             rhs=wagT[64 * d:64 * d + 64, 1, :], start=True, stop=True)
                    m.then_inc(s_ram, 1)
            pe.wait_ge(s_rgs, 2)
            pe.wait_ge(s_pr, 1)
            pe.wait_ge(s_rv, 2)
            for t in range(NT):
                for f in range(RW_F):
                    m = nc.tensor.matmul(bank[6][:, t * RW_H + 2 * f:t * RW_H + 2 * f + 2],
                                         lhsT=rpr[:, f, t * P:(t + 1) * P], rhs=const[:, C["half_cols"]],
                                         start=True, stop=True)
            m.then_inc(s_prm, 1)
            pe.wait_ge(s_lw, 1)
            pe.wait_ge(s_ra, 8)
            pe.wait_ge(s_kkms, 1)
            pe.wait_ge(s_bon, 1)
            pe_rwkv_cum(pe, 0)
            pe_rwkv_pairs(pe, 0, 0)
            pe_rwkv_pairs(pe, 0, 1)
            for f in range(RW_F):
                def between(slot):
                    if f and slot < 6:
                        pe_rwkv_tail(pe, f - 1, slot)
                    if f + 1 < RW_F and slot == CUM_SLOT:
                        pe_rwkv_cum(pe, f + 1)
                    if f + 1 < RW_F and slot in PAIR_SLOT:
                        pe_rwkv_pairs(pe, f + 1, PAIR_SLOT.index(slot))

                pe_inv(pe, 4 + f, rw_inv[f % 2], between)
            for step in range(6):
                pe_rwkv_tail(pe, RW_F - 1, step)
            pe.wait_ge(s_ry, 1)
            for b in range(2):
                for i in range(2):
                    for t in range(NT):
                        m = nc.tensor.transpose(aux[b][:, (2 * i + t) * P:(2 * i + t + 1) * P],
                                                Ytok[:, t, (2 * b + i) * P:(2 * b + i + 1) * P], ident)
                m.then_inc(s_ryt, 1)
            pe.wait_ge(s_yT, 8)
            for c in range(4):
                Gemm(pe, "od_out").row_chunk(c, hT_tile, k_tiles=8)

        CUM_SLOT, PAIR_SLOT = 6, (8, 10)

        def pair_banks(f, d):
            return bank[4:8] if f == 0 and d == 0 else bank[0:4]

        def pe_rwkv_cum(pe, f):
            if f >= 2:
                pe.wait_ge(s_os, f + 3)
            if f:
                pe.wait_ge(s_rMAT, 8 * f)
            for d in range(2):
                i0 = C["cum_mid"].start + 256 * d
                for t in range(NT):
                    m = nc.tensor.matmul(bank[d][:, t * S:(t + 1) * S], lhsT=lw[:, t, d, f * P:(f + 1) * P],
                                         rhs=const[:, i0:i0 + 256], start=True, stop=True)
                m.then_inc(s_rc, 1)

        def pe_rwkv_pairs(pe, f, d):
            pe.wait_ge(s_rRA, 2 * f + d + 1)
            pe.wait_ge(s_rbk, 2 * f + d + 1)
            pe.wait_ge(s_rF, 2 * f + 2)
            if d and f:
                pe.wait_ge(s_rMAT, 8 * f + 4)
            for i in range(2):
                for t in range(NT):
                    bk = pair_banks(f, d)[2 * i + t]
                    rows = slice(64 * i, 64 * i + 64)
                    for j, lhs in enumerate((btl[f % 2], ktl[f % 2])):
                        m = nc.tensor.matmul(bk[:, j * 256:(j + 1) * 256], lhsT=lhs[rows, d, t, :],
                                             rhs=RA[f % 2][rows, d, t].rearrange("p k s -> p (k s)"), start=True, stop=True)
                    m.then_inc(s_rM, 1)

        def pe_rwkv_tail(pe, f, step):
            Tt, mat, ra = rw_Tt[f % 2], MAT[f % 2], RA[f % 2]
            both = [(d, i) for d in range(2) for i in range(2)]
            at = lambda d, i: slice((2 * d + i) * RW_N, (2 * d + i + 1) * RW_N)
            if step == 0:
                pe.wait_ge(s_rMAT, 8 * min(f + 2, RW_F))
                for d in range(2):
                    for j, src in enumerate((btl[f % 2], ktl[f % 2])):
                        m = nc.tensor.transpose(bank[2][:, (2 * d + j) * P:(2 * d + j + 1) * P], src[:, d, FIRST_T[d], :], ident)
                m.then_inc(s_rbt, 1)
                for d, i in both:
                    t1, h = FIRST_T[d], 2 * f + i
                    m = nc.tensor.matmul(bank[3][:, at(d, i)], lhsT=mat[:, d, 2 * i + t1, 2],
                                         rhs=rv[:, t1, h * RW_N:(h + 1) * RW_N], start=True, stop=True)
                m.then_inc(s_rz1, 1)
            elif step == 1:
                pe.wait_ge(iv_t, nth(4 + f, LEVELS - 1, 1))
                pe.wait_ge(s_rz1s, f + 1)
                for d, i in both:
                    m = nc.tensor.matmul(bank[3][:, at(d, i)], lhsT=Tt[:, d, 2 * i + FIRST_T[d]], rhs=Z1[:, d, i],
                                         start=True, stop=True)
                m.then_inc(s_vn1, 1)
            elif step == 2:
                pe.wait_ge(s_rBK, f + 1)
                pe.wait_ge(s_vn1s, f + 5)
                for d in range(2):
                    out = bank[2][:, d * P:(d + 1) * P]
                    nc.tensor.matmul(out, lhsT=BK[:, d, 1], rhs=rv[:, FIRST_T[d], f * P:(f + 1) * P], start=True, stop=False)
                    m = nc.tensor.matmul(out, lhsT=BK[:, d, 0], rhs=U1[:, d].rearrange("p i e -> p (i e)"), start=False, stop=True)
                m.then_inc(s_S, 1)
            elif step == 3:
                pe.wait_ge(s_Ss, f + 5)
                for d in range(2):
                    t2 = 1 - FIRST_T[d]
                    nc.tensor.matmul(bank[3][:, d * P:(d + 1) * P], lhsT=ra[:, d, t2, 0], rhs=SD[:, d], start=True, stop=False)
                    for i in range(2):
                        h = 2 * f + i
                        m = nc.tensor.matmul(bank[3][:, at(d, i)], lhsT=mat[:, d, 2 * i + t2, 2],
                                             rhs=rv[:, t2, h * RW_N:(h + 1) * RW_N], start=False, stop=i == 1)
                m.then_inc(s_kS, 1)
            elif step == 4:
                pe.wait_ge(s_R, f + 5)
                for d, i in both:
                    m = nc.tensor.matmul(bank[2][:, at(d, i)], lhsT=Tt[:, d, 2 * i + 1 - FIRST_T[d]], rhs=Z2[:, d, i],
                                         start=True, stop=True)
                m.then_inc(s_vn2, 1)
            else:
                pe.wait_ge(s_vn2s, f + 5)
                for t in range(NT):
                    d2 = 1 if t == 0 else 0
                    nc.tensor.matmul(bank[0][:, t * P:(t + 1) * P], lhsT=ra[:, d2, t, 1], rhs=SD[:, d2], start=True, stop=False)
                    for d in range(2):
                        U = U1 if t == FIRST_T[d] else U2
                        for i in range(2):
                            h = 2 * f + i
                            out = bank[0][:, t * P + i * RW_N:t * P + (i + 1) * RW_N]
                            nc.tensor.matmul(out, lhsT=mat[:, d, 2 * i + t, 3], rhs=rv[:, t, h * RW_N:(h + 1) * RW_N],
                                             start=False, stop=False)
                            m = nc.tensor.matmul(out, lhsT=mat[:, d, 2 * i + t, 1], rhs=U[:, d, i], start=False,
                                                 stop=d == 1 and i == 1)
                m.then_inc(s_o, 1)

        FIRST_T = (0, 1)

        def act_rwkv(act):
            act.dma_start(wide_w, wide[:, 0:2560]).then_inc(s_wide, 16)
            for t in range(NT):
                act.wait_ge(s_rgm, t + 1)
                nc.scalar.activation(gout[:, t, :], bank[4 + t][:, :], ACT.Copy).then_inc(s_rgs, 1)
            act.wait_ge(s_rlw0, 4)
            nc.scalar.activation(lw, lw, ACT.Sigmoid).then_inc(s_lw, 1)
            for d in range(2):
                for fp in range(2):
                    act.wait_ge(s_ram, 2 * d + fp + 1)
                    for i in range(2):
                        f = 2 * fp + i
                        j = Q["rw_a0"].start + 4 * d + f
                        nc.scalar.activation(aT[:, d, f, :], bank[2 * d + fp][:, i * S:(i + 1) * S], ACT.Sigmoid,
                                             bias=par[:, j:j + 1]).then_inc(s_ra, 1)
            act_rwkv_pre(act, 0)
            for f in range(RW_F):
                def between(level):
                    if f and level <= 3:
                        act_rwkv_tail(act, f - 1, level)
                    if f + 1 < RW_F and level == 4:
                        act_rwkv_pre(act, f + 1)
                    if f + 1 == RW_F and level == 4:
                        act.wait_ge(s_o, 4 + RW_F - 1)
                        hi_upto(act, starts["od_out"][1] + AHEAD)

                act_inv(act, 4 + f, rw_inv[f % 2], between)
            for level in range(1, 4):
                act_rwkv_tail(act, RW_F - 1, level)
            act.wait_ge(s_o, 4 + RW_F)
            nc.scalar.activation(hT_hi[:, 0:4, :], ycT, ACT.Copy).then_inc(s_ysp, 1)
            act.wait_ge(s_gms, 1)
            nc.scalar.activation(gsd, gms, ACT.Sqrt).then_inc(s_gsd, 1)
            for b in range(2):
                act.wait_ge(s_ryt, b + 1)
                nc.scalar.activation(hT_hi[:, 4 + 2 * b:6 + 2 * b, :], aux[b][:, :].rearrange("p (h s) -> p h s", s=S),
                                     ACT.Copy).then_inc(s_ysp, 1)
            for c in range(4):
                hi_upto(act, chunk_done("od_out", c) + AHEAD)

        def act_rwkv_pre(act, f):
            for d in range(2):
                act.wait_ge(s_rc, 2 * f + d + 1)
                v = bank[d][:, :].rearrange("p (t k s) -> p t k s", t=NT, k=2)
                nc.scalar.activation(Fx[:, d, :, 0:2, :], v, ACT.Exp, scale=-KAPPA)
                nc.scalar.activation(Fx[:, d, :, 2, :], v[:, :, 0, :], ACT.Exp, scale=KAPPA).then_inc(s_rF, 1)

        def act_rwkv_tail(act, f, level):
            c4 = lambda v: v.rearrange("p d i e -> p (d i e)")
            if level == 1:
                act.wait_ge(s_rbt, f + 1)
                nc.scalar.activation(BK.rearrange("p d k c -> p (d k) c"), four(bank[2]), ACT.Copy).then_inc(s_rBK, 1)
                act.wait_ge(s_rz1, f + 1)
                nc.scalar.activation(c4(Z1), bank[3][:, 0:256], ACT.Copy).then_inc(s_rz1s, 1)
            ready, src, dst, scale, done = ((s_vn1, 3, U1, -1.0, s_vn1s), (s_kS, 3, Z2, 1.0, s_R),
                                            (s_vn2, 2, U2, -1.0, s_vn2s))[level - 1]
            act.wait_ge(ready, f + 5)
            nc.scalar.activation(c4(dst), bank[src][:, 0:256], ACT.Copy, scale=scale).then_inc(done, 1)

        def dve_shift(dve, src, dst, tile0, n):
            for i in range(n):
                m = nc.vector.tensor_scalar(dst[:, i], src[:, i, 1:S + 1], mid_w[:, tile0 + i:tile0 + i + 1], None, MULT)
            dve_step(m)
            for at in (0, 2):
                for i in range(n):
                    m = nc.vector.scalar_tensor_tensor(out=dst[:, i], in0=src[:, i, at:at + S],
                                                       scalar=side_w[:, tile0 + i:tile0 + i + 1], in1=dst[:, i],
                                                       op0=MULT, op1=ADD)
                if at == 0:
                    dve_step(m)
            m.then_inc(s_rw, 1)

        def dve_rwkv(dve):
            dve.wait_ge(s_oyc, len(ITEMS))
            nc.vector.tensor_tensor(kkT, kk0T, krsT, MULT).then_inc(s_kk, 1)
            w0v = w0.rearrange("p (d n) -> p d n", d=2)
            for d in range(2):
                for t in range(NT):
                    dve.wait_ge(s_rwm, 2 * d + t + 1)
                    nc.vector.tensor_tensor(lw[:, t, d, :], bank[2 * d + t][:, :], w0v[:, d], ADD).then_inc(s_rlw0, 1)
            for b in range(2):
                dve.wait_ge(s_rvt, b + 1)
                nc.vector.tensor_copy(rv[:, :, 2 * b * P:(2 * b + 2) * P],
                                      bank[6 + b][:, :].rearrange("p (t n) -> p t n", t=NT)).then_inc(s_rv, 1)
            for d in range(2):
                for f in range(RW_F):
                    dve.wait_ge(s_ra, 4 * d + f + 1)
                    j = Q["rw_ka"].start + f
                    m = nc.vector.tensor_scalar(kdT[:, d, f, :], aT[:, d, f, :], par[:, j:j + 1], one_ka[:, f:f + 1], MULT, ADD)
                dve_step(m)
                m = nc.vector.tensor_tensor(kdT[:, d], kdT[:, d], krT, MULT)
            m.then_inc(s_kd, 1)
            dve.wait_ge(s_kd, 1)
            dve_step(nc.vector.tensor_tensor(rpr, kdT[:, 0], kdT[:, 1], ADD))
            for f in range(RW_F):
                j = Q["rw_rk"].start + f
                m = nc.vector.scalar_tensor_tensor(out=rpr[:, f, :], in0=rpr[:, f, :], scalar=par[:, j:j + 1],
                                                   in1=rT[:, f, :], op0=MULT, op1=MULT)
            m.then_inc(s_pr, 1)
            dve.wait_ge(s_prm, 1)
            nc.vector.tensor_copy(bon, bank[6][:, 0:16].rearrange("p (t h) -> p t h", t=NT)).then_inc(s_bon, 1)
            dve.wait_ge(s_kk, 1)
            dve_rwkv_pre(dve, 0)
            dve_rwkv_pairs(dve, 0, 0)
            dve_rwkv_pairs(dve, 0, 1)
            for f in range(RW_F):
                def between(level):
                    if f and level == 1:
                        dve_rwkv_state(dve, f - 1)
                    if f and level == 3:
                        dve_rwkv_out(dve, f - 1)
                    if f + 1 < RW_F and level == 4:
                        dve_rwkv_pre(dve, f + 1)
                    if f + 1 < RW_F and level >= 5:
                        dve_rwkv_pairs(dve, f + 1, level - 5)
                    if f + 1 == RW_F and level == 4:
                        lo_upto(dve, starts["od_out"][1] + AHEAD)

                dve_inv(dve, 4 + f, rw_inv[f % 2], between)
            dve_rwkv_state(dve, RW_F - 1)
            dve_rwkv_out(dve, RW_F - 1)
            dve.wait_ge(s_os, RW_F + 4)
            y16 = Ytok[:, :, :].rearrange("p t (h e) -> p (t h) e", e=RW_N)
            z = W(10240, NT, RW_W)
            z16 = z.rearrange("p t (h e) -> p (t h) e", e=RW_N)
            dve_step(nc.vector.reduce_sum(gsum, y16, AX_X))
            dve_step(nc.vector.tensor_scalar(gmean, gsum, 1.0 / RW_N, None, MULT))
            dve_step(nc.vector.tensor_tensor(y16, y16, lanes(gmean, RW_N), SUB))
            dve_step(nc.vector.tensor_tensor(z16, y16, y16, MULT))
            dve_step(nc.vector.reduce_sum(gvar, z16, AX_X))
            nc.vector.tensor_scalar(gms, gvar, 1.0 / RW_N, GN_EPS, MULT, ADD).then_inc(s_gms, 1)
            dve_step(nc.vector.tensor_tensor(z16, rv.rearrange("p t (h e) -> p (t h) e", e=RW_N),
                                             lanes(bon.rearrange("p t h -> p (t h)"), RW_N), MULT))
            dve.wait_ge(s_ysp, 6)
            nc.vector.tensor_tensor(hT_lo[:, 0:4, :], ycT, f32(hT_hi[:, 0:4, :]), SUB).then_inc(s_yT, 1)
            dve.wait_ge(s_gsd, 1)
            dve_step(nc.vector.reciprocal(grs, gsd))
            dve_step(nc.vector.tensor_tensor(y16, y16, lanes(grs, RW_N), MULT))
            row = lambda j: ln_wb[:, j].unsqueeze(1).broadcast_to([P, NT, RW_W])
            dve_step(nc.vector.tensor_tensor(Ytok[:, :, :], Ytok[:, :, :], row(0), MULT))
            dve_step(nc.vector.tensor_tensor(Ytok[:, :, :], Ytok[:, :, :], row(1), ADD))
            dve_step(nc.vector.tensor_tensor(Ytok[:, :, :], Ytok[:, :, :], z, ADD))
            nc.vector.tensor_tensor(Ytok[:, :, :], Ytok[:, :, :], gout, MULT).then_inc(s_ry, 1)
            for b in range(2):
                dve.wait_ge(s_ysp, b + 7)
                nc.vector.tensor_tensor(hT_lo[:, 4 + 2 * b:6 + 2 * b, :], aux[b][:, :].rearrange("p (h s) -> p h s", s=S),
                                        f32(hT_hi[:, 4 + 2 * b:6 + 2 * b, :]), SUB).then_inc(s_yT, 1)
            for c in range(4):
                dve_add_to_x(dve, "od_out", c)

        def dve_rwkv_pre(dve, f):
            for d in range(2):
                dve.wait_ge(s_rF, 2 * f + d + 1)
                nc.vector.tensor_tensor(RA[f % 2][:, d, :, 0, :], f_cols(kkT, f), Fx[:, d, :, 1, :], MULT)
                nc.vector.tensor_tensor(RA[f % 2][:, d, :, 1, :], f_cols(rT, f), Fx[:, d, :, 0, :], MULT).then_inc(s_rRA, 1)
            for d in range(2):
                t1, last, first = FIRST_T[d], (P - 1, 0)[d], (0, P - 1)[d]
                dve_step(nc.vector.reciprocal(sc0[:, d:d + 1], Fx[:, d, 1 - t1, 1, first:first + 1]))
                m = nc.vector.tensor_tensor(scl[f % 2][:, d:d + 1], sc0[:, d:d + 1], Fx[:, d, t1, 0, last:last + 1], MULT)
            dve_step(m)

        def dve_rwkv_pairs(dve, f, d):
            for m_ in range(4):
                dve.wait_ge(s_rM, 8 * f + 4 * d + m_ + 1)
                i0 = C["causal"].start + 256 * d
                mask = const[:, i0:i0 + 256].unsqueeze(1).broadcast_to([P, 2, 256])
                nc.vector.tensor_tensor(MAT[f % 2][:, d, m_].rearrange("p (two k) s -> p two (k s)", two=2),
                                        pair_banks(f, d)[m_][:, :].rearrange("p (two k) -> p two k", two=2),
                                        mask, MULT).then_inc(s_rMAT, 1)

        def dve_rwkv_state(dve, f):
            dve.wait_ge(s_S, f + 5)
            for d in range(2):
                m = nc.vector.scalar_tensor_tensor(out=SD[:, d], in0=bank[2][:, d * P:(d + 1) * P], scalar=scl[f % 2][:, d:d + 1],
                                                   in1=const[:, C["halves"]], op0=MULT, op1=MULT)
            m.then_inc(s_Ss, 1)

        def dve_rwkv_out(dve, f):
            dve.wait_ge(s_o, f + 5)
            nc.vector.tensor_copy(Ytok[:, :, f * P:(f + 1) * P],
                                  bank[0][:, 0:256].rearrange("p (t n) -> p t n", t=NT)).then_inc(s_os, 1)

        def pool_rwkv_pre(pool, f):
            for d in range(2):
                pool.wait_ge(s_rF, 2 * f + d + 1)
                nc.gpsimd.tensor_tensor(btl[f % 2][:, d], f_cols(aT[:, d], f), Fx[:, d, :, 2, :], MULT)
                nc.gpsimd.tensor_tensor(ktl[f % 2][:, d], f_cols(kdT[:, d], f), Fx[:, d, :, 2, :], MULT).then_inc(s_rbk, 1)

        def pool_odd(pool):
            pool.wait_ge(s_kk, 1)
            pool.wait_ge(s_kd, 1)
            for d in range(2):
                m = nc.gpsimd.tensor_tensor(aT[:, d], aT[:, d], kkT, MULT)
            pool_step(m)
            pool_rwkv_pre(pool, 0)
            for f in range(RW_F):
                AT = [MAT[f % 2][:, d, :, 0, :] for d in range(2)]
                for d in range(2):
                    pool.wait_ge(s_rMAT, 8 * f + 4 * d + 4)
                    for level in range(2):
                        pool_inv_mask(pool, 4 + f, AT, rw_inv[f % 2], level, d)
                for level in range(2, LEVELS):
                    if level == LEVELS - 1 and f + 1 < RW_F:
                        pool_rwkv_pre(pool, f + 1)
                    for d in range(2):
                        pool_inv_mask(pool, 4 + f, AT, rw_inv[f % 2], level, d)

        def pe_odd(pe):
            pe_window(pe)
            pe_rwkv(pe)

        def act_odd(act):
            act_window(act)
            act_rwkv(act)

        def dve_odd(dve):
            dve_window(dve)
            dve_rwkv(dve)

        def norm_src(name):
            return memx if name.startswith("mem") else x

        HT_FREE = {"mem0": 0, "mem1": chunk_done("mem_v0", 0), "mix0": chunk_done("mem_v1", 0),
                   "xattn0": chunk_done("ev_out", 3), "ffn0": chunk_done("xa_q0", 0),
                   "mix1": chunk_done("ffn0", FF_TURNS * FF_CHUNKS - 1), "xattn1": chunk_done("od_out", 3),
                   "ffn1": chunk_done("xa_q1", 0)}

        def after(name):
            return starts[name][0] + dict((n, c) for n, c, _ in GEMMS)[name]

        X_READY = {"xattn0": after("ev_out"), "ffn0": after("xa_o0"), "mix1": after("ffn0"),
                   "xattn1": after("od_out"), "ffn1": after("xa_o1")}

        def run_norm(eng, norm, name):
            if name in X_READY:
                wait_chunks_taken(eng, X_READY[name])
            norm(eng, name, norm_src(name), HT_FREE[name])

        @block.tensor
        def _(pe):
            pe_bias(pe)
            pe.wait_ge(s_load, 32)
            pe.wait_ge(s_mem_in, 16)
            pe_norm(pe, "mem0", before=[(s_bias_s, DSA_G)])
            pe_memory(pe, 0)
            pe_norm(pe, "mem1")
            pe_memory(pe, 1)
            pe_norm(pe, "mix0")
            pe_even(pe)
            for l in range(2):
                if l:
                    pe_norm(pe, "mix1", before=[(s_xoT, 2)])
                    pe_odd(pe)
                pe_norm(pe, f"xattn{l}")
                pe_cross(pe, l)
                pe_norm(pe, f"ffn{l}")
                pe_ffn(pe, l)

        @block.scalar
        def _(act):
            act_bias(act)
            act.wait_ge(s_mem_in, 16)
            for l in range(2):
                run_norm(act, act_norm, f"mem{l}")
                act_memory(act, l)
                act_bias_out(act, l)
            act.wait_ge(s_x_in, 16)
            run_norm(act, act_norm, "mix0")
            act.wait_ge(s_bias_out, 16 * DSA_G)
            act_even(act)
            for l in range(2):
                if l:
                    run_norm(act, act_norm, "mix1")
                    act_odd(act)
                run_norm(act, act_norm, f"xattn{l}")
                act_cross(act, l)
                run_norm(act, act_norm, f"ffn{l}")
                act_ffn(act, l)

        @block.vector
        def _(dve):
            dve.wait_ge(s_load, 32)
            dve.wait_ge(s_mem_in, 16)
            nc.vector.tensor_tensor(gqk, par[:, Q["xa_qn"]], par[:, Q["xa_kn"]], MULT).then_inc(s_gqk, 1)
            for l in range(2):
                run_norm(dve, dve_norm, f"mem{l}")
                dve_memory(dve, l)
            dve.wait_ge(s_x_in, 16)
            run_norm(dve, dve_norm, "mix0")
            dve.wait_ge(s_bias_out, 16 * DSA_G)
            dve_even(dve)
            for l in range(2):
                if l:
                    run_norm(dve, dve_norm, "mix1")
                    dve_odd(dve)
                run_norm(dve, dve_norm, f"xattn{l}")
                dve_cross(dve, l)
                run_norm(dve, dve_norm, f"ffn{l}")
                dve_ffn(dve, l)

        @block.gpsimd
        def _(pool):
            nc.gpsimd.memset(rel[N_BUCKETS:NB], NEG).then_inc(s_neg, 1)
            pool.wait_ge(s_load, 32)
            pool_even(pool)
            pool_odd(pool)


def constants():
    import math

    import numpy as np

    at, n = columns(CONST_COLS)
    c = np.zeros((P, n), np.float32)
    s, t = np.arange(P)[:, None], np.arange(P)[None, :]
    c[:, at["ident"]] = s == t
    level = np.zeros((P, 2, LEVELS, P), np.float32)
    for n_, size in enumerate(1 << np.arange(LEVELS)):
        pair = (s // (2 * size)) == (t // (2 * size))
        level[:, 0, n_] = pair & (s // size < t // size)
        level[:, 1, n_] = pair & (s // size > t // size)
    c[:, at["level"]] = level.reshape(P, -1)
    c[:, at["neg"]] = np.where(np.hstack([s <= t, s >= t]), 0.0, NEG)
    low, high = s < P // 2, s >= P // 2
    mid = [(s <= t) * 1.0 - low, (s < t) * 1.0 - low, (s >= t) * 1.0 - high, (s > t) * 1.0 - high]
    c[:, at["cum_mid"]] = np.hstack(mid)
    c[:, at["causal"]] = np.hstack([s < t, s <= t, s > t, s >= t])
    c[:, at["halves"]] = (s // RW_N) == (t // RW_N)
    c[:, at["ones"]] = 1.0
    c[:, at["half_cols"]] = np.hstack([low, high])

    table = np.zeros((N_BUCKETS + 1, DSA_G, 512), np.float32)
    half = N_BUCKETS // 2
    exact = half // 2
    for g, dil in enumerate(DILATIONS):
        rel = np.arange(512) - (S - 1)
        inside = (rel % dil == 0) & (np.abs(rel) <= N_SIDE * dil)
        dist = np.abs(rel)
        ratio = np.maximum(dist, exact).astype(np.float32) / np.float32(exact)
        scaled = np.log(ratio) / np.float32(math.log(MAX_DIST / exact))
        large = np.minimum(exact + (scaled * np.float32(half - exact)).astype(np.int32), half - 1)
        bucket = np.where(rel > 0, half, 0) + np.where(dist < exact, dist, large)
        for n_ in range(512):
            table[bucket[n_] if inside[n_] else N_BUCKETS, g, n_] = 1.0
    return c, table.reshape(N_BUCKETS + 1, -1)


def kernel(**inputs):
    import numpy as np
    import concourse.bacc as bacc
    from concourse.bass_utils import run_bass_kernel_spmd

    a = {name: np.asarray(value) for name, value in inputs.items()}

    sc = a["ev_w_in"][0][:, 4 * DN_W + 4 * DN_H:]
    sc_order = [(part, half) for half in range(2) for part in (1, 2, 0)]
    rw = a["od_w_in"][0][:, 3 * DSA_H * P:]
    matrices = {
        "ev_qkv": a["ev_w_in"][0][:, :3 * DN_W],
        "ev_gate": a["ev_w_in"][0][:, 3 * DN_W:4 * DN_W],
        "ev_sc": np.hstack([sc[:, p * 1024 + h * 512:p * 1024 + h * 512 + 512] for p, h in sc_order]),
        "ev_out": a["ev_w_out"][0],
        "od_q": a["od_w_in"][0][:, :DSA_H * P],
        "od_k": a["od_w_in"][0][:, DSA_H * P:2 * DSA_H * P],
        "od_v": a["od_w_in"][0][:, 2 * DSA_H * P:3 * DSA_H * P],
        "od_rw": np.pad(rw, ((0, 0), (0, 2048 - rw.shape[1]))),
        "od_out": a["od_w_out"][0],
    }
    for l in range(2):
        matrices[f"mem_k{l}"], matrices[f"mem_v{l}"] = a["xa_wk"][l], a["xa_wv"][l]
        matrices[f"xa_q{l}"], matrices[f"xa_o{l}"] = a["xa_wq"][l], a["xa_wo"][l]
    starts, _, n_units = gemm_starts()
    stream = np.zeros((n_units, P, UNIT), np.float32)

    def row_units(w):
        k, n = w.shape
        return w.reshape(k // 256, 2, P, n // 512, 512).transpose(3, 0, 2, 1, 4).reshape(-1, P, UNIT)

    def column_units(w):
        k, n = w.shape
        return w.reshape(k // 1024, 8, P, n // P, P).transpose(3, 0, 2, 1, 4).reshape(-1, P, UNIT)

    for name, _, _ in GEMMS:
        u = starts[name][1]
        if name.startswith("ffn"):
            l, width = int(name[-1]), F_FF // FF_TURNS
            parts = []
            for i in range(FF_TURNS):
                parts.append(column_units(a["ffn_w1"][l][:, i * width:(i + 1) * width]))
                parts.append(row_units(a["ffn_w2"][l][i * width:(i + 1) * width]))
            got = np.concatenate(parts)
        elif name in ("ev_qkv", "ev_sc", "od_q", "od_rw", "xa_q0", "xa_q1"):
            got = column_units(matrices[name])
        else:
            got = row_units(matrices[name])
        stream[u:u + len(got)] = got
    stream = stream.reshape(n_units // 2, 2, P, UNIT).transpose(0, 2, 1, 3).reshape(n_units // 2, P, BLOCK)

    tiles = lambda v: np.ascontiguousarray(v.reshape(-1, P).T)
    rows = lambda v: np.broadcast_to(v.reshape(1, -1), (P, v.size))
    at, n = columns(PARAM_COLS)
    small = np.zeros((P, n), np.float32)
    for l in range(2):
        for name, source in (("mix", "norm_mix"), ("xattn", "norm_xattn"), ("mem", "norm_mem"), ("ffn", "norm_ffn")):
            small[:, at[f"g_{name}{l}"]] = tiles(a[source][l])
    small[:, at["xa_qn"]], small[:, at["xa_kn"]] = a["xa_qn"].T, a["xa_kn"].T
    small[:, at["dn_conv"]] = a["dn_conv"][0].reshape(24, P, 3).transpose(1, 0, 2).reshape(P, 72)
    small[:, at["sc_conv"]] = a["sc_conv"][0].reshape(8, P, 3).transpose(1, 0, 2).reshape(P, 24)
    small[:, at["dn_norm"]] = rows(a["dn_norm"][0])
    small[:, at["a_log"]], small[:, at["dt_bias"]] = rows(a["dn_a_log"][0]), rows(a["dn_dt_bias"][0])
    small[:, at["ab_w"]] = (a["ev_w_in"][0][:, 4 * DN_W:4 * DN_W + 4 * DN_H]
                            .reshape(KD, P, 4 * DN_H).transpose(1, 0, 2).reshape(P, 512))
    small[:, at["ca_qn"]], small[:, at["ca_kn"]] = a["ca_qn"].T, a["ca_kn"].T
    small[:, at["rw_mu"]] = tiles(a["rw_mu"][0])
    small[:, at["rw_a0"]] = tiles(a["rw_a0"][0])
    small[:, at["rw_kk"]], small[:, at["rw_ka"]] = tiles(a["rw_k_k"][0]), tiles(a["rw_k_a"][0])
    small[:, at["rw_rk"]] = tiles(a["rw_r_k"][0])
    at, n = columns(WIDE_COLS)
    wide = np.zeros((P, n), np.float32)
    wide[:, at["w2"]], wide[:, at["a2"]] = a["rw_w2"][0].reshape(P, RW_W), a["rw_a2"][0].reshape(P, RW_W)
    wide[:, at["g2"]] = a["rw_g2"][0]
    wide[:, at["w0"]] = rows(a["rw_w0"][0])
    wide[:, at["ln_w"]], wide[:, at["ln_b"]] = rows(a["rw_ln_w"][0]), rows(a["rw_ln_b"][0])

    masks, table = constants()
    sent = {
        "x": a["x"][0], "mem": a["mem"][0], "stream": stream, "small": small, "wide": wide,
        "masks": masks, "bias_table": table, "rel_bias": a["rel_bias"],
    }
    nc = bacc.Bacc("TRN2", target_bir_lowering=False, num_devices=1, dynamic_dma_scratch_size=1024)
    arrays = {f"in_{name}": np.ascontiguousarray(v) for name, v in sent.items()}
    aps = [nc.dram_tensor(name, v.shape, mybir.dt.from_np(v.dtype), kind="ExternalInput").ap()
           for name, v in arrays.items()]
    out = nc.dram_tensor("out", (S, D), F32, kind="ExternalOutput").ap()
    scratch = nc.dram_tensor("bias_rows", (DSA_H, P, 512), F32, kind="Internal").ap()
    build(nc, *aps, scratch, out)
    r = run_bass_kernel_spmd(nc, [arrays], core_ids=[0])
    return r.results[0]["out"].reshape(1, S, D)
```
